# Optimizing a Trainium2 kernel written in Bass

```python
import math
import jax, jax.numpy as jnp
from jax import lax
import numpy as np

D_MODEL = 1024
BATCH = 1
SEQ = 512
DEPTH = 2

HEAD_DIM = 64
N_EVEN = (DEPTH + 1) // 2
N_ODD = DEPTH // 2
A_HEADS = D_MODEL // (4 * HEAD_DIM)
B_HEADS = D_MODEL // (2 * HEAD_DIM)
IDX_HEADS = 8
IDX_DIM = 64
TOPK_MAX = 256
C_HEADS = D_MODEL // HEAD_DIM
C_KV_HEADS = C_HEADS // 4
WINDOW = 128
FFN_HIDDEN = ((8 * D_MODEL // 3 + 255) // 256) * 256
Q_BLOCK = 128
NORM_EPS = 1e-6

EVEN_SIZES = (A_HEADS * 2 * HEAD_DIM,
              A_HEADS * 2 * HEAD_DIM,
              A_HEADS * 2 * HEAD_DIM,
              B_HEADS * HEAD_DIM,
              HEAD_DIM,
              HEAD_DIM,
              IDX_HEADS * IDX_DIM,
              IDX_DIM,
              IDX_HEADS)
EVEN_COLS = sum(EVEN_SIZES)
ODD_SIZES = (C_HEADS * HEAD_DIM, C_KV_HEADS * HEAD_DIM, C_KV_HEADS * HEAD_DIM)
ODD_COLS = sum(ODD_SIZES)


def _rms_norm(x, g):
    xf = x.astype(jnp.float32)
    y = xf * lax.rsqrt(jnp.mean(xf * xf, axis=-1, keepdims=True) + NORM_EPS)
    return (y * g.astype(jnp.float32)).astype(x.dtype)

def _split_cols(t, sizes):
    offs = np.cumsum(np.asarray(sizes))[:-1].tolist()
    return jnp.split(t, offs, axis=-1)

def _alibi_slopes(n):
    return jnp.asarray(2.0 ** (-8.0 * np.arange(1, n + 1) / n), dtype=jnp.float32)

def _diff_attention(q, k, v, lam, slopes):
    b, s, h = q.shape[:3]
    nb = s // Q_BLOCK
    qb = jnp.moveaxis(q.reshape(b, nb, Q_BLOCK, h, 2, HEAD_DIM), 1, 0)
    key_pos = jnp.arange(s)
    scale = HEAD_DIM ** -0.5

    def block(args):
        qi, i = args
        dist = (i * Q_BLOCK + jnp.arange(Q_BLOCK))[:, None] - key_pos[None, :]
        logits = jnp.einsum('bqhmd,bshmd->bhmqs', qi, k).astype(jnp.float32) * scale
        logits = logits - slopes[None, :, None, None, None] * dist.astype(jnp.float32)
        logits = jnp.where(dist >= 0, logits, -jnp.inf)
        p = jax.nn.softmax(logits, axis=-1)
        a = p[:, :, 0] - lam * p[:, :, 1]
        return jnp.einsum('bhqs,bshe->bqhe', a.astype(v.dtype), v)

    out = lax.map(block, (qb, jnp.arange(nb)))
    return jnp.moveaxis(out, 0, 1).reshape(b, s, h, 2 * HEAD_DIM)

def _dsa_attention(q, k, v, iq, ik, iw, slopes, topk):
    b, s, h = q.shape[:3]
    nb = s // Q_BLOCK
    key_pos = jnp.arange(s)
    scale = HEAD_DIM ** -0.5
    gather = jax.vmap(lambda t, idx: t[idx])

    def blocks(t):
        return jnp.moveaxis(t.reshape((b, nb, Q_BLOCK) + t.shape[2:]), 1, 0)

    def block(args):
        qi, iqi, iwi, i = args
        q_pos = i * Q_BLOCK + jnp.arange(Q_BLOCK)
        causal = key_pos[None, :] <= q_pos[:, None]
        idx_logits = jnp.einsum('bqhd,bsd->bqhs', iqi, ik).astype(jnp.float32) * IDX_DIM ** -0.5
        score = jnp.einsum('bqhs,bqh->bqs', jax.nn.relu(idx_logits), iwi.astype(jnp.float32))
        score = jnp.where(causal[None], score, -jnp.inf)
        _, sel = lax.top_k(score, topk)
        k_sel = gather(k, sel)
        v_sel = gather(v, sel)
        dist = (q_pos[None, :, None] - sel)[:, None]
        logits = jnp.einsum('bqhd,bqkd->bhqk', qi, k_sel).astype(jnp.float32) * scale
        logits = logits - slopes[None, :, None, None] * dist.astype(jnp.float32)
        logits = jnp.where(dist >= 0, logits, -jnp.inf)
        p = jax.nn.softmax(logits, axis=-1)
        return jnp.einsum('bhqk,bqkd->bqhd', p.astype(v.dtype), v_sel)

    out = lax.map(block, (blocks(q), blocks(iq), blocks(iw), jnp.arange(nb)))
    return jnp.moveaxis(out, 0, 1).reshape(b, s, h, HEAD_DIM)

def _swa_sink_attention(q, k, v, sinks, slopes):
    b, s = q.shape[:2]
    nb = s // WINDOW
    g = C_HEADS // C_KV_HEADS
    qb = q.reshape(b, nb, WINDOW, C_KV_HEADS, g, HEAD_DIM)

    def band(t):
        tb = t.reshape(b, nb, WINDOW, C_KV_HEADS, HEAD_DIM)
        prev = jnp.pad(tb, ((0, 0), (1, 0), (0, 0), (0, 0), (0, 0)))[:, :-1]
        return jnp.concatenate([prev, tb], axis=2)

    kk, vv = band(k), band(v)
    i = jnp.arange(WINDOW)
    j = jnp.arange(2 * WINDOW)
    dist = WINDOW + i[:, None] - j[None, :]
    key_pos = jnp.arange(nb)[:, None] * WINDOW - WINDOW + j[None, :]
    valid = ((dist >= 0) & (dist < WINDOW))[None] & (key_pos >= 0)[:, None, :]
    logits = jnp.einsum('bnqhgd,bnkhd->bnhgqk', qb, kk).astype(jnp.float32) * HEAD_DIM ** -0.5
    sl = slopes.reshape(C_KV_HEADS, g)
    logits = logits - sl[None, None, :, :, None, None] * dist.astype(jnp.float32)
    logits = jnp.where(valid[None, :, None, None], logits, -jnp.inf)
    sink = jnp.broadcast_to(sinks.astype(jnp.float32).reshape(1, 1, C_KV_HEADS, g, 1, 1),
                            logits.shape[:-1] + (1,))
    p = jax.nn.softmax(jnp.concatenate([logits, sink], axis=-1), axis=-1)[..., :-1]
    out = jnp.einsum('bnhgqk,bnkhd->bnqhgd', p.astype(v.dtype), vv)
    return out.reshape(b, s, C_HEADS * HEAD_DIM)

def _even_mixer(h, w_in, qn_a, kn_a, lam_q1, lam_k1, lam_q2, lam_k2, subln_a, qn_b, kn_b, layer_idx):
    b, s, _ = h.shape
    aq, ak, av, bq, bk, bv, iq, ik, iw = _split_cols(h @ w_in, EVEN_SIZES)
    aq = _rms_norm(aq.reshape(b, s, A_HEADS, 2, HEAD_DIM), qn_a)
    ak = _rms_norm(ak.reshape(b, s, A_HEADS, 2, HEAD_DIM), kn_a)
    av = av.reshape(b, s, A_HEADS, 2 * HEAD_DIM)
    lam_init = 0.8 - 0.6 * math.exp(-0.3 * layer_idx)
    f32 = jnp.float32
    lam = (jnp.exp(jnp.sum(lam_q1.astype(f32) * lam_k1.astype(f32)))
           - jnp.exp(jnp.sum(lam_q2.astype(f32) * lam_k2.astype(f32))) + lam_init)
    ya = _diff_attention(aq, ak, av, lam, _alibi_slopes(A_HEADS))
    ya = _rms_norm(ya, subln_a) * (1.0 - lam_init)
    bq = _rms_norm(bq.reshape(b, s, B_HEADS, HEAD_DIM), qn_b)
    bk = _rms_norm(bk, kn_b)
    iq = iq.reshape(b, s, IDX_HEADS, IDX_DIM)
    iw = iw * IDX_HEADS ** -0.5
    topk = min(TOPK_MAX, s // 4)
    yb = _dsa_attention(bq, bk, bv, iq, ik, iw, _alibi_slopes(B_HEADS), topk)
    return jnp.concatenate([ya.reshape(b, s, -1), yb.reshape(b, s, -1)], axis=-1)

def _odd_mixer(h, w_in, qn_c, kn_c, sinks):
    b, s, _ = h.shape
    q, k, v = _split_cols(h @ w_in, ODD_SIZES)
    q = _rms_norm(q.reshape(b, s, C_HEADS, HEAD_DIM), qn_c)
    k = _rms_norm(k.reshape(b, s, C_KV_HEADS, HEAD_DIM), kn_c)
    v = v.reshape(b, s, C_KV_HEADS, HEAD_DIM)
    return _swa_sink_attention(q, k, v, sinks, _alibi_slopes(C_HEADS))

def _swiglu(h, wg, wu, wd):
    return (jax.nn.silu(h @ wg) * (h @ wu)) @ wd

def first_inputs(seed: int = 0) -> dict:
    key = jax.random.key(seed)
    ks = iter(list(jax.random.split(key, 32)))
    d, f = D_MODEL, FFN_HIDDEN

    def nrm(shape, scale):
        return jax.random.normal(next(ks), shape, jnp.float32) * scale

    def gain(shape):
        return 1.0 + nrm(shape, 0.02)

    return {
        'x': nrm((BATCH, SEQ, d), 1.0),
        'c': nrm((BATCH, d), 1.0),
        'ada_w': nrm((DEPTH, d, 6 * d), 0.5 * d ** -0.5),
        'ada_b': nrm((DEPTH, 6 * d), 0.02),
        'norm_mix': gain((DEPTH, d)),
        'norm_ffn': gain((DEPTH, d)),
        'w_out': nrm((DEPTH, d, d), d ** -0.5),
        'ffn_gate': nrm((DEPTH, d, f), d ** -0.5),
        'ffn_up': nrm((DEPTH, d, f), d ** -0.5),
        'ffn_down': nrm((DEPTH, f, d), f ** -0.5),
        'w_in_even': nrm((N_EVEN, d, EVEN_COLS), d ** -0.5),
        'qn_a': gain((N_EVEN, HEAD_DIM)),
        'kn_a': gain((N_EVEN, HEAD_DIM)),
        'lam_q1': nrm((N_EVEN, HEAD_DIM), 0.1),
        'lam_k1': nrm((N_EVEN, HEAD_DIM), 0.1),
        'lam_q2': nrm((N_EVEN, HEAD_DIM), 0.1),
        'lam_k2': nrm((N_EVEN, HEAD_DIM), 0.1),
        'subln_a': gain((N_EVEN, 2 * HEAD_DIM)),
        'qn_b': gain((N_EVEN, HEAD_DIM)),
        'kn_b': gain((N_EVEN, HEAD_DIM)),
        'w_in_odd': nrm((N_ODD, d, ODD_COLS), d ** -0.5),
        'qn_c': gain((N_ODD, HEAD_DIM)),
        'kn_c': gain((N_ODD, HEAD_DIM)),
        'sinks_c': nrm((N_ODD, C_HEADS), 0.5),
    }

def first_block(x, c, ada_w, ada_b, norm_mix, norm_ffn, w_out, ffn_gate, ffn_up, ffn_down,
              w_in_even, qn_a, kn_a, lam_q1, lam_k1, lam_q2, lam_k2, subln_a, qn_b, kn_b,
              w_in_odd, qn_c, kn_c, sinks_c):
    cond = jax.nn.silu(c)
    for l in range(DEPTH):
        mod = cond @ ada_w[l] + ada_b[l]
        sh1, sc1, g1, sh2, sc2, g2 = [m[:, None, :] for m in jnp.split(mod, 6, axis=-1)]
        h = _rms_norm(x, norm_mix[l]) * (1.0 + sc1) + sh1
        if l % 2 == 0:
            e = l // 2
            y = _even_mixer(h, w_in_even[e], qn_a[e], kn_a[e], lam_q1[e], lam_k1[e],
                            lam_q2[e], lam_k2[e], subln_a[e], qn_b[e], kn_b[e], l)
        else:
            o = l // 2
            y = _odd_mixer(h, w_in_odd[o], qn_c[o], kn_c[o], sinks_c[o])
        x = x + g1 * (y @ w_out[l])
        h = _rms_norm(x, norm_ffn[l]) * (1.0 + sc2) + sh2
        x = x + g2 * _swiglu(h, ffn_gate[l], ffn_up[l], ffn_down[l])
    return x


N_MIXERS = 2
N_A_LAYERS = (DEPTH + N_MIXERS - 1) // N_MIXERS
N_B_LAYERS = DEPTH // N_MIXERS

SSM_EXPAND = 2
D_INNER = SSM_EXPAND * D_MODEL
N_HEADS = D_INNER // HEAD_DIM
N_GROUPS = 4
HEADS_PER_GROUP = N_HEADS // N_GROUPS
D_STATE = 128
SSM_CONV = 4
CONV_DIM = D_INNER + 2 * N_GROUPS * D_STATE
D_IN_PROJ = 2 * D_INNER + 2 * N_GROUPS * D_STATE + N_HEADS
CHUNK = 128
DT_MIN = 0.001
DT_MAX = 0.1

CONV_KERNEL = 31

D_FF = -(-8 * D_MODEL // (3 * 256)) * 256

EPS = 1e-5


def rmsnorm(x, g):
    xf = x.astype(jnp.float32)
    y = xf * lax.rsqrt(jnp.mean(xf * xf, axis=-1, keepdims=True) + EPS)
    return (y * g).astype(x.dtype)

def layernorm(x, g, b):
    xf = x.astype(jnp.float32)
    mu = jnp.mean(xf, axis=-1, keepdims=True)
    xc = xf - mu
    var = jnp.mean(xc * xc, axis=-1, keepdims=True)
    return (xc * lax.rsqrt(var + EPS) * g + b).astype(x.dtype)

def gated_group_rmsnorm(y, z, g):
    h = (y * jax.nn.silu(z)).astype(jnp.float32)
    shp = h.shape
    h = h.reshape(shp[:-1] + (N_GROUPS, shp[-1] // N_GROUPS))
    h = h * lax.rsqrt(jnp.mean(h * h, axis=-1, keepdims=True) + EPS)
    return (h.reshape(shp) * g).astype(y.dtype)

def causal_depthwise_conv(x, w, b):
    k = w.shape[0]
    y = lax.conv_general_dilated(
        x, w[:, None, :], window_strides=(1,), padding=[(k - 1, 0)],
        dimension_numbers=("NWC", "WIO", "NWC"), feature_group_count=x.shape[-1])
    return y + b

def segsum(a):
    t = a.shape[-1]
    ar = jnp.broadcast_to(a[..., :, None], a.shape + (t,))
    ar = jnp.where(jnp.tril(jnp.ones((t, t), dtype=bool), -1), ar, 0.0)
    cs = jnp.cumsum(ar, axis=-2)
    return jnp.where(jnp.tril(jnp.ones((t, t), dtype=bool), 0), cs, -jnp.inf)

def ssd_chunked(x, da, bm, cm):
    b, l, h, p = x.shape
    c = l // CHUNK
    dt_ = x.dtype
    x = x.reshape(b, c, CHUNK, N_GROUPS, HEADS_PER_GROUP, p)
    bm = bm.reshape(b, c, CHUNK, N_GROUPS, D_STATE)
    cm = cm.reshape(b, c, CHUNK, N_GROUPS, D_STATE)
    a = da.reshape(b, c, CHUNK, N_GROUPS, HEADS_PER_GROUP).transpose(0, 3, 4, 1, 2)
    a_cs = jnp.cumsum(a, axis=-1)

    lmat = jnp.exp(segsum(a)).astype(dt_)
    cb = jnp.einsum("bclgn,bcsgn->bgcls", cm, bm)
    y_diag = jnp.einsum("bgrcls,bcsgrp->bclgrp", cb[:, :, None] * lmat, x)

    decay_states = jnp.exp(a_cs[..., -1:] - a_cs).astype(dt_)
    xd = x * decay_states.transpose(0, 3, 4, 1, 2)[..., None]
    states = jnp.einsum("bclgn,bclgrp->bcgrpn", bm, xd)

    chunk_tot = jnp.pad(a_cs[..., -1], ((0, 0), (0, 0), (0, 0), (1, 0)))
    decay_chunk = jnp.exp(segsum(chunk_tot))[..., :c, 1:].astype(dt_)
    states_in = jnp.einsum("bgrzj,bjgrpn->bzgrpn", decay_chunk, states)

    state_decay_out = jnp.exp(a_cs).astype(dt_).transpose(0, 3, 4, 1, 2)
    y_off = jnp.einsum("bclgn,bcgrpn->bclgrp", cm, states_in) * state_decay_out[..., None]
    return (y_diag + y_off).reshape(b, l, h, p)

def mamba2_mixer(u, w_in, conv_w, conv_b, dt_bias, a_log, d_skip, gate_norm, w_out):
    b, l, _ = u.shape
    zxbcdt = u @ w_in
    z, xbc, dt = jnp.split(zxbcdt, [D_INNER, D_INNER + CONV_DIM], axis=-1)
    xbc = jax.nn.silu(causal_depthwise_conv(xbc, conv_w, conv_b))
    xs, bm, cm = jnp.split(xbc, [D_INNER, D_INNER + N_GROUPS * D_STATE], axis=-1)
    xs = xs.reshape(b, l, N_HEADS, HEAD_DIM)
    bm = bm.reshape(b, l, N_GROUPS, D_STATE)
    cm = cm.reshape(b, l, N_GROUPS, D_STATE)
    dt = jax.nn.softplus(dt.astype(jnp.float32) + dt_bias.astype(jnp.float32))
    a = -jnp.exp(a_log.astype(jnp.float32))
    y = ssd_chunked(xs * dt[..., None].astype(xs.dtype), dt * a, bm, cm)
    y = y + xs * d_skip[:, None]
    y = gated_group_rmsnorm(y.reshape(b, l, D_INNER), z, gate_norm)
    return y @ w_out

def conformer_conv_module(u, w_pw1, b_pw1, dw_w, dw_b, ln_g, ln_b, w_pw2, b_pw2):
    h = u @ w_pw1 + b_pw1
    a, g = jnp.split(h, 2, axis=-1)
    h = a * jax.nn.sigmoid(g)
    h = causal_depthwise_conv(h, dw_w, dw_b)
    h = jax.nn.silu(layernorm(h, ln_g, ln_b))
    return h @ w_pw2 + b_pw2

def swiglu_ffn(u, w_gate, w_up, w_down):
    return (jax.nn.silu(u @ w_gate) * (u @ w_up)) @ w_down

def second_inputs(seed: int = 0) -> dict:
    key = jax.random.key(seed)
    ks = iter(jax.random.split(key, 40))

    def nrm(shape, scale):
        return jax.random.normal(next(ks), shape, jnp.float32) * scale

    na, nb = N_A_LAYERS, N_B_LAYERS
    x = nrm((BATCH, SEQ, D_MODEL), 1.0)

    u = jax.random.uniform(next(ks), (na, N_HEADS), jnp.float32)
    dt0 = jnp.exp(u * (math.log(DT_MAX) - math.log(DT_MIN)) + math.log(DT_MIN))
    dt0 = jnp.maximum(dt0, 1e-4)
    ssm_dt_bias = dt0 + jnp.log(-jnp.expm1(-dt0))
    ssm_a_log = jnp.log(jax.random.uniform(next(ks), (na, N_HEADS), jnp.float32, 1.0, 16.0))

    return {
        "x": x,
        "ssm_norm": 1.0 + nrm((na, D_MODEL), 0.05),
        "ssm_w_in": nrm((na, D_MODEL, D_IN_PROJ), D_MODEL ** -0.5),
        "ssm_conv_w": nrm((na, SSM_CONV, CONV_DIM), SSM_CONV ** -0.5),
        "ssm_conv_b": nrm((na, CONV_DIM), 0.02),
        "ssm_dt_bias": ssm_dt_bias,
        "ssm_a_log": ssm_a_log,
        "ssm_d": 1.0 + nrm((na, N_HEADS), 0.1),
        "ssm_gate_norm": 1.0 + nrm((na, D_INNER), 0.05),
        "ssm_w_out": nrm((na, D_INNER, D_MODEL), D_INNER ** -0.5),
        "cv_norm": 1.0 + nrm((nb, D_MODEL), 0.05),
        "cv_w_pw1": nrm((nb, D_MODEL, 2 * D_MODEL), D_MODEL ** -0.5),
        "cv_b_pw1": nrm((nb, 2 * D_MODEL), 0.02),
        "cv_dw_w": nrm((nb, CONV_KERNEL, D_MODEL), CONV_KERNEL ** -0.5),
        "cv_dw_b": nrm((nb, D_MODEL), 0.02),
        "cv_ln_g": 1.0 + nrm((nb, D_MODEL), 0.05),
        "cv_ln_b": nrm((nb, D_MODEL), 0.02),
        "cv_w_pw2": nrm((nb, D_MODEL, D_MODEL), D_MODEL ** -0.5),
        "cv_b_pw2": nrm((nb, D_MODEL), 0.02),
        "ffn_norm": 1.0 + nrm((DEPTH, D_MODEL), 0.05),
        "ffn_w_gate": nrm((DEPTH, D_MODEL, D_FF), D_MODEL ** -0.5),
        "ffn_w_up": nrm((DEPTH, D_MODEL, D_FF), D_MODEL ** -0.5),
        "ffn_w_down": nrm((DEPTH, D_FF, D_MODEL), D_FF ** -0.5),
        "final_norm": 1.0 + nrm((D_MODEL,), 0.05),
    }

def second_block(x, ssm_norm, ssm_w_in, ssm_conv_w, ssm_conv_b, ssm_dt_bias, ssm_a_log, ssm_d,
              ssm_gate_norm, ssm_w_out, cv_norm, cv_w_pw1, cv_b_pw1, cv_dw_w, cv_dw_b, cv_ln_g,
              cv_ln_b, cv_w_pw2, cv_b_pw2, ffn_norm, ffn_w_gate, ffn_w_up, ffn_w_down, final_norm):
    h = x
    for i in range(DEPTH):
        j = i // N_MIXERS
        if i % N_MIXERS == 0:
            h = h + mamba2_mixer(rmsnorm(h, ssm_norm[j]), ssm_w_in[j], ssm_conv_w[j], ssm_conv_b[j],
                                 ssm_dt_bias[j], ssm_a_log[j], ssm_d[j], ssm_gate_norm[j], ssm_w_out[j])
        else:
            h = h + conformer_conv_module(rmsnorm(h, cv_norm[j]), cv_w_pw1[j], cv_b_pw1[j], cv_dw_w[j],
                                          cv_dw_b[j], cv_ln_g[j], cv_ln_b[j], cv_w_pw2[j], cv_b_pw2[j])
        h = h + swiglu_ffn(rmsnorm(h, ffn_norm[i]), ffn_w_gate[i], ffn_w_up[i], ffn_w_down[i])
    return rmsnorm(h, final_norm)


def setup_inputs(seed=0):
    out = dict(first_inputs(seed))
    for name, value in second_inputs(seed + 1).items():
        if name != "x":
            out[name + "_2"] = value
    return out


def reference(
    x, c, ada_w, ada_b, norm_mix, norm_ffn, w_out, ffn_gate, ffn_up, ffn_down, w_in_even, qn_a,
    kn_a, lam_q1, lam_k1, lam_q2, lam_k2, subln_a, qn_b, kn_b, w_in_odd, qn_c, kn_c, sinks_c,
    ssm_norm_2, ssm_w_in_2, ssm_conv_w_2, ssm_conv_b_2, ssm_dt_bias_2, ssm_a_log_2, ssm_d_2,
    ssm_gate_norm_2, ssm_w_out_2, cv_norm_2, cv_w_pw1_2, cv_b_pw1_2, cv_dw_w_2, cv_dw_b_2,
    cv_ln_g_2, cv_ln_b_2, cv_w_pw2_2, cv_b_pw2_2, ffn_norm_2, ffn_w_gate_2, ffn_w_up_2,
    ffn_w_down_2, final_norm_2,
):
    x = first_block(
        x, c, ada_w, ada_b, norm_mix, norm_ffn, w_out, ffn_gate, ffn_up, ffn_down, w_in_even,
        qn_a, kn_a, lam_q1, lam_k1, lam_q2, lam_k2, subln_a, qn_b, kn_b, w_in_odd, qn_c, kn_c,
        sinks_c,
    )
    return second_block(
        x, ssm_norm_2, ssm_w_in_2, ssm_conv_w_2, ssm_conv_b_2, ssm_dt_bias_2, ssm_a_log_2,
        ssm_d_2, ssm_gate_norm_2, ssm_w_out_2, cv_norm_2, cv_w_pw1_2, cv_b_pw1_2, cv_dw_w_2,
        cv_dw_b_2, cv_ln_g_2, cv_ln_b_2, cv_w_pw2_2, cv_b_pw2_2, ffn_norm_2, ffn_w_gate_2,
        ffn_w_up_2, ffn_w_down_2, final_norm_2,
    )


_drawn_inputs = setup_inputs


def setup_inputs(seed=0):
    import zlib

    import numpy as np

    out = dict(_drawn_inputs(seed))
    spreads = {}
    factors = {'norm_mix': 2.715,
     'norm_ffn': 4.725,
     'qn_a': 8.0,
     'kn_a': 8.0,
     'lam_q1': 5.867,
     'lam_k1': 8.0,
     'lam_q2': 5.776,
     'lam_k2': 8.0,
     'subln_a': 8.0,
     'qn_b': 8.0,
     'kn_b': 8.0,
     'qn_c': 8.0,
     'kn_c': 8.0,
     'sinks_c': 45.48,
     'cv_norm_2': 68.178,
     'cv_b_pw1_2': 162.968,
     'cv_dw_b_2': 200.0,
     'cv_ln_b_2': 114.229,
     'cv_b_pw2_2': 83.731,
     'ssm_norm_2': 5.618,
     'ssm_conv_b_2': 8.0,
     'ssm_d_2': 57.224,
     'ssm_gate_norm_2': 8.0,
     'cv_ln_g_2': 48.234,
     'ffn_norm_2': 6.909}
    for name, (base, spread) in spreads.items():
        noise = np.random.default_rng([zlib.crc32(name.encode()), seed]).standard_normal(out[name].shape)
        drawn = base * np.exp(spread * noise) if base else spread * noise
        out[name] = __import__('jax').numpy.asarray(drawn.astype(out[name].dtype))
    for name, factor in factors.items():
        out[name] = (out[name] * factor).astype(out[name].dtype)
    return out
```

```python
import math
from contextlib import ExitStack

import concourse.bass as bass
from concourse import mybir

ALU = mybir.AluOpType
ACT = mybir.ActivationFunctionType
AX_X = mybir.AxisListType.X
F32 = mybir.dt.float32
F32R = mybir.dt.float32r

P = 128
S = 512
NT = S // P
D = 1024
DC = D // P
HD = 64
F = 2816
FC = F // P
SLOT_W = 256
SLOT_K = 8
A_HEADS, B_HEADS, I_HEADS, C_HEADS, KV_HEADS = 4, 8, 8, 16, 4
TOPK = 128
DI = 2048
MH = 32
MG = 4
HPG = MH // MG
NCONV = 24
TAPS = 31
BIG = 1.0e30
SCORE_MASKED = -3.0e38
SCORE_TAKEN = -3.3e38
LAM_INIT = 0.8 - 0.6 * math.exp(0.0)

AQ, AK, AV, BQ, BK, BV, IQ, IK, IW = 0, 512, 1024, 1536, 2048, 2112, 2176, 2688, 2752

N_EVEN, N_ODD, N_SSM, N_CV = 12, 7, 21, 8
N_GU, N_DOWN = 2 * FC // 2, 12


def slot_bases(stop):
    parts = [("even", N_EVEN), ("out0", 4), ("gu0", N_GU), ("down0", N_DOWN),
             ("odd", N_ODD), ("out1", 4), ("gu1", N_GU), ("down1", N_DOWN),
             ("ssm", N_SSM), ("ssm_out", 8), ("gu2", N_GU), ("down2", N_DOWN),
             ("cv", N_CV), ("pw2", 4), ("gu3", N_GU), ("down3", N_DOWN)]
    at, out = 0, {}
    for name, n in parts:
        out[name] = at
        at += n
    out["end"] = at
    return out


SLOT = slot_bases(8)

ROWS = {}


def stack_rows():
    at = 0
    for name, n in [("ada_b", 96), ("norm_mix", 16), ("norm_ffn", 16)]:
        ROWS[name] = at
        at += n
    assert at == 128
    for name, n in [("cv_norm", 8), ("cv_b_pw1", 16), ("cv_dw_b", 8), ("cv_ln_g", 8), ("cv_ln_b", 8),
                    ("cv_b_pw2", 8), ("ffn_norm", 16), ("ssm_norm", 8), ("ssm_conv_b", 24),
                    ("final_norm", 8), ("c", 8), ("qk_gain", 6)]:
        ROWS[name] = at
        at += n
    assert at <= 256
    ROWS["rows1"] = at - 128
    at = 256
    for name, n in [("conv_w", 96), ("gate_norm", 16), ("subln", 1)]:
        ROWS[name] = at
        at += n
    ROWS["rows2"] = at - 256
    ROWS["dw_w"] = 384


stack_rows()
NSTACK = 5
N_PARAM_LOADS = 32
N_CONSTS = 15
AHEAD = 2
STACK_ROWS = [128, ROWS["rows1"], ROWS["rows2"], 128, (TAPS - 16) * DC]

def square_counts(sublayers):
    order = [("n0", 8, 1), ("even", 13, 13), ("n1", 8, 1), ("n2", 8, 1), ("odd", 12, 12), ("n3", 8, 1),
             ("n4", 8, 1), ("n5", 8, 1), ("n6", 8, 1), ("ln", 8, 1), ("n7", 8, 1)]
    if sublayers < 8:
        order = order[:order.index((f"n{sublayers}", 8, 1))]
    z = r = 0
    squares, roots = {}, {}
    for name, n, m in order + [("n8", 8, 1)]:
        squares[name], roots[name] = z, r
        z += n
        r += m
    return squares, roots


def build(nc, t, out, sublayers=8):
    with ExitStack() as ctx:
        def sem(name):
            return ctx.enter_context(nc.semaphore(name))

        base = [(nc.sbuf_base + 63) // 64 * 64]

        def place(name, shape, dt=F32, offset=None):
            nbytes = 4
            for n in shape[1:]:
                nbytes *= n
            if offset is None:
                offset = base[0]
                base[0] += (nbytes + 31) // 32 * 32
            return nc.alloc_sbuf_tensor_at(name, shape, dt, offset=offset)

        x_off = base[0]
        x_cm = place("x_cm", [P, DC, S])
        h_hi = place("h_hi", [P, DC, S], F32R)
        h_lo = place("h_lo", [P, DC, S], F32R)
        w_raw = [place(f"w_raw{j}", [P, SLOT_K, SLOT_W]) for j in range(2)]
        w_hi = [place(f"w_hi{j}", [P, SLOT_K, SLOT_W], F32R) for j in range(2)]
        w_lo = [place(f"w_lo{j}", [P, SLOT_K, SLOT_W], F32R) for j in range(2)]
        big = base[0]
        big_size = 2 * FC * S * 4
        base[0] += big_size
        ident = place("ident", [P, P])
        ones = place("ones", [P, P])
        head_ones = place("head_ones", [P, P])
        upto = place("upto", [P, P])
        after = place("after", [P, P])
        dist_off = base[0]
        dist = place("dist", [P, S])
        win_off = base[0]
        dist_win = place("dist_win", [P, 2 * P])
        cols = place("cols", [P, NSTACK * P])
        mod = place("mod", [P, 96])
        cond = place("cond", [P, DC])
        gain = place("gain", [P, 4, DC])
        qk_gain = place("qk_gain", [P, 6])
        neg_lam = place("neg_lam", [P, 1])
        sink_row = place("sink_row", [P, C_HEADS])
        neg_sink = place("neg_sink", [P, C_HEADS])
        dtb_row = place("dtb_row", [P, MH])
        alog_row = place("alog_row", [P, MH])
        dskip_row = place("dskip_row", [P, MH])
        tmp = [place(f"tmp{j}", [P, S]) for j in range(2)]
        sq = [place(f"sq{j}", [P, S]) for j in range(2)]
        root = [place(f"root{j}", [P, S]) for j in range(2)]
        least = place("least", [P, 2, C_HEADS])
        total = place("total", [P, 2, C_HEADS])
        pinv = place("pinv", [P, C_HEADS])
        sink_exp = place("sink_exp", [P, C_HEADS])
        stat = place("stat", [P, 4])
        log_decay = place("log_decay", [P, NT, MH])
        decay = place("decay", [P, 3, NT, MH])
        assert base[0] <= nc.sbuf_usable_end, (base[0], nc.sbuf_usable_end)

        KB = 1024

        def in_big(name, shape, kb, dt=F32):
            nbytes = 4
            for n in shape[1:]:
                nbytes *= n
            assert kb * KB + nbytes <= big_size, name
            return place(name, shape, dt, offset=big + int(kb * KB))

        x_tok = in_big("x_tok", [P, NT, D], 0)
        rows = in_big("rows", [P, NSTACK, P], 16)
        lam_row = in_big("lam_row", [1, 4, HD], 20)
        lam_prod = in_big("lam_prod", [1, 2, HD], 21)
        lam_sum = in_big("lam_sum", [1, 2], 22)
        lam_exp = in_big("lam_exp", [1, 2], 22.5)
        lam_val = in_big("lam_val", [1, 1], 23)
        ada_w = [in_big(f"ada_w{j}", [P, 4, SLOT_W], 46 + 4 * j) for j in range(2)]
        ada_acc = [in_big(f"ada_acc{j}", [P, SLOT_W], 54 + j) for j in range(2)]
        aq = in_big("aq", [P, 4, S], 0)
        ak = in_big("ak", [P, 4, S], 8)
        bq = in_big("bq", [P, 4, S], 16)
        iq = in_big("iq", [P, 4, S], 24)
        bk = in_big("bk", [P, S], 32)
        ik = in_big("ik", [P, S], 34)
        av = in_big("av", [P, NT, S], 36)
        bv = in_big("bv", [P, NT, HD], 44)
        iw = in_big("iw", [P, NT, I_HEADS], 45)
        score = in_big("score", [P, 3, S], 56)
        dist_sel = in_big("dist_sel", [P, 3, S], 62)
        neg_logit = [in_big(f"neg_logit{j}", [P, S], 68 + 2 * j) for j in range(2)]
        prob = [in_big(f"prob{j}", [P, S], 72 + 2 * j) for j in range(4)]
        prob_t = [in_big(f"prob_t{j}", [P, S], 80 + 2 * j) for j in range(2)]
        y_tok = [in_big(f"y_tok{j}", [P, S], 84 + 2 * j) for j in range(2)]
        eps_col = {1e-6: place("eps6", [P, 1]), 1e-5: place("eps5", [P, 1])}
        subln_col = place("subln_col", [P, 1])
        y_wide_buf = root
        top8 = place("top8", [P, 8])
        assert base[0] <= nc.sbuf_usable_end
        cq = in_big("cq", [P, 8, S], 0)
        ck = in_big("ck", [P, 4, S], 16)
        cv = in_big("cv", [P, NT, 2 * P], 24)
        a_hi = in_big("a_hi", [P, FC, S], 0, F32R)
        a_lo = in_big("a_lo", [P, FC, S], FC * S * 4 / KB, F32R)
        z_tok = in_big("z_tok", [P, NT, DI], 0)
        xs_tok = in_big("xs_tok", [P, NT, DI], 32)
        b_tok = in_big("b_tok", [P, NT, MG * P], 64)
        b_cm = in_big("b_cm", [P, MG, S], 72)
        c_cm = in_big("c_cm", [P, MG, S], 80)
        g_hi = in_big("g_hi", [P, NT, DI], 0, F32R)
        g_lo = in_big("g_lo", [P, NT, DI], 32, F32R)
        dt_tok = place("dt_tok", [P, NT, MH], offset=win_off)
        dt_abs = place("dt_abs", [P, NT, MH], offset=win_off + P * 4)
        cb_mask = place("cb_mask", [P, MG * P], offset=dist_off)
        h_off = x_off + DC * S * 4
        xdt = place("xdt", [P, DI], offset=h_off)
        xdec = place("xdec", [P, DI], offset=h_off + 8 * KB)
        state = place("state", [P, DI], offset=h_off + 16 * KB)
        y_ssm = place("y_ssm", [P, DI], offset=h_off + 24 * KB)
        y_out = in_big("y_out", [P, NT, D], 0)
        u_pad = in_big("u_pad", [P, DC, TAPS - 1 + S], 0)
        v_cm = in_big("v_cm", [P, DC, S], 20)

        bank = [ctx.enter_context(nc.psum_tensor(f"bank{j}", [P, S], F32)) for j in range(8)]

        params_in = sem("params_in")
        bcast_in = sem("bcast_in")
        w_full = [sem(f"w_full{j}") for j in range(2)]
        w_rounded = sem("w_rounded")
        w_split = sem("w_split")
        w_used = sem("w_used")
        consts = sem("consts")
        ada_full = [sem(f"ada_full{j}") for j in range(2)]
        ada_step = sem("ada_step")
        ada_col = sem("ada_col")
        rows_t = sem("rows_t")
        cols_ready = sem("cols_ready")
        cond_ready = sem("cond_ready")
        lam_s = sem("lam_s")
        x_t = sem("x_t")
        x_ready = sem("x_ready")
        sq_ready = sem("sq_ready")
        sq_summed = sem("sq_summed")
        root_done = sem("root_done")
        rinv_ready = sem("rinv_ready")
        h_scaled = sem("h_scaled")
        h_shifted = sem("h_shifted")
        h_rounded = sem("h_rounded")
        h_ready = sem("h_ready")
        gains_ready = sem("gains_ready")
        out_t = sem("out_t")
        out_copied = sem("out_copied")
        out_dma = sem("out_dma")
        qk_normed = sem("qk_normed")
        plain_copied = sem("plain_copied")
        s_summed = sem("s_summed")
        s_biased = sem("s_biased")
        s_least = sem("s_least")
        exp_done = sem("exp_done")
        mixed = sem("mixed")
        p_turned = sem("p_turned")
        pt_copied = sem("pt_copied")
        pv_done = sem("pv_done")
        y_stat = sem("y_stat")
        y_scaled = sem("y_scaled")
        y_turned = sem("y_turned")
        y_wide = sem("y_wide")
        y_rounded = sem("y_rounded")
        y_ready = sem("y_ready")
        idx_summed = sem("idx_summed")
        idx_relu = sem("idx_relu")
        idx_added = sem("idx_added")
        silu_done = sem("silu_done")
        gated = sem("gated")
        a_rounded = sem("a_rounded")
        a_ready = sem("a_ready")

        act_chain = sem("act_chain")
        dve_chain = sem("dve_chain")
        y_squares = sem("y_squares")
        y_root = sem("y_root")
        sink_step = sem("sink_step")
        dt_step = sem("dt_step")
        dt_act = sem("dt_act")
        decay_sums = sem("decay_sums")
        decay_ready = sem("decay_ready")
        conv_done = sem("conv_done")
        conv_silu = sem("conv_silu")
        conv_turned = sem("conv_turned")
        conv_copied = sem("conv_copied")
        z_ready = sem("z_ready")
        x_weighted = sem("x_weighted")
        cb_summed = sem("cb_summed")
        cb_masked = sem("cb_masked")
        seg_in = sem("seg_in")
        seg_summed = sem("seg_summed")
        seg_exp = sem("seg_exp")
        mix_ready = sem("mix_ready")
        yd_summed = sem("yd_summed")
        yo_summed = sem("yo_summed")
        st_summed = sem("st_summed")
        st_done = sem("st_done")
        yg_done = sem("yg_done")
        yg_squares = sem("yg_squares")
        yg_root = sem("yg_root")
        ys_scaled = sem("ys_scaled")
        ys_turned = sem("ys_turned")
        ys_wide = sem("ys_wide")
        ys_rounded = sem("ys_rounded")
        ys_ready = sem("ys_ready")
        sig_done = sem("sig_done")
        glu_done = sem("glu_done")
        taps_done = sem("taps_done")
        mean_summed = sem("mean_summed")
        centred = sem("centred")

        XR = {nn: DC * nn for nn in range(8)}
        XR[8] = DC * sublayers
        n_sub = sublayers
        SQ_BASE, ROOT_BASE = square_counts(n_sub)
        block = ctx.enter_context(nc.Block())

        ORDER = ["even", "out0", "gu0", "down0", "odd", "out1", "gu1", "down1", "ssm", "ssm_out", "gu2", "down2",
                 "cv", "pw2", "gu3", "down3", "end"]
        end_slot = SLOT[ORDER[2 * n_sub]]
        FFN_W = [(t["ffn_gate"][0], t["ffn_up"][0], t["ffn_down"][0]), (t["ffn_gate"][1], t["ffn_up"][1], t["ffn_down"][1]),
                 (t["ffn_w_gate_2"][0], t["ffn_w_up_2"][0], t["ffn_w_down_2"][0]),
                 (t["ffn_w_gate_2"][1], t["ffn_w_up_2"][1], t["ffn_w_down_2"][1])]

        def col(name, j=0):
            r = ROWS[name] + j
            return cols[:, r:r + 1]

        def col_range(name, j, n):
            r = ROWS[name] + j
            return cols[:, r:r + n]

        def h_shifts():
            return DC * (n_sub + (1 if n_sub > 6 else 0))

        H_BASE = {0: 0, 1: 8, 2: 16, 3: 24, 4: 32, 5: 40, 6: 48, "ln": 56, 7: 64}
        NORM_EPS = {0: 1e-6, 1: 1e-6, 2: 1e-6, 3: 1e-6}
        NORM_GAIN = {4: ("ssm_norm", 0), 5: ("ffn_norm", 0), 6: ("cv_norm", 0), 7: ("ffn_norm", 8), 8: ("final_norm", 0)}
        SHIFT_COL = {0: 0, 1: 24, 2: 48, 3: 72}

        def ssm_loads(sp, load_slot):
            w = t["ssm_w_in_2"][0]
            n = SLOT["ssm"]
            load_slot(n, [(0, w[:, DI + 3072:DI + 3072 + MH])])
            for j in range(12):
                load_slot(n + 1 + j, [(0, w[:, DI + 256 * j:DI + 256 * j + 256])])
            for j in range(8):
                load_slot(n + 13 + j, [(0, w[:, 256 * j:256 * j + 256])])
            for m in range(4):
                for k in range(2):
                    load_slot(SLOT["ssm_out"] + 2 * m + k,
                              [(0, t["ssm_w_out_2"][0][1024 * k:1024 * k + 1024, 256 * m:256 * m + 256])])

        @block.sync
        def _(sp):
            def row128(ap):
                return ap.rearrange("(r p) -> r p", p=P)

            def load_rows(stack, row, src):
                n = src.shape[0]
                sp.dma_start(rows[row:row + n, stack, 0:src.shape[1]], src).then_inc(params_in, 16)
                loads[0] += 1

            loads = [0]
            load_rows(1, ROWS["c"] - 128, row128(t["c"][0]))
            load_rows(0, ROWS["ada_b"], t["ada_b"].rearrange("l (r p) -> (l r) p", p=P))
            load_rows(0, ROWS["norm_mix"], t["norm_mix"].rearrange("l (r p) -> (l r) p", p=P))
            load_rows(0, ROWS["norm_ffn"], t["norm_ffn"].rearrange("l (r p) -> (l r) p", p=P))
            load_rows(1, ROWS["ffn_norm"] - 128, t["ffn_norm_2"].rearrange("l (r p) -> (l r) p", p=P))
            for name, src in [("cv_norm", "cv_norm_2"), ("cv_b_pw1", "cv_b_pw1_2"), ("cv_dw_b", "cv_dw_b_2"),
                              ("cv_ln_g", "cv_ln_g_2"), ("cv_ln_b", "cv_ln_b_2"), ("cv_b_pw2", "cv_b_pw2_2"),
                              ("ssm_norm", "ssm_norm_2"), ("ssm_conv_b", "ssm_conv_b_2")]:
                load_rows(1, ROWS[name] - 128, row128(t[src][0]))
            load_rows(1, ROWS["final_norm"] - 128, row128(t["final_norm_2"]))
            for j, name in enumerate(["qn_a", "kn_a", "qn_b", "kn_b", "qn_c", "kn_c"]):
                r = ROWS["qk_gain"] - 128 + j
                for half in range(2):
                    sp.dma_start(rows[r:r + 1, 1, HD * half:HD * half + HD], t[name]).then_inc(params_in, 16)
                    loads[0] += 1
            load_rows(2, ROWS["conv_w"] - 256, t["ssm_conv_w_2"][0].rearrange("k (r p) -> (k r) p", p=P))
            load_rows(2, ROWS["gate_norm"] - 256, row128(t["ssm_gate_norm_2"][0]))
            load_rows(2, ROWS["subln"] - 256, t["subln_a"])
            taps = t["cv_dw_w_2"][0].rearrange("k (r p) -> (k r) p", p=P)
            load_rows(3, 0, taps[0:P, :])
            load_rows(4, 0, taps[P:TAPS * DC, :])
            sp.dma_start(x_tok[:], t["x"][0].rearrange("(t p) d -> p t d", p=P)).then_inc(params_in, 16)
            loads[0] += 1
            assert loads[0] == N_PARAM_LOADS, loads[0]
            for j, name in enumerate(["lam_q1", "lam_k1", "lam_q2", "lam_k2"]):
                sp.dma_start(lam_row[0:1, j, :], t[name]).then_inc(bcast_in, 16)
            for dst, name in [(sink_row, "sinks_c"), (dtb_row, "ssm_dt_bias_2"), (alog_row, "ssm_a_log_2"),
                              (dskip_row, "ssm_d_2")]:
                sp.dma_start(dst[:], t[name].partition_broadcast(P)
                             if len(t[name].shape) == 1 else t[name][0].partition_broadcast(P)).then_inc(bcast_in, 16)

            def load_slot(n, parts):
                if n >= 2:
                    sp.wait_ge(w_split, 2 * (n - 1))
                for at, src in parts:
                    sp.dma_start(w_raw[n % 2][:, 0:src.shape[0] // P, at:at + src.shape[1]],
                                 src.rearrange("(k p) m -> p k m", p=P)).then_inc(w_full[n % 2], 16)

            def load_ada(g):
                l, c0 = divmod(g * SLOT_W, 6 * D)
                for half in range(2):
                    hg = 2 * g + half
                    if hg >= 2:
                        sp.wait_ge(ada_step, 4 * (hg - 1))
                    src = t["ada_w"][l, 512 * half:512 * half + 512, c0:c0 + SLOT_W]
                    sp.dma_start(ada_w[half][:], src.rearrange("(k p) m -> p k m", p=P)).then_inc(ada_full[half], 16)

            def load_swiglu(f):
                wg, wu, wd = FFN_W[f]
                n0 = SLOT[f"gu{f}"]
                with sp.Fori(0, FC // 2) as i:
                    for j, w in enumerate((wg, wu)):
                        sp.wait_ge(w_split, i * 4 + 2 * (n0 + j - 1))
                        sp.dma_start(w_raw[(n0 + j) % 2][:], w.rearrange("(k p) m -> p k m", p=P)[
                            :, :, bass.ds(i * SLOT_W, SLOT_W)]).then_inc(w_full[(n0 + j) % 2], 16)
                n0 = SLOT[f"down{f}"]
                with sp.Fori(0, 2) as i:
                    for j in range(6):
                        g, k0 = divmod(j, 3)
                        nk = 8 if k0 < 2 else FC - 16
                        sp.wait_ge(w_split, i * 12 + 2 * (n0 + j - 1))
                        sp.dma_start(w_raw[(n0 + j) % 2][:, 0:nk, :],
                                     wd.rearrange("(k p) m -> p k m", p=P)[
                                         :, 8 * k0:8 * k0 + nk, bass.ds(i * 2 * SLOT_W + g * SLOT_W, SLOT_W)]
                                     ).then_inc(w_full[(n0 + j) % 2], 16)

            we = t["w_in_even"][0]
            even = [[(0, we[:, BK:BK + HD]), (64, we[:, BK:BK + HD]), (128, we[:, IK:IK + HD]), (192, we[:, IK:IK + HD])],
                    [(0, we[:, BV:BV + HD]), (64, we[:, IW:IW + I_HEADS])]]
            for c0 in (IQ, BQ, AQ, AK, AV):
                even += [[(0, we[:, c0 + 256 * j:c0 + 256 * j + 256])] for j in range(2)]
            for n in range(2):
                load_slot(n, even[n])
            for g in range(8):
                load_ada(g)
            even += [[(0, t["w_out"][0][:, 256 * m:256 * m + 256])] for m in range(4)]
            for n in range(N_EVEN):
                load_slot(n + 2, even[n + 2])
                for g in range(8 + 2 * n, 10 + 2 * n):
                    load_ada(g)
            for g in range(32, 48):
                load_ada(g)
            for m in range(2, 4):
                load_slot(SLOT["out0"] + m, even[SLOT["out0"] + m])
            if n_sub > 1:
                load_swiglu(0)
            if n_sub > 2:
                wo = t["w_in_odd"][0]
                odd = [[(64 * q, wo[:, 1024 + 64 * (2 * j + q // 2):1088 + 64 * (2 * j + q // 2)]) for q in range(4)]
                       for j in range(2)]
                odd += [[(0, wo[:, 1280:1536])]]
                odd += [[(0, wo[:, 256 * j:256 * j + 256])] for j in range(4)]
                for n, parts in enumerate(odd):
                    load_slot(SLOT["odd"] + n, parts)
                for m in range(4):
                    load_slot(SLOT["out1"] + m, [(0, t["w_out"][1][:, 256 * m:256 * m + 256])])
            if n_sub > 3:
                load_swiglu(1)
            if n_sub > 4:
                ssm_loads(sp, load_slot)
            if n_sub > 5:
                load_swiglu(2)
            if n_sub > 6:
                for j in range(4):
                    for q, c0 in enumerate((256 * j, D + 256 * j)):
                        load_slot(SLOT["cv"] + 2 * j + q, [(0, t["cv_w_pw1_2"][0][:, c0:c0 + 256])])
                for m in range(4):
                    load_slot(SLOT["pw2"] + m, [(0, t["cv_w_pw2_2"][0][:, 256 * m:256 * m + 256])])
            if n_sub > 7:
                load_swiglu(3)
            sp.wait_ge(out_copied, DC)
            for i in range(NT):
                sp.dma_start(out[0, P * i:P * i + P, :], y_out[:, i, :]).then_inc(out_dma, 16)
            sp.wait_ge(out_dma, 16 * NT)

        tok_slots = {1, 10, 11, SLOT["odd"] + 2, SLOT["ssm"]} | set(range(SLOT["ssm"] + 13, SLOT["ssm"] + 21))
        parts_of = {0: 4, 1: 2, SLOT["odd"]: 4, SLOT["odd"] + 1: 4}
        widths = {1: 72, SLOT["ssm"]: MH}
        loads_upto = {}
        count = [0, 0]
        for n in range(SLOT["end"]):
            loads_upto[n] = count[n % 2]
            count[n % 2] += parts_of.get(n, 1)

        @block.gpsimd
        def _(pool):
            step = [0]

            def then(ins):
                step[0] += 1
                ins.then_inc(consts, 1)
                pool.wait_ge(consts, step[0])

            then(pool.memset(ident[:], 0.0))
            then(pool.memset(ones[:], 1.0))
            then(pool.memset(head_ones[:], 0.0))
            then(pool.memset(upto[:], 1.0))
            then(pool.memset(after[:], 1.0))
            then(pool.iota(dist[:], pattern=[[-1, S]], base=S - P, channel_multiplier=1, allow_small_or_imprecise_dtypes=True))
            then(pool.iota(dist_win[:], pattern=[[-1, 2 * P]], base=P, channel_multiplier=1, allow_small_or_imprecise_dtypes=True))
            then(pool.affine_select(out=ident[:], in_=ident[:], compare_op=ALU.not_equal, fill=1.0, base=0,
                                    pattern=[[-1, P]], channel_multiplier=1))
            then(pool.memset(head_ones[0:HD, 0:HD], 1.0))
            then(pool.memset(head_ones[HD:P, HD:P], 1.0))
            then(pool.affine_select(out=upto[:], in_=upto[:], compare_op=ALU.is_ge, fill=0.0, base=0,
                                    pattern=[[1, P]], channel_multiplier=-1))
            then(pool.affine_select(out=after[:], in_=after[:], compare_op=ALU.is_gt, fill=0.0, base=0,
                                    pattern=[[-1, P]], channel_multiplier=1))
            then(pool.affine_select(out=dist[:], in_=dist[:], compare_op=ALU.is_ge, fill=BIG, base=S - P,
                                    pattern=[[-1, S]], channel_multiplier=1))
            then(pool.affine_select(out=dist_win[:], in_=dist_win[:], compare_op=ALU.is_ge, fill=BIG, base=P,
                                    pattern=[[-1, 2 * P]], channel_multiplier=1))
            then(pool.affine_select(out=dist_win[:], in_=dist_win[:], compare_op=ALU.is_gt, fill=BIG, base=0,
                                    pattern=[[1, 2 * P]], channel_multiplier=-1))
            assert step[0] == N_CONSTS, step[0]

            def low_part(n, parity, nk, width):
                for m in range(2):
                    half = slice(width // 2 * m, width // 2 * m + width // 2)
                    pool.wait_ge(w_rounded, n * 2 + (m + 1))
                    pool.tensor_tensor(w_lo[parity][:, 0:nk, half], w_raw[parity][:, 0:nk, half],
                                       w_hi[parity][:, 0:nk, half].bitcast(F32), ALU.subtract).then_inc(w_split, 1)

            n = 0
            while n < end_slot:
                if n not in [SLOT[f"gu{f}"] for f in range(4)]:
                    low_part(n, n % 2, SLOT_K, widths.get(n, SLOT_W))
                    n += 1
                    continue
                with pool.Fori(0, FC // 2) as i:
                    for j in range(2):
                        low_part(i * 2 + (n + j), (n + j) % 2, SLOT_K, SLOT_W)
                n += N_GU
                with pool.Fori(0, 2) as i:
                    for j in range(6):
                        low_part(i * 6 + (n + j), (n + j) % 2, 8 if j % 3 < 2 else FC - 16, SLOT_W)
                n += N_DOWN

        def ssm_pe(pe, take, freed, slot_tok, slot_cm, h_chunk, out_project):
            n0 = SLOT["ssm"]
            for m in range(2):
                take(m, dt_step, 1)
            dst = [bank[i // 2][:, SLOT_W * (i % 2):SLOT_W * (i % 2) + MH] for i in range(NT)]
            slot_tok(n0, dst, MH, h_chunk(4))

            def turn(c):
                if c >= 20:
                    return
                pe.wait_ge(conv_silu, c + 1)
                take(6 + c % 2, conv_copied, c + 1)
                src = tmp[c % 2][:] if c < 16 else b_cm[:, c - 16, :]
                for i in range(NT):
                    ins = pe.transpose(bank[6 + c % 2][:, P * i:P * i + P], src[:, P * i:P * i + P], ident[:])
                ins.then_inc(conv_turned, 1)

            for s in range(12):
                dst = []
                for q in range(2):
                    c = 2 * s + q
                    dst.append(take((c + 2) % 4, conv_done, c + 1))
                slot_cm(n0 + 1 + s, (n0 + 1 + s) % 2, lambda k: h_hi[:, k, :], lambda k: h_lo[:, k, :], dst)
                if s == 0:
                    pe.wait_ge(dt_step, 3)
                    take(5, decay_ready, 1)
                    for j, tri in enumerate((upto, after, ones)):
                        ins = pe.matmul(bank[5][:, P * j:P * j + P], tri[:], log_decay[:].rearrange("p i h -> p (i h)"),
                                        start=True, stop=True)
                    ins.then_inc(decay_sums, 1)
                if s >= 1:
                    turn(2 * s - 2)
                    turn(2 * s - 1)
            for s in range(8):
                n = n0 + 13 + s
                banks = ((2 * s + 2) % 4, (2 * s + 3) % 4)
                for m in range(2):
                    take(banks[m], z_ready, 2 * s + m + 1)
                slot_tok(n, [bank[banks[i // 2]][:, SLOT_W * (i % 2):SLOT_W * (i % 2) + SLOT_W] for i in range(NT)], SLOT_W)

            for i in range(NT):
                tok = slice(P * i, P * i + P)
                take(0, cb_masked, i + 1)
                pe.wait_ge(conv_silu, NCONV)
                for g in range(MG):
                    ins = pe.matmul(bank[0][:, P * g:P * g + P], b_cm[:, g, tok], c_cm[:, g, tok], start=True, stop=True)
                ins.then_inc(cb_summed, 1)

                def segments(q):
                    Q = 8 * i + q
                    pe.wait_ge(seg_in, Q + 1)
                    take(1 + q % 2, seg_exp, Q + 1)
                    for j in range(4):
                        ins = pe.matmul(bank[1 + q % 2][:, P * j:P * j + P], root[q % 2][:, P * j:P * j + P], upto[:],
                                        start=True, stop=True)
                    ins.then_inc(seg_summed, 1)

                def within(q):
                    Q, g = 8 * i + q, q // 2
                    pe.wait_ge(mix_ready, Q + 1)
                    pe.wait_ge(x_weighted, 2 * i + 2 if i < NT - 1 else 2 * i + 1)
                    if q % 2 == 0:
                        take(3 + g % 2, yg_done, 4 * i + g + 1)
                    for j in range(4):
                        at = 256 * (q % 2) + HD * j
                        ins = pe.matmul(bank[3 + g % 2][:, at:at + HD], sq[q % 2][:, P * j:P * j + P],
                                        xdt[:, HD * (4 * q + j):HD * (4 * q + j) + HD], start=True, stop=True)
                    ins.then_inc(yd_summed, 1)

                def carried(g):
                    if i > 0:
                        pe.wait_ge(st_done, 4 * (i - 1) + g + 1)
                        take(5 + g % 2, yg_done, 4 * i + g + 1)
                        pe.matmul(bank[5 + g % 2][:], c_cm[:, g, tok], state[:, S * g:S * g + S], start=True, stop=True
                                  ).then_inc(yo_summed, 1)

                def own_state(g):
                    if i < NT - 1:
                        take(7, st_done, 4 * i + g + 1)
                        pe.matmul(bank[7][:], b_tok[:, i, P * g:P * g + P], xdec[:, S * g:S * g + S], start=True, stop=True
                                  ).then_inc(st_summed, 1)

                for q in range(8 + 2):
                    if q < 8:
                        segments(q)
                        if q % 2 == 0:
                            carried(q // 2)
                    if q >= 2:
                        within(q - 2)
                        if q % 2 == 1:
                            own_state((q - 2) // 2)
                for k in range(4):
                    K = 4 * i + k
                    pe.wait_ge(ys_scaled, i + 1)
                    take(5 + k % 2, ys_wide, K + 1)
                    for c in range(4):
                        at = P * (4 * k + c)
                        ins = pe.transpose(bank[5 + k % 2][:, P * c:P * c + P], y_ssm[:, at:at + P], ident[:])
                    ins.then_inc(ys_turned, 1)
            gh = g_hi[:].rearrange("p i (c q) -> p c i q", q=P)
            gl = g_lo[:].rearrange("p i (c q) -> p c i q", q=P)
            pe.wait_ge(ys_ready, 16)
            out_project(SLOT["ssm_out"], 40, lambda k: gh[:, k, :, :], lambda k: gl[:, k, :, :], kslots=2)

        def cv_pe(pe, take, freed, slot_cm, h_chunk, out_project):
            n0 = SLOT["cv"]
            for j in range(4):
                for q, by in enumerate((glu_done, sig_done)):
                    dst = [take(2 * q + m, by, 2 * j + m + 1) for m in range(2)]
                    slot_cm(n0 + 2 * j + q, (n0 + 2 * j + q) % 2, lambda k: h_hi[:, k, :], lambda k: h_lo[:, k, :], dst,
                            before=h_chunk(6) if j == 0 and q == 0 else None)
            take(4, centred, DC)
            for c in range(DC):
                pe.wait_ge(taps_done, c + 1)
                ins = pe.matmul(bank[4][:], ones[:], v_cm[:, c, :], start=c == 0, stop=c == DC - 1)
            ins.then_inc(mean_summed, 1)
            z0, r = SQ_BASE["ln"], ROOT_BASE["ln"]
            take(4, root_done, r + 1)
            for c in range(DC):
                pe.wait_ge(sq_ready, z0 + c + 1)
                pe.matmul(bank[4][:], ones[:], sq[(z0 + c) % 2][:], start=c == 0, stop=c == DC - 1).then_inc(sq_summed, 1)
            out_project(SLOT["pw2"], 56, lambda k: h_hi[:, k, :], lambda k: h_lo[:, k, :],
                        before=lambda k: pe.wait_ge(h_ready, H_BASE["ln"] + k + 1))

        @block.tensor
        def _(pe):
            freed = [None] * 8

            def take(b, by, count):
                if freed[b] is not None:
                    pe.wait_ge(*freed[b])
                freed[b] = (by, count)
                return bank[b]

            def slot_cm(n, parity, src_hi, src_lo, dst, nk=SLOT_K, k0=0, first=True, last=True, before=None, widths=(P, P)):
                for m in range(2):
                    pe.wait_ge(w_split, n * 2 + (m + 1))
                    for k in range(nk):
                        if before is not None and m == 0:
                            before(k)
                        hi, lo = w_hi[parity][:, k, P * m:P * m + P], w_lo[parity][:, k, P * m:P * m + P]
                        pe.matmul(dst[m][:], hi, src_hi(k0 + k), start=first and k == 0, stop=False)
                        pe.matmul(dst[m][:], hi, src_lo(k0 + k), start=False, stop=False)
                        ins = pe.matmul(dst[m][:], lo, src_hi(k0 + k), start=False, stop=last and k == nk - 1)
                    ins.then_inc(w_used, 1)

            def slot_tok(n, dst, width, before=None):
                parity = n % 2
                pe.wait_ge(w_split, 2 * n + 2)
                for i in range(NT):
                    for k in range(SLOT_K):
                        if before is not None and i == 0:
                            before(k)
                        a_hi_, a_lo_ = h_hi[:, k, P * i:P * i + P], h_lo[:, k, P * i:P * i + P]
                        b_hi_, b_lo_ = w_hi[parity][:, k, 0:width], w_lo[parity][:, k, 0:width]
                        pe.matmul(dst[i], a_hi_, b_hi_, start=k == 0, stop=False)
                        pe.matmul(dst[i], a_lo_, b_hi_, start=False, stop=False)
                        ins = pe.matmul(dst[i], a_hi_, b_lo_, start=False, stop=k == SLOT_K - 1)
                    if i % 2 == 1:
                        ins.then_inc(w_used, 1)

            def norm_sums(nn):
                z0, r = SQ_BASE[f"n{nn}"], ROOT_BASE[f"n{nn}"]
                take(4, root_done, r + 1)
                for c in range(DC):
                    pe.wait_ge(sq_ready, z0 + c + 1)
                    pe.matmul(bank[4][:], ones[:], sq[(z0 + c) % 2][:], start=c == 0, stop=c == DC - 1).then_inc(sq_summed, 1)

            def h_chunk(nh):
                def wait(k):
                    pe.wait_ge(h_ready, H_BASE[nh] + k + 1)
                return wait

            ada_at = [0]

            def ada_sums(upto_group):
                for g in range(ada_at[0], upto_group):
                    if g == 8:
                        pe.wait_ge(gains_ready, 1)
                    pe.wait_ge(ada_step, 8 * (g + 1))
                    for j in range(2):
                        ins = pe.matmul(bank[7][:, 2 * g + j:2 * g + j + 1], ada_acc[g % 2][:, P * j:P * j + P],
                                        ones[:, 0:1], start=True, stop=True)
                    ins.then_inc(ada_col, 1)
                ada_at[0] = max(ada_at[0], upto_group)

            pe.wait_ge(consts, N_CONSTS)
            pe.wait_ge(params_in, 16 * N_PARAM_LOADS)
            for s in range(NSTACK):
                b, at = (5, s * P) if s < 4 else (6, 0)
                n = STACK_ROWS[s]
                pe.transpose(bank[b][:, at:at + n], rows[0:n, s, :], ident[0:n, 0:n]).then_inc(rows_t, 1)
            freed[5] = (cols_ready, NSTACK)
            freed[6] = (cols_ready, NSTACK)
            for c in range(DC):
                take(c % 4, x_ready, c + 1)
                for i in range(NT):
                    ins = pe.transpose(bank[c % 4][:, P * i:P * i + P], x_tok[:, i, P * c:P * c + P], ident[:])
                ins.then_inc(x_t, 1)
            pe.wait_ge(lam_s, 4)
            take(6, lam_s, 6)
            pe.matmul(bank[6][:, 0:1], ones[0:1, :], lam_val[:], start=True, stop=True).then_inc(lam_s, 1)
            norm_sums(0)
            ada_sums(8)

            def project(parts, nh, base_slot, qk_sq0, qk_root0, qk0, plain0, after_slot=None):
                chunk = 0
                qk = plain = 0
                pending = []

                def head_sums():
                    z, r = pending.pop(0)
                    take(4, root_done, r + 1)
                    pe.wait_ge(sq_ready, z + 1)
                    pe.matmul(bank[4][:], head_ones[:], sq[z % 2][:], start=True, stop=True).then_inc(sq_summed, 1)

                for s, part in enumerate(parts):
                    n = base_slot + s
                    banks = (chunk % 4, (chunk + 1) % 4)
                    before = h_chunk(nh) if s == 0 else None
                    if part[0] == "tok":
                        width = part[1]
                        per = 1 if width > P else 0
                        for m in range(2):
                            take(banks[m], plain_copied, plain0 + plain + 1 + m)
                        dst = [bank[banks[i // 2]][:, SLOT_W * (i % 2):SLOT_W * (i % 2) + width] for i in range(NT)]
                        slot_tok(n, dst, width, before)
                        plain += 2
                        while pending:
                            head_sums()
                    else:
                        for m in range(2):
                            pe.wait_ge(w_split, 2 * n + m + 1)
                            if part[m] == "qk":
                                take(banks[m], qk_normed, qk0 + qk + 1)
                            else:
                                take(banks[m], plain_copied, plain0 + plain + 1)
                                plain += 1
                            for k in range(SLOT_K):
                                if before is not None and m == 0:
                                    before(k)
                                hi, lo = w_hi[n % 2][:, k, P * m:P * m + P], w_lo[n % 2][:, k, P * m:P * m + P]
                                d = bank[banks[m]]
                                pe.matmul(d[:], hi, h_hi[:, k, :], start=k == 0, stop=False)
                                pe.matmul(d[:], hi, h_lo[:, k, :], start=False, stop=False)
                                ins = pe.matmul(d[:], lo, h_hi[:, k, :], start=False, stop=k == SLOT_K - 1)
                            ins.then_inc(w_used, 1)
                            while pending:
                                head_sums()
                            if part[m] == "qk":
                                pending.append((qk_sq0 + qk, qk_root0 + qk))
                                qk += 1
                    chunk += 2
                    if after_slot is not None:
                        after_slot(s)
                while pending:
                    head_sums()

            def out_project(base_slot, x_base, src_hi, src_lo, kslots=1, before=None):
                for m in range(4):
                    dst = []
                    for q in range(2):
                        b = (2 * m + q) % 4
                        dst.append(take(b, x_ready, x_base + 2 * m + q + 1))
                    for k in range(kslots):
                        n = base_slot + kslots * m + k
                        slot_cm(n, n % 2, src_hi, src_lo, dst, k0=SLOT_K * k, first=k == 0, last=k == kslots - 1,
                                before=before if m == 0 else None)

            def swiglu(f, nh):
                n0 = SLOT[f"gu{f}"]
                for b in range(4):
                    take(b, None, None)
                m0 = FC * f
                pe.wait_ge(h_ready, H_BASE[nh] + DC)
                for j in range(2):
                    slot_cm(n0 + j, (n0 + j) % 2, lambda k: h_hi[:, k, :], lambda k: h_lo[:, k, :],
                            [bank[2 * j], bank[2 * j + 1]])
                with pe.Fori(1, FC // 2) as i:
                    for j, (by, c0) in enumerate(((silu_done, m0), (gated, m0 + AHEAD))):
                        pe.wait_ge(by, i * 2 + c0)
                        slot_cm(i * 2 + (n0 + j), (n0 + j) % 2, lambda k: h_hi[:, k, :], lambda k: h_lo[:, k, :],
                                [bank[2 * j], bank[2 * j + 1]])
                pe.wait_ge(gated, m0 + FC + AHEAD)
                n0 = SLOT[f"down{f}"]
                x0 = DC * (2 * f + 2)
                for k in range(FC):
                    pe.wait_ge(a_ready, m0 + k + 1 + AHEAD)

                def down_step(i, waits):
                    for g in range(2):
                        if waits:
                            pe.wait_ge(x_ready, i * 4 + (x0 - 4 + 2 * g + 2))
                        for k0 in range(3):
                            j = 3 * g + k0
                            slot_cm(i * 6 + (n0 + j), (n0 + j) % 2, lambda k: a_hi[:, k, :], lambda k: a_lo[:, k, :],
                                    [bank[2 * g], bank[2 * g + 1]], nk=8 if k0 < 2 else FC - 16, k0=8 * k0,
                                    first=k0 == 0, last=k0 == 2)
                down_step(0, False)
                down_step(1, True)
                for b in range(4):
                    freed[b] = (x_ready, x0 + 5 + b)

            def attention(name, scores, blocks, values, npair, nyb, u0, heads, waits=()):
                for w in waits:
                    pe.wait_ge(*w)
                units = [(i, h) for i in range(NT) for h in range(heads)]
                U = len(units)
                hw = S * nyb // heads

                def do_scores(u):
                    i, h = units[u]
                    for m in range(npair):
                        v = npair * u + m
                        b = v % 3
                        take(b, s_biased, u0["s"] + v + 1)
                        scores(i, h, m, bank[b])

                def do_turn(u):
                    i, h = units[u]
                    b = 3 + (u0["t"] + u) % 2
                    if npair == 2:
                        pe.wait_ge(mixed, u0["mix"] + 2 * (u + 1))
                    else:
                        pe.wait_ge(exp_done, u0["e"] + u + 1)
                    take(b, pt_copied, u0["t"] + u + 1)
                    src = prob[(2 * u) % 4] if npair == 2 else prob[u % 4]
                    for q in range(len(blocks(i))):
                        ins = pe.transpose(bank[b][:, P * q:P * q + P], src[:, P * q:P * q + P], ident[:])
                    ins.then_inc(p_turned, 1)

                def do_values(u):
                    i, h = units[u]
                    pe.wait_ge(pt_copied, u0["t"] + u + 1)
                    yb, at = divmod(h * hw, S)
                    b = 5 + (i * nyb + yb) % 2
                    if at == 0:
                        take(b, y_scaled, u0["y"] + nyb * i + yb + 1)
                    js = blocks(i)
                    for q, j in enumerate(js):
                        ins = pe.matmul(bank[b][:, at:at + hw], prob_t[(u0["t"] + u) % 2][:, P * q:P * q + P], values(j, h),
                                        start=q == 0, stop=q == len(js) - 1)
                    ins.then_inc(pv_done, 1)

                def tile_back(k):
                    pe.wait_ge(y_scaled, u0["y"] + k + 1)
                    take(7, y_wide, u0["y"] + k + 1)
                    for c in range(4):
                        ins = pe.transpose(bank[7][:, P * c:P * c + P], y_tok[k % 2][:, P * c:P * c + P], ident[:])
                    ins.then_inc(y_turned, 1)

                done_rows = 0
                for step in range(U + 3):
                    if step < U:
                        do_scores(step)
                    if 2 <= step < U + 2:
                        do_turn(step - 2)
                    if step >= 3:
                        do_values(step - 3)
                        while done_rows < NT * nyb and (done_rows + 1) * (heads // nyb) <= step - 3 - 1:
                            tile_back(done_rows)
                            done_rows += 1
                while done_rows < NT * nyb:
                    tile_back(done_rows)
                    done_rows += 1

            idx_units = [(i, h) for i in range(1, NT) for h in range(I_HEADS)]

            def index_scores(v):
                i, h = idx_units[v]
                b = 5 + v % 2
                w = P * (i + 1)
                take(b, idx_relu, v + 1)
                lo = HD * (h % 2)
                pe.matmul(bank[b][:, 0:w], iq[lo:lo + HD, h // 2, P * i:P * i + P], ik[lo:lo + HD, 0:w],
                          start=True, stop=True).then_inc(idx_summed, 1)

            def after_even(s):
                ada_sums(8 + 2 * (s + 1))
                if 4 <= s < 10:
                    pe.wait_ge(plain_copied, 7)
                    for v in range(4 * (s - 4), 4 * (s - 4) + 4):
                        index_scores(v)

            EVEN_PARTS = [("qk", "plain"), ("tok", 72), ("plain", "plain"), ("plain", "plain"), ("qk", "qk"), ("qk", "qk"),
                          ("qk", "qk"), ("qk", "qk"), ("qk", "qk"), ("qk", "qk"), ("tok", 256), ("tok", 256)]
            project(EVEN_PARTS, 0, 0, SQ_BASE["even"], ROOT_BASE["even"], 0, 0, after_even)
            ada_sums(48)
            freed[7] = (gains_ready, 2)

            def diff_scores(i, h, m, d):
                lo = HD * m
                pe.matmul(d[:, 0:P * (i + 1)], aq[lo:lo + HD, h, P * i:P * i + P], ak[lo:lo + HD, h, 0:P * (i + 1)],
                          start=True, stop=True).then_inc(s_summed, 1)

            attention("diff", diff_scores, lambda i: list(range(i + 1)), lambda j, h: av[:, j, P * h:P * h + P], 2, 1,
                      dict(s=0, mix=0, e=0, t=0, y=0), A_HEADS, [(qk_normed, 13), (plain_copied, 11)])

            def dsa_scores(i, h, m, d):
                lo = HD * (h % 2)
                pe.matmul(d[:, 0:P * (i + 1)], bq[lo:lo + HD, h // 2, P * i:P * i + P], bk[lo:lo + HD, 0:P * (i + 1)],
                          start=True, stop=True).then_inc(s_summed, 1)

            attention("dsa", dsa_scores, lambda i: list(range(i + 1)), lambda j, h: bv[:, j, :], 1, 1,
                      dict(s=32, mix=32, e=32, t=16, y=4), B_HEADS)

            out_project(SLOT["out0"], 8, lambda k: h_hi[:, k, :], lambda k: h_lo[:, k, :],
                        before=lambda k: pe.wait_ge(y_ready, 8))
            if n_sub > 1:
                norm_sums(1)
                swiglu(0, 1)
            if n_sub > 2:
                norm_sums(2)
                ODD_PARTS = [("qk", "qk"), ("qk", "qk"), ("tok", 256)] + [("qk", "qk")] * 4
                project(ODD_PARTS, 2, SLOT["odd"], SQ_BASE["odd"], ROOT_BASE["odd"], 13, 11)

                def win_scores(i, h, m, d):
                    lo = HD * (h % 2)
                    k0 = P * max(i - 1, 0)
                    k1 = P * (i + 1)
                    pe.matmul(d[:, 0:k1 - k0], cq[lo:lo + HD, h // 2, P * i:P * i + P], ck[lo:lo + HD, h // 4, k0:k1],
                              start=True, stop=True).then_inc(s_summed, 1)

                attention("win", win_scores, lambda i: list(range(max(i - 1, 0), i + 1)),
                          lambda j, h: cv[:, j, HD * (h // 4):HD * (h // 4) + HD], 1, 2,
                          dict(s=64, mix=32, e=64, t=48, y=8), C_HEADS, [(qk_normed, 25), (plain_copied, 13)])
                out_project(SLOT["out1"], 24, lambda k: h_hi[:, k, :], lambda k: h_lo[:, k, :],
                            before=lambda k: pe.wait_ge(y_ready, 16))
            if n_sub > 3:
                norm_sums(3)
                swiglu(1, 3)
            if n_sub > 4:
                norm_sums(4)
                ssm_pe(pe, take, freed, slot_tok, slot_cm, h_chunk, out_project)
            if n_sub > 5:
                norm_sums(5)
                swiglu(2, 5)
            if n_sub > 6:
                norm_sums(6)
                cv_pe(pe, take, freed, slot_cm, h_chunk, out_project)
            if n_sub > 7:
                norm_sums(7)
                swiglu(3, 7)
            norm_sums(8)
            for c in range(DC):
                pe.wait_ge(h_shifted, h_shifts() + c + 1)
                take(c % 4, out_copied, c + 1)
                for i in range(NT):
                    ins = pe.transpose(bank[c % 4][:, P * i:P * i + P], tmp[c % 2][:, P * i:P * i + P], ident[:])
                ins.then_inc(out_t, 1)

        def ssm_act(act, round_half):
            n0 = SLOT["ssm"]
            act.wait_ge(bcast_in, 16 * 8)
            act.activation(alog_row[:], alog_row[:], ACT.Exp).then_inc(dt_act, 1)
            for m in range(2):
                round_half(n0 + 2, m)
            act.wait_ge(dt_step, 2)
            act.activation(dt_abs[:], dt_abs[:], ACT.Exp, scale=-1.0).then_inc(dt_act, 1)
            act.wait_ge(dt_act, 2)
            act.activation(dt_abs[:], dt_abs[:], ACT.Ln, bias=1.0).then_inc(dt_act, 1)

            def conv_act(c):
                act.wait_ge(conv_done, c + 1)
                dst = tmp[c % 2][:] if c < 16 else b_cm[:, c - 16, :] if c < 20 else c_cm[:, c - 20, :]
                act.activation(dst, tmp[c % 2][:], ACT.Silu).then_inc(conv_silu, 1)

            def copy_out(c):
                if c < 20:
                    act.wait_ge(conv_turned, c + 1)
                    src = bank[6 + c % 2][:].rearrange("p (i q) -> p i q", q=P)
                    dst = xs_tok[:, :, P * c:P * c + P] if c < 16 else b_tok[:, :, P * (c - 16):P * (c - 16) + P]
                    act.activation(dst, src, ACT.Copy).then_inc(conv_copied, 1)

            for s in range(12):
                for q in range(2):
                    round_half(n0 + 1 + s + 2, q)
                    conv_act(2 * s + q)
                    if s == 1 and q == 1:
                        act.wait_ge(decay_sums, 1)
                        act.activation(decay[:], bank[5][:, 0:3 * P].rearrange("p (j i h) -> p j i h", j=3, i=NT), ACT.Exp
                                       ).then_inc(decay_ready, 1)
                    if s >= 1:
                        copy_out(2 * s - 2 + q)
            for s in range(8):
                for m in range(2):
                    act.wait_ge(w_used, 2 * (n0 + 13 + s) + m + 1)
                    v = bank[(2 * s + m + 2) % 4][:].rearrange("p (i w) -> p i w", i=2)
                    act.activation(z_tok[:, 2 * m:2 * m + 2, SLOT_W * s:SLOT_W * s + SLOT_W], v, ACT.Silu).then_inc(z_ready, 1)
                for m in range(2):
                    round_half(n0 + 13 + s + 2, m)
            for i in range(NT):
                for q in range(8):
                    Q = 8 * i + q
                    act.wait_ge(seg_summed, Q + 1)
                    if Q >= 2:
                        act.wait_ge(mix_ready, Q - 1)
                    act.activation(tmp[q % 2][:], bank[1 + q % 2][:], ACT.Exp).then_inc(seg_exp, 1)
                for g in range(MG):
                    act.wait_ge(yg_done, 4 * i + g + 1)
                    act.activation(xdt[:, S * g:S * g + S], y_ssm[:, S * g:S * g + S], ACT.Square,
                                   accum_out=stat[:, g:g + 1]).then_inc(yg_squares, 1)
                act.wait_ge(yg_squares, 4 * (i + 1))
                act.activation(stat[:], stat[:], ACT.Sqrt, bias=eps_col[1e-5][:], scale=1.0 / S).then_inc(yg_root, 1)
                for k in range(4):
                    K = 4 * i + k
                    act.wait_ge(ys_wide, K + 1)
                    act.activation(g_hi[:, i, S * k:S * k + S], root[k % 2][:], ACT.Copy).then_inc(ys_rounded, 1)

        @block.scalar
        def _(act):
            chain = [0]

            def link(ins):
                chain[0] += 1
                ins.then_inc(act_chain, 1)
                act.wait_ge(act_chain, chain[0])

            def slot_rows(n):
                for f in range(4):
                    if 0 <= n - SLOT[f"down{f}"] < N_DOWN and (n - SLOT[f"down{f}"]) % 3 == 2:
                        return FC - 16
                return SLOT_K

            def round_half(n, m):
                if n >= end_slot:
                    return
                half_w = widths.get(n, SLOT_W) // 2
                half = slice(half_w * m, half_w * m + half_w)
                nk = slot_rows(n)
                if m == 0:
                    act.wait_ge(w_full[n % 2], 16 * (loads_upto[n] + parts_of.get(n, 1)))
                if n >= 2:
                    whole = n - 2 in tok_slots or n in widths
                    act.wait_ge(w_used, 2 * (n - 2) + (2 if whole else m + 1))
                act.activation(w_hi[n % 2][:, 0:nk, half], w_raw[n % 2][:, 0:nk, half], ACT.Copy).then_inc(w_rounded, 1)

            def norm_squares(nn):
                z0 = SQ_BASE[f"n{nn}"]
                for c in range(DC):
                    act.wait_ge(x_ready, XR[nn] + c + 1)
                    if z0 + c >= 2:
                        act.wait_ge(sq_summed, z0 + c - 1)
                    act.activation(sq[(z0 + c) % 2][:], x_cm[:, c, :], ACT.Square).then_inc(sq_ready, 1)

            def rms(name, z_last, width, eps):
                act.wait_ge(sq_summed, z_last + 1)
                r = ROOT_BASE[name]
                act.activation(root[r % 2][:], bank[4][:], ACT.Sqrt, bias=eps_col[eps][:], scale=1.0 / width
                               ).then_inc(root_done, 1)

            def h_chunks(nn, hb, func, scale, shift, rounded=True):
                for c in range(DC):
                    act.wait_ge(h_scaled, hb + c + 1)
                    act.activation(tmp[c % 2][:], tmp[c % 2][:], func, bias=shift(c), scale=scale(c)).then_inc(h_shifted, 1)
                    if rounded:
                        act.wait_ge(h_shifted, hb + c + 1)
                        act.activation(h_hi[:, c, :], tmp[c % 2][:], ACT.Copy).then_inc(h_rounded, 1)

            def norm(nn):
                norm_squares(nn)
                rms(f"n{nn}", SQ_BASE[f"n{nn}"] + DC - 1, D, NORM_EPS.get(nn, 1e-5))
                if nn < 4:
                    act.wait_ge(gains_ready, 1 if nn == 0 else 2)
                    h_chunks(nn, H_BASE[nn], ACT.Identity, lambda c: gain[:, nn, c:c + 1],
                             lambda c: mod[:, SHIFT_COL[nn] + c:SHIFT_COL[nn] + c + 1])
                elif nn < 8:
                    h_chunks(nn, H_BASE[nn], ACT.Identity, lambda c: col(*g_of(nn, c)), lambda c: 0.0)
                else:
                    h_chunks(nn, h_shifts(), ACT.Identity, lambda c: col(*g_of(nn, c)), lambda c: 0.0, rounded=False)

            def g_of(nn, c):
                name, j = NORM_GAIN[nn]
                return name, j + c

            def project(parts, base_slot, sq0, root0, qk0, dests, after_slot=None):
                qk = 0
                pending = []

                def head_root():
                    z, r, j = pending.pop(0)
                    act.wait_ge(sq_summed, z + 1)
                    if j >= 2:
                        act.wait_ge(qk_normed, j - 1)
                    act.activation(root[r % 2][:], bank[4][:], ACT.Sqrt, bias=eps_col[1e-6][:], scale=1.0 / HD
                                   ).then_inc(root_done, 1)

                for s, part in enumerate(parts):
                    n = base_slot + s
                    if part[0] == "tok":
                        for m in range(2):
                            act.wait_ge(w_used, 2 * n + m + 1)
                            dests(s, m)
                        for m in range(2):
                            round_half(n + 2, m)
                        while pending:
                            head_root()
                        if after_slot is not None:
                            after_slot(s)
                        continue
                    for m in range(2):
                        b = (2 * s + m) % 4
                        act.wait_ge(w_used, 2 * n + m + 1)
                        if part[m] == "qk":
                            z = sq0 + qk
                            if z >= 2:
                                act.wait_ge(sq_summed, z - 1)
                            act.activation(sq[z % 2][:], bank[b][:], ACT.Square).then_inc(sq_ready, 1)
                        else:
                            dests(s, m)
                        round_half(n + 2, m)
                        while pending:
                            head_root()
                        if part[m] == "qk":
                            pending.append((sq0 + qk, root0 + qk, qk0 + qk))
                            qk += 1
                    if after_slot is not None:
                        after_slot(s)
                while pending:
                    head_root()

            def attention(npair, nyb, u0, heads, chunk0, width, kind):
                hpl = heads // nyb
                units = [(i, h) for i in range(NT) for h in range(heads)]
                U, L = len(units), NT * nyb
                for step in range(U + 8):
                    if step < U:
                        i, h = units[step]
                        w = width(i)
                        for m in range(npair):
                            v = u0["s"] + npair * step + m
                            c = npair * h + m
                            act.wait_ge(s_least, v + 1)
                            if npair == 2:
                                if step >= 2:
                                    act.wait_ge(p_turned, u0["t"] + step - 1)
                                dst = prob[(2 * step + m) % 4]
                            else:
                                act.wait_ge(p_turned, u0["t"] + max(step - 3, 0))
                                dst = prob[step % 4]
                            act.activation(dst[:, 0:w], neg_logit[v % 2][:, 0:w], ACT.Exp, scale=-1.0,
                                           bias=least[:, i % 2, c:c + 1], accum_out=total[:, i % 2, c:c + 1]
                                           ).then_inc(exp_done, 1)
                    if 2 <= step < U + 2:
                        u = step - 2
                        i, h = units[u]
                        T = u0["t"] + u
                        act.wait_ge(p_turned, T + 1)
                        if T >= 2:
                            act.wait_ge(pv_done, T - 1)
                        act.activation(prob_t[T % 2][:, 0:width(i)], bank[3 + T % 2][:, 0:width(i)], ACT.Copy
                                       ).then_inc(pt_copied, 1)
                    for k in range(L):
                        Y = u0["y"] + k
                        if step == (k + 1) * hpl + 3:
                            if kind == "diff":
                                act.wait_ge(pv_done, u0["t"] + (k + 1) * hpl)
                                act.activation(tmp[0][:], bank[5 + k % 2][:], ACT.Square).then_inc(y_squares, 1)
                                act.wait_ge(y_stat, k + 1)
                                act.activation(stat[:], stat[:], ACT.Sqrt, bias=eps_col[1e-6][:], scale=1.0 / P
                                               ).then_inc(y_root, 1)
                        if step == (k + 1) * hpl + 5:
                            act.wait_ge(y_turned, Y + 1)
                            if Y >= 2:
                                act.wait_ge(y_ready, Y - 1)
                            c0 = chunk0 + 4 * (k % nyb)
                            ti = k // nyb
                            wide = y_wide_buf[Y % 2]
                            act.activation(wide[:], bank[7][:], ACT.Identity,
                                           scale=subln_col[:] if kind == "diff" else 1.0).then_inc(y_wide, 1)
                            act.wait_ge(y_wide, Y + 1)
                            act.activation(h_hi[:, c0:c0 + 4, P * ti:P * ti + P],
                                           wide[:].rearrange("p (c q) -> p c q", q=P), ACT.Copy).then_inc(y_rounded, 1)
                    if kind == "win" and step >= hpl and step % hpl == 0 and step <= U:
                        k = step // hpl - 1
                        act.wait_ge(sink_step, 3 * k + 1)
                        act.activation(sink_exp[:, 0:hpl], sink_exp[:, 0:hpl], ACT.Exp).then_inc(sink_step, 1)

            def swiglu(f):
                m0, n0 = FC * f, SLOT[f"gu{f}"]

                def round_in_loop(i, j, m):
                    par = (n0 + j) % 2
                    half = slice(P * m, P * m + P)
                    if m == 0:
                        act.wait_ge(w_full[par], i * 16 + 16 * (loads_upto[n0 + 2 + j] + 1))
                    act.wait_ge(w_used, i * 4 + (2 * (n0 + j) + m + 1))
                    act.activation(w_hi[par][:, :, half], w_raw[par][:, :, half], ACT.Copy).then_inc(w_rounded, 1)

                with act.Fori(0, FC // 2) as i:
                    for q in range(2):
                        act.wait_ge(w_used, i * 4 + (2 * n0 + q + 1))
                        act.wait_ge(gated, i * 2 + (m0 + q + AHEAD))
                        act.activation(sq[q][:], bank[q][:], ACT.Silu).then_inc(silu_done, 1)
                        round_in_loop(i, 0, q)
                    for q in range(2):
                        round_in_loop(i, 1, q)
                        act.wait_ge(gated, i * 2 + (m0 + q + 1 + AHEAD))
                        act.activation(a_hi[:, bass.ds(i * 2 + q, 1), :], tmp[q][:].unsqueeze(1), ACT.Copy
                                       ).then_inc(a_rounded, 1)
                round_slots(SLOT[f"down{f}"], N_DOWN)

            def round_slots(base, n):
                for j in range(n):
                    for m in range(2):
                        round_half(base + j + 2, m)

            act.wait_ge(bcast_in, 16 * 8)
            act.wait_ge(cols_ready, NSTACK)
            act.activation(cond[:], col_range("c", 0, DC), ACT.Silu).then_inc(cond_ready, 1)
            act.wait_ge(lam_s, 2)
            act.activation(lam_exp[:], lam_sum[:], ACT.Exp).then_inc(lam_s, 1)
            round_slots(-2, 2)
            norm(0)

            def even_dest(s, m):
                if s == 0:
                    act.activation(ik[:], bank[1][:], ACT.Copy).then_inc(plain_copied, 1)
                elif s == 1:
                    v = bank[2 + m][:].rearrange("p (i w) -> p i w", i=2)
                    act.activation(bv[:, 2 * m:2 * m + 2, :], v[:, :, 0:HD], ACT.Copy)
                    act.activation(iw[:, 2 * m:2 * m + 2, :], v[:, :, HD:HD + I_HEADS], ACT.Copy,
                                   scale=I_HEADS ** -0.5).then_inc(plain_copied, 1)
                elif s in (2, 3):
                    c = 2 * (s - 2) + m
                    act.activation(iq[:, c, :], bank[(2 * s + m) % 4][:], ACT.Copy).then_inc(plain_copied, 1)
                else:
                    v = bank[(2 * s + m) % 4][:].rearrange("p (i w) -> p i w", i=2)
                    act.activation(av[:, 2 * m:2 * m + 2, 256 * (s - 10):256 * (s - 10) + 256], v, ACT.Copy
                                   ).then_inc(plain_copied, 1)

            idx_units = [(i, h) for i in range(1, NT) for h in range(I_HEADS)]

            def index_relu(s):
                if not 4 <= s < 10:
                    return
                for v in range(4 * (s - 4), 4 * (s - 4) + 4):
                    i, h = idx_units[v]
                    act.wait_ge(idx_summed, v + 1)
                    if v >= 2:
                        act.wait_ge(idx_added, v - 1)
                    w = P * (i + 1)
                    act.activation(neg_logit[v % 2][:, 0:w], bank[5 + v % 2][:, 0:w], ACT.Relu, scale=HD ** -0.5
                                   ).then_inc(idx_relu, 1)

            EVEN = [("qk", "plain"), ("tok",), ("plain", "plain"), ("plain", "plain")] + [("qk", "qk")] * 6 + [("tok",), ("tok",)]
            project(EVEN, 0, SQ_BASE["even"], ROOT_BASE["even"], 0, even_dest, index_relu)
            act.wait_ge(w_used, 2 * N_EVEN)
            attention(2, 1, dict(s=0, t=0, y=0), A_HEADS, 0, lambda i: P * (i + 1), "diff")
            attention(1, 1, dict(s=32, t=16, y=4), B_HEADS, 4, lambda i: P * (i + 1), "dsa")
            round_slots(SLOT["out0"], 4)
            if n_sub > 1:
                norm(1)
                swiglu(0)
            if n_sub > 2:
                norm(2)

                def odd_dest(s, m):
                    v = bank[(2 * s + m) % 4][:].rearrange("p (i w) -> p i w", i=2)
                    act.activation(cv[:, 2 * m:2 * m + 2, :], v, ACT.Copy).then_inc(plain_copied, 1)

                ODD = [("qk", "qk"), ("qk", "qk"), ("tok",)] + [("qk", "qk")] * 4
                project(ODD, SLOT["odd"], SQ_BASE["odd"], ROOT_BASE["odd"], 13, odd_dest)
                act.wait_ge(w_used, 2 * SLOT["out1"])
                attention(1, 2, dict(s=64, t=48, y=8), C_HEADS, 0, lambda i: P * (2 if i else 1), "win")
                round_slots(SLOT["out1"], 4)
            if n_sub > 3:
                norm(3)
                swiglu(1)
            if n_sub > 4:
                norm(4)
                ssm_act(act, round_half)
                round_slots(SLOT["ssm_out"], 8)
            if n_sub > 5:
                norm(5)
                swiglu(2)
            if n_sub > 6:
                norm(6)
                for c in range(DC):
                    if c % 2 == 0:
                        round_slots(SLOT["cv"] + c, 1)
                    act.wait_ge(w_used, 2 * (SLOT["cv"] + 2 * (c // 2) + 1) + c % 2 + 1)
                    if c >= 2:
                        act.wait_ge(glu_done, c - 1)
                    act.activation(tmp[c % 2][:], bank[2 + c % 2][:], ACT.Sigmoid, bias=col("cv_b_pw1", DC + c)
                                   ).then_inc(sig_done, 1)
                    round_half(SLOT["cv"] + 2 * (c // 2) + 1 + 2, c % 2)
                z0 = SQ_BASE["ln"]
                for c in range(DC):
                    act.wait_ge(centred, c + 1)
                    act.wait_ge(sq_summed, z0 + c - 1)
                    act.activation(sq[(z0 + c) % 2][:], v_cm[:, c, :], ACT.Square).then_inc(sq_ready, 1)
                rms("ln", z0 + DC - 1, D, 1e-5)
                h_chunks(None, H_BASE["ln"], ACT.Silu, lambda c: col("cv_ln_g", c), lambda c: col("cv_ln_b", c))
                round_slots(SLOT["pw2"], 4)
            if n_sub > 7:
                norm(7)
                swiglu(3)
            norm(8)

        def ssm_dve(dve, link):
            n0 = SLOT["ssm"]
            bc_tile = lambda row: row.unsqueeze(1).to_broadcast([P, NT, MH])
            dve.wait_ge(w_used, 2 * n0 + 2)
            for m in range(2):
                v = bank[m][:].rearrange("p (i w) -> p i w", i=2)[:, :, 0:MH]
                ins = dve.tensor_tensor(dt_tok[:, 2 * m:2 * m + 2, :], v, dtb_row[:].unsqueeze(1).to_broadcast([P, 2, MH]), ALU.add)
            ins.then_inc(dt_step, 1)
            dve.wait_ge(dt_step, 1)
            dve.scalar_tensor_tensor(out=dt_abs[:], in0=dt_tok[:], scalar=-1.0, in1=dt_tok[:], op0=ALU.mult, op1=ALU.max
                                     ).then_inc(dt_step, 1)
            dve.wait_ge(dt_act, 3)
            link(dve.scalar_tensor_tensor(out=dt_tok[:], in0=dt_tok[:], scalar=0.0, in1=dt_abs[:], op0=ALU.max, op1=ALU.add))
            dve.scalar_tensor_tensor(out=log_decay[:], in0=dt_tok[:], scalar=-1.0, in1=bc_tile(alog_row[:]),
                                     op0=ALU.mult, op1=ALU.mult).then_inc(dt_step, 1)
            for c in range(NCONV):
                src, acc = bank[(c + 2) % 4], tmp[c % 2]
                dve.wait_ge(w_used, 2 * (n0 + 1) + c + 1)
                if 2 <= c < 18:
                    dve.wait_ge(conv_turned, c - 1)
                elif c >= 18:
                    dve.wait_ge(conv_silu, c - 1)
                w = lambda k: col("conv_w", NCONV * k + c)
                link(dve.tensor_scalar(acc[:], src[:], w(3), col("ssm_conv_b", c), ALU.mult, ALU.add))
                for k in (2, 1, 0):
                    sh = 3 - k
                    ins = dve.scalar_tensor_tensor(out=acc[:, sh:S], in0=src[:, 0:S - sh], scalar=w(k), in1=acc[:, sh:S],
                                                   op0=ALU.mult, op1=ALU.add)
                    if k:
                        link(ins)
                ins.then_inc(conv_done, 1)
            dve.wait_ge(decay_ready, 1)
            dve.wait_ge(z_ready, 16)
            dve.wait_ge(w_used, 2 * SLOT["ssm_out"])

            def heads(ap, n=HPG):
                return ap.rearrange("p (h e) -> p h e", e=HD)

            for i in range(NT):
                dt_b = dt_tok[:, i, :].unsqueeze(2).to_broadcast([P, MH, HD])
                if i >= 1:
                    dve.wait_ge(yg_squares, 4 * i)
                    dve.wait_ge(st_summed, 4 * i)
                dve.wait_ge(conv_copied, 20)
                dve.tensor_tensor(heads(xdt[:]), heads(xs_tok[:, i, :]), dt_b, ALU.mult).then_inc(x_weighted, 1)
                dve.wait_ge(x_weighted, 2 * i + 1)
                if i < NT - 1:
                    dve.tensor_tensor(heads(xdec[:]), heads(xdt[:]),
                                      decay[:, 1, i, :].unsqueeze(2).to_broadcast([P, MH, HD]), ALU.mult).then_inc(x_weighted, 1)
                dve.wait_ge(cb_summed, i + 1)
                if i >= 1:
                    dve.wait_ge(mix_ready, 8 * i)
                dve.tensor_tensor(cb_mask[:].rearrange("p (g l) -> p g l", l=P), bank[0][:].rearrange("p (g l) -> p g l", l=P),
                                  upto[:].unsqueeze(1).to_broadcast([P, MG, P]), ALU.mult).then_inc(cb_masked, 1)

                def place_decays(q):
                    Q = 8 * i + q
                    if Q >= 2:
                        dve.wait_ge(seg_summed, Q - 1)
                    if q < 2 and i >= 1:
                        dve.wait_ge(ys_ready, 4 * i)
                    dve.tensor_tensor(root[q % 2][:].rearrange("p (j l) -> p j l", l=P),
                                      after[:].unsqueeze(1).to_broadcast([P, 4, P]),
                                      log_decay[:, i, 4 * q:4 * q + 4].unsqueeze(2).to_broadcast([P, 4, P]), ALU.mult
                                      ).then_inc(seg_in, 1)

                def weights(q):
                    Q, g = 8 * i + q, q // 2
                    dve.wait_ge(seg_exp, Q + 1)
                    dve.wait_ge(cb_masked, i + 1)
                    if Q >= 2:
                        dve.wait_ge(yd_summed, Q - 1)
                    dve.tensor_tensor(sq[q % 2][:].rearrange("p (j l) -> p j l", l=P),
                                      tmp[q % 2][:].rearrange("p (j l) -> p j l", l=P),
                                      cb_mask[:, P * g:P * g + P].unsqueeze(1).to_broadcast([P, 4, P]), ALU.mult
                                      ).then_inc(mix_ready, 1)

                def gate_group(g):
                    G = 4 * i + g
                    y = y_ssm[:, S * g:S * g + S]
                    hd = slice(HPG * g, HPG * g + HPG)
                    xg, zg = xs_tok[:, i, S * g:S * g + S], z_tok[:, i, S * g:S * g + S]
                    bc = lambda a: a.unsqueeze(2).to_broadcast([P, HPG, HD])
                    if i >= 1:
                        dve.wait_ge(ys_turned, 4 * i)
                    link(dve.tensor_tensor(heads(y), heads(xg), bc(dskip_row[:, hd]), ALU.mult))
                    dve.wait_ge(yd_summed, 8 * i + 2 * g + 2)
                    link(dve.tensor_tensor(y, bank[3 + g % 2][:], y, ALU.add))
                    if i >= 1:
                        dve.wait_ge(yo_summed, 4 * (i - 1) + g + 1)
                        link(dve.tensor_tensor(heads(xg), heads(bank[5 + g % 2][:]), bc(decay[:, 0, i, hd]), ALU.mult))
                        link(dve.tensor_tensor(y, y, xg, ALU.add))
                    dve.tensor_tensor(y, y, zg, ALU.mult).then_inc(yg_done, 1)
                    if i < NT - 1:
                        st = state[:, S * g:S * g + S]
                        dve.wait_ge(st_summed, G + 1)
                        if i == 0:
                            dve.tensor_copy(st, bank[7][:]).then_inc(st_done, 1)
                        else:
                            link(dve.tensor_tensor(heads(st), heads(st), bc(decay[:, 2, i, hd]), ALU.mult))
                            dve.tensor_tensor(st, st, bank[7][:], ALU.add).then_inc(st_done, 1)

                place_decays(0)
                place_decays(1)
                for q in range(8):
                    weights(q)
                    if q + 2 < 8:
                        place_decays(q + 2)
                    if q in (3, 5, 7):
                        gate_group((q - 3) // 2)
                gate_group(3)
                dve.wait_ge(yg_root, i + 1)
                link(dve.reciprocal(stat[:], stat[:]))
                yv = y_ssm[:].rearrange("p (g e) -> p g e", e=S)
                dve.tensor_tensor(yv, yv, stat[:].unsqueeze(2).to_broadcast([P, MG, S]), ALU.mult).then_inc(ys_scaled, 1)

                def low(k):
                    dve.wait_ge(ys_rounded, 4 * i + k + 1)
                    dve.tensor_tensor(g_lo[:, i, S * k:S * k + S], root[k % 2][:], g_hi[:, i, S * k:S * k + S].bitcast(F32),
                                      ALU.subtract).then_inc(ys_ready, 1)

                for k in range(4):
                    K = 4 * i + k
                    dve.wait_ge(ys_turned, K + 1)
                    if k < 2:
                        dve.wait_ge(seg_summed, 8 * i + 8)
                    else:
                        dve.wait_ge(ys_ready, K - 1)
                    gcols = cols[:, ROWS["gate_norm"] + 4 * k:ROWS["gate_norm"] + 4 * k + 4]
                    dve.tensor_tensor(root[k % 2][:].rearrange("p (c q) -> p c q", q=P),
                                      bank[5 + k % 2][:].rearrange("p (c q) -> p c q", q=P),
                                      gcols.unsqueeze(2).to_broadcast([P, 4, P]), ALU.mult).then_inc(ys_wide, 1)
                    if k >= 1:
                        low(k - 1)
                low(3)

        def cv_dve(dve, link):
            n0 = SLOT["cv"]
            pad = TAPS - 1
            link(dve.memset(u_pad[:, :, 0:pad], 0.0))
            for c in range(DC):
                dve.wait_ge(sig_done, c + 1)
                dve.scalar_tensor_tensor(out=u_pad[:, c, pad:pad + S], in0=bank[c % 2][:], scalar=col("cv_b_pw1", c),
                                         in1=tmp[c % 2][:], op0=ALU.add, op1=ALU.mult).then_inc(glu_done, 1)
                dve.wait_ge(glu_done, c + 1)
                v = v_cm[:, c, :]
                tap = lambda k: cols[:, ROWS["dw_w"] + DC * k + c:ROWS["dw_w"] + DC * k + c + 1]
                link(dve.tensor_scalar(v, u_pad[:, c, 0:S], tap(0), col("cv_dw_b", c), ALU.mult, ALU.add))
                for k in range(1, TAPS):
                    ins = dve.scalar_tensor_tensor(out=v, in0=u_pad[:, c, k:k + S], scalar=tap(k), in1=v,
                                                   op0=ALU.mult, op1=ALU.add)
                    if k < TAPS - 1:
                        link(ins)
                ins.then_inc(taps_done, 1)
            dve.wait_ge(mean_summed, 1)
            for c in range(DC):
                dve.scalar_tensor_tensor(out=v_cm[:, c, :], in0=bank[4][:], scalar=-1.0 / D, in1=v_cm[:, c, :],
                                         op0=ALU.mult, op1=ALU.add).then_inc(centred, 1)
            dve.wait_ge(centred, DC)

        @block.vector
        def _(dve):
            chain = [0]

            def link(ins):
                chain[0] += 1
                ins.then_inc(dve_chain, 1)
                dve.wait_ge(dve_chain, chain[0])

            def rinv(name, job=0):
                r = ROOT_BASE[name] + job
                dve.wait_ge(root_done, r + 1)
                dve.reciprocal(root[r % 2][:], root[r % 2][:]).then_inc(rinv_ready, 1)
                dve.wait_ge(rinv_ready, r + 1)
                return root[r % 2]

            def norm_scale(name, hb, src, turned=False):
                ri = rinv(name)

                def low(c):
                    dve.wait_ge(h_rounded, LOW[0] + c + 1)
                    dve.tensor_tensor(h_lo[:, c, :], tmp[c % 2][:], h_hi[:, c, :].bitcast(F32), ALU.subtract
                                      ).then_inc(h_ready, 1)

                for c in range(DC):
                    if turned:
                        if c >= 2:
                            dve.wait_ge(out_t, c - 1)
                    elif c >= 2:
                        low(c - 2)
                        dve.wait_ge(h_ready, LOW[0] + c - 1)
                    dve.tensor_tensor(tmp[c % 2][:], src(c), ri[:], ALU.mult).then_inc(h_scaled, 1)
                    if turned:
                        if c >= 1:
                            out_copy(c - 1)
                if turned:
                    out_copy(DC - 1)
                else:
                    low(DC - 2)
                    low(DC - 1)
                    LOW[0] += DC

            LOW = [0]

            def out_copy(c):
                dve.wait_ge(out_t, c + 1)
                dve.tensor_copy(y_out[:, :, P * c:P * c + P], bank[c % 4][:].rearrange("p (i q) -> p i q", q=P)
                                ).then_inc(out_copied, 1)

            def norm(nn):
                norm_scale(f"n{nn}", H_BASE[nn], lambda c: x_cm[:, c, :])

            def ada_group(g):
                acc = ada_acc[g % 2]
                if g >= 2:
                    dve.wait_ge(ada_col, g - 1)
                for k in range(8):
                    w = ada_w[k // 4][:, k % 4, :]
                    if k % 4 == 0:
                        dve.wait_ge(ada_full[k // 4], 16 * (g + 1))
                    if k == 0:
                        dve.tensor_scalar(acc[:], w, cond[:, 0:1], None, ALU.mult).then_inc(ada_step, 1)
                    else:
                        dve.wait_ge(ada_step, 8 * g + k)
                        dve.scalar_tensor_tensor(out=acc[:], in0=w, scalar=cond[:, k:k + 1], in1=acc[:],
                                                 op0=ALU.mult, op1=ALU.add).then_inc(ada_step, 1)

            def qk_norm(j, r, b, g, dst):
                dve.wait_ge(root_done, r + 1)
                dve.reciprocal(root[r % 2][:], root[r % 2][:]).then_inc(rinv_ready, 1)
                dve.wait_ge(rinv_ready, r + 1)
                dve.scalar_tensor_tensor(out=dst, in0=bank[b][:], scalar=g, in1=root[r % 2][:], op0=ALU.mult, op1=ALU.mult
                                         ).then_inc(qk_normed, 1)

            def x_add(x0, gates, bias=False, last_slots=lambda m: 0):
                for m in range(4):
                    for q in range(2):
                        c = 2 * m + q
                        dve.wait_ge(w_used, 2 * last_slots(m) + q + 1)
                        dve.scalar_tensor_tensor(out=x_cm[:, c, :], in0=bank[c % 4][:], scalar=gates(c), in1=x_cm[:, c, :],
                                                 op0=ALU.add if bias else ALU.mult, op1=ALU.add).then_inc(x_ready, 1)

            def swiglu(f, gate):
                m0, n0 = FC * f, SLOT[f"gu{f}"]
                with dve.Fori(0, FC // 2) as i:
                    for q in range(2):
                        dve.wait_ge(w_used, i * 4 + (2 * n0 + 2 + q + 1))
                        dve.wait_ge(silu_done, i * 2 + (m0 + q + 1))
                        dve.wait_ge(a_ready, i * 2 + (m0 + AHEAD))
                        dve.tensor_tensor(tmp[q][:], sq[q][:], bank[2 + q][:], ALU.mult).then_inc(gated, 1)
                    for q in range(2):
                        dve.wait_ge(a_rounded, i * 2 + (m0 + q + 1))
                        hi = a_hi[:, bass.ds(i * 2 + q, 1), :].bitcast(F32)
                        dve.tensor_tensor(a_lo[:, bass.ds(i * 2 + q, 1), :], tmp[q][:].unsqueeze(1), hi, ALU.subtract
                                          ).then_inc(a_ready, 1)
                n0 = SLOT[f"down{f}"]
                with dve.Fori(0, 2) as i:
                    for j in range(4):
                        dve.wait_ge(w_used, i * 12 + (2 * (n0 + 3 * (j // 2) + 2) + j % 2 + 1))
                        xc = x_cm[:, bass.ds(i * 4 + j, 1), :].squeeze(1)
                        if gate is None:
                            dve.tensor_tensor(xc, bank[j][:], xc, ALU.add).then_inc(x_ready, 1)
                        else:
                            dve.scalar_tensor_tensor(out=xc, in0=bank[j][:], scalar=mod[:, bass.ds(i * 4 + (gate + j), 1)],
                                                     in1=xc, op0=ALU.mult, op1=ALU.add).then_inc(x_ready, 1)

            dve.memset(eps_col[1e-6][:], 1e-6).then_inc(gated, AHEAD)
            dve.memset(eps_col[1e-5][:], 1e-5).then_inc(a_ready, AHEAD)
            for s in range(NSTACK):
                n = STACK_ROWS[s]
                b, at = (5, s * P) if s < 4 else (6, 0)
                dve.wait_ge(rows_t, NSTACK)
                dve.tensor_copy(cols[:, P * s:P * s + n], bank[b][:, at:at + n]).then_inc(cols_ready, 1)
            for c in range(DC):
                dve.wait_ge(x_t, c + 1)
                dve.tensor_copy(x_cm[:, c, :], bank[c % 4][:]).then_inc(x_ready, 1)
            dve.wait_ge(bcast_in, 16 * 8)
            pairs = lam_row[:].rearrange("o (a b) d -> o a b d", b=2)
            dve.tensor_tensor(lam_prod[:], pairs[:, :, 0, :], pairs[:, :, 1, :], ALU.mult).then_inc(lam_s, 1)
            dve.wait_ge(lam_s, 1)
            dve.tensor_reduce(lam_sum[:], lam_prod[:], AX_X, ALU.add).then_inc(lam_s, 1)
            dve.wait_ge(lam_s, 3)
            link(dve.tensor_tensor(lam_val[:], lam_exp[0:1, 1:2], lam_exp[0:1, 0:1], ALU.subtract))
            dve.tensor_scalar(lam_val[:], lam_val[:], -LAM_INIT, None, ALU.add).then_inc(lam_s, 1)
            dve.wait_ge(lam_s, 5)
            dve.tensor_copy(neg_lam[:], bank[6][:, 0:1]).then_inc(lam_s, 1)
            dve.wait_ge(cols_ready, NSTACK)
            for j in range(6):
                dve.tensor_scalar(qk_gain[:, j:j + 1], col("qk_gain", j), -(HD ** -0.5) if j % 2 == 0 else 1.0, None, ALU.mult)
            dve.tensor_scalar(subln_col[:], col("subln"), 1.0 - LAM_INIT, None, ALU.mult)
            link(dve.tensor_scalar(neg_sink[:], sink_row[:], -1.0, None, ALU.mult))
            dve.wait_ge(cond_ready, 1)
            for g in range(8):
                ada_group(g)
            dve.wait_ge(ada_col, 8)
            link(dve.tensor_tensor(mod[:, 0:16], bank[7][:, 0:16], col_range("ada_b", 0, 16), ALU.add))

            def make_gain(nn, scale0, name, j):
                return dve.scalar_tensor_tensor(out=gain[:, nn, :], in0=mod[:, scale0:scale0 + 8], scalar=1.0,
                                                in1=col_range(name, j, 8), op0=ALU.add, op1=ALU.mult)

            make_gain(0, 8, "norm_mix", 0).then_inc(gains_ready, 1)
            norm(0)
            dve.wait_ge(h_ready, DC)
            link(dve.tensor_scalar(tmp[0][:, 0:P], dist[:, S - P:S], BIG / 10, SCORE_MASKED, ALU.is_ge, ALU.mult))

            idx_units = [(i, h) for i in range(1, NT) for h in range(I_HEADS)]

            def index_add(s):
                for v in range(4 * (s - 4), 4 * (s - 4) + 4):
                    i, h = idx_units[v]
                    w = P * (i + 1)
                    dve.wait_ge(idx_relu, v + 1)
                    sc, r = score[:, i - 1, 0:w], neg_logit[v % 2][:, 0:w]
                    if h == 0:
                        dve.tensor_scalar(sc, r, iw[:, i, 0:1], None, ALU.mult).then_inc(idx_added, 1)
                    else:
                        dve.wait_ge(idx_added, v)
                        dve.scalar_tensor_tensor(out=sc, in0=r, scalar=iw[:, i, h:h + 1], in1=sc, op0=ALU.mult, op1=ALU.add
                                                 ).then_inc(idx_added, 1)

            def take_top(i, r0, r1):
                w = P * (i + 1)
                sc = score[:, i - 1, 0:w]
                if r0 == 0:
                    dve.wait_ge(idx_added, I_HEADS * i)
                    diag = score[:, i - 1, P * i:w]
                    link(dve.tensor_tensor(diag, diag, tmp[0][:, 0:P], ALU.add))
                for _ in range(r0, r1):
                    link(dve.max(top8[:], sc))
                    link(dve.match_replace(sc, top8[:], sc, SCORE_TAKEN))
                if r1 == TOPK // 8:
                    link(dve.tensor_scalar(sc, sc, (SCORE_MASKED + SCORE_TAKEN) / 2 - 1e37, BIG, ALU.is_gt, ALU.mult))
                    link(dve.tensor_tensor(dist_sel[:, i - 1, 0:w], sc, dist[:, S - w:S], ALU.add))

            jr = [0]

            def even_slot(s):
                if s == 0:
                    items = [(0, 3, bk[:])]
                elif s in (4, 5):
                    items = [((2 * s + m) % 4, 2, bq[:, 2 * (s - 4) + m, :]) for m in range(2)]
                elif s in (6, 7):
                    items = [((2 * s + m) % 4, 0, aq[:, 2 * (s - 6) + m, :]) for m in range(2)]
                elif s in (8, 9):
                    items = [((2 * s + m) % 4, 1, ak[:, 2 * (s - 8) + m, :]) for m in range(2)]
                else:
                    items = []
                return items

            pending = []

            def flush_qk(keep):
                while len(pending) > keep:
                    b, g, dst = pending.pop(0)
                    qk_norm(jr[0], ROOT_BASE["even"] + jr[0], b, qk_gain[:, g:g + 1], dst)
                    jr[0] += 1

            for s in range(N_EVEN):
                pending += even_slot(s)
                if s > 0:
                    flush_qk(1 if 4 <= s < 10 else 0)
                for g in range(8 + 2 * s, 10 + 2 * s):
                    ada_group(g)
                if 4 <= s < 10:
                    index_add(s)
                if 6 <= s < 12:
                    i = (s - 6) // 2 + 1
                    take_top(i, 8 * (s % 2), 8 * (s % 2) + 8)
            for g in range(32, 48):
                ada_group(g)
            dve.wait_ge(ada_col, 48)
            link(dve.tensor_tensor(mod[:, 16:96], bank[7][:, 16:96], col_range("ada_b", 16, 80), ALU.add))
            make_gain(1, 32, "norm_ffn", 0)
            make_gain(2, 48 + 8, "norm_mix", 8)
            make_gain(3, 48 + 32, "norm_ffn", 8).then_inc(gains_ready, 1)

            def attention(npair, nyb, u0, heads, chunk0, width, dist_of, kind):
                hpl = heads // nyb
                units = [(i, h) for i in range(NT) for h in range(heads)]
                U, L = len(units), NT * nyb
                slope = [2.0 ** (-8.0 * (h + 1) / heads) for h in range(heads)]
                for step in range(U + 8):
                    if step < U:
                        i, h = units[step]
                        w = width(i)
                        for m in range(npair):
                            v = u0["s"] + npair * step + m
                            c = npair * h + m
                            neg = neg_logit[v % 2][:, 0:w]
                            dve.wait_ge(s_summed, v + 1)
                            if v >= 2:
                                dve.wait_ge(exp_done, v - 1)
                            dve.scalar_tensor_tensor(out=neg, in0=dist_of(i), scalar=slope[h],
                                                     in1=bank[(npair * step + m) % 3][:, 0:w], op0=ALU.mult, op1=ALU.add
                                                     ).then_inc(s_biased, 1)
                            dve.wait_ge(s_biased, v + 1)
                            lc = least[:, i % 2, c:c + 1]
                            if kind == "win":
                                link(dve.tensor_reduce(lc, neg, AX_X, ALU.min))
                                dve.tensor_tensor(lc, lc, neg_sink[:, h:h + 1], ALU.min).then_inc(s_least, 1)
                            else:
                                dve.tensor_reduce(lc, neg, AX_X, ALU.min).then_inc(s_least, 1)
                    if npair == 2 and 1 <= step < U + 1:
                        u = step - 1
                        i, h = units[u]
                        w = width(i)
                        dve.wait_ge(exp_done, u0["s"] + 2 * u + 2)
                        if u >= 1:
                            dve.wait_ge(mixed, 2 * u)
                        link(dve.reciprocal(pinv[:, 0:2], total[:, i % 2, 2 * h:2 * h + 2]))
                        link(dve.tensor_tensor(pinv[:, 1:2], pinv[:, 1:2], neg_lam[:], ALU.mult))
                        p0, p1 = prob[(2 * u) % 4][:, 0:w], prob[(2 * u + 1) % 4][:, 0:w]
                        dve.tensor_scalar(p0, p0, pinv[:, 0:1], None, ALU.mult).then_inc(mixed, 1)
                        dve.wait_ge(mixed, 2 * u + 1)
                        dve.scalar_tensor_tensor(out=p0, in0=p1, scalar=pinv[:, 1:2], in1=p0, op0=ALU.mult, op1=ALU.add
                                                 ).then_inc(mixed, 1)
                    for k in range(L):
                        Y = u0["y"] + k
                        i = k // nyb
                        if kind == "win" and step == (k + 1) * hpl:
                            c0 = hpl * (k % 2)
                            if k >= 1:
                                dve.wait_ge(sink_step, 3 * k)
                            dve.wait_ge(s_least, u0["s"] + (k + 1) * hpl)
                            dve.tensor_tensor(sink_exp[:, 0:hpl], least[:, i % 2, c0:c0 + hpl], sink_row[:, c0:c0 + hpl], ALU.add
                                              ).then_inc(sink_step, 1)
                        if step == (k + 1) * hpl + 4:
                            rows_ = bank[5 + k % 2]
                            if kind == "diff":
                                dve.wait_ge(y_squares, k + 1)
                                if k >= 1:
                                    dve.wait_ge(y_scaled, k)
                                dve.tensor_reduce(stat[:], tmp[0][:].rearrange("p (h e) -> p h e", e=P), AX_X, ALU.add
                                                  ).then_inc(y_stat, 1)
                                dve.wait_ge(y_root, k + 1)
                                link(dve.reciprocal(stat[:], stat[:]))
                                sc, e = stat[:], P
                            else:
                                dve.wait_ge(pv_done, u0["t"] + (k + 1) * hpl)
                                c0 = hpl * (k % nyb)
                                if kind == "win":
                                    dve.wait_ge(sink_step, 3 * k + 2)
                                    tt = total[:, i % 2, c0:c0 + hpl]
                                    dve.tensor_tensor(tt, tt, sink_exp[:, 0:hpl], ALU.add).then_inc(sink_step, 1)
                                    dve.wait_ge(sink_step, 3 * k + 3)
                                dve.wait_ge(mixed, 2 * 16)
                                dve.wait_ge(y_scaled, Y)
                                link(dve.reciprocal(pinv[:, 0:hpl], total[:, i % 2, c0:c0 + hpl]))
                                sc, e = pinv[:, 0:hpl], HD
                            if Y >= 2:
                                dve.wait_ge(y_turned, Y - 1)
                            n = S // e
                            dve.tensor_tensor(y_tok[k % 2][:].rearrange("p (h e) -> p h e", e=e),
                                              rows_[:].rearrange("p (h e) -> p h e", e=e),
                                              sc.unsqueeze(2).to_broadcast([P, n, e]), ALU.mult).then_inc(y_scaled, 1)
                        if step == (k + 1) * hpl + 6:
                            dve.wait_ge(y_rounded, Y + 1)
                            c0 = chunk0 + 4 * (k % nyb)
                            dve.tensor_tensor(h_lo[:, c0:c0 + 4, P * i:P * i + P],
                                              y_wide_buf[Y % 2][:].rearrange("p (c q) -> p c q", q=P),
                                              h_hi[:, c0:c0 + 4, P * i:P * i + P].bitcast(F32), ALU.subtract
                                              ).then_inc(y_ready, 1)

            causal = lambda i: P * (i + 1)
            attention(2, 1, dict(s=0, t=0, y=0), A_HEADS, 0, causal, lambda i: dist[:, S - P * (i + 1):S], "diff")
            attention(1, 1, dict(s=32, t=16, y=4), B_HEADS, 4, causal,
                      lambda i: dist_sel[:, i - 1, 0:P * (i + 1)] if i else dist[:, S - P:S], "dsa")
            x_add(8, lambda c: mod[:, 16 + c:17 + c], last_slots=lambda m: SLOT["out0"] + m)
            if n_sub > 1:
                norm(1)
                swiglu(0, 40)
            if n_sub > 2:
                norm(2)
                for s in (0, 1, 3, 4, 5, 6):
                    for m in range(2):
                        b = (2 * s + m) % 4
                        j = 2 * s + m if s < 2 else 2 * s + m - 2
                        dst = ck[:, j, :] if s < 2 else cq[:, j - 4, :]
                        qk_norm(13 + j, ROOT_BASE["odd"] + j, b, qk_gain[:, 5:6] if s < 2 else qk_gain[:, 4:5], dst)
                attention(1, 2, dict(s=64, t=48, y=8), C_HEADS, 0, lambda i: P * (2 if i else 1),
                          lambda i: dist_win[:] if i else dist_win[:, P:2 * P], "win")
                x_add(24, lambda c: mod[:, 64 + c:65 + c], last_slots=lambda m: SLOT["out1"] + m)
            if n_sub > 3:
                norm(3)
                swiglu(1, 88)
            if n_sub > 4:
                norm(4)
                ssm_dve(dve, link)
                for m in range(4):
                    for q in range(2):
                        c = 2 * m + q
                        dve.wait_ge(w_used, 2 * (SLOT["ssm_out"] + 2 * m + 1) + q + 1)
                        dve.tensor_tensor(x_cm[:, c, :], bank[c % 4][:], x_cm[:, c, :], ALU.add).then_inc(x_ready, 1)
            if n_sub > 5:
                norm(5)
                swiglu(2, None)
            if n_sub > 6:
                norm(6)
                cv_dve(dve, link)
                norm_scale("ln", H_BASE["ln"], lambda c: v_cm[:, c, :])
                x_add(56, lambda c: col("cv_b_pw2", c), bias=True, last_slots=lambda m: SLOT["pw2"] + m)
            if n_sub > 7:
                norm(7)
                swiglu(3, None)
            norm_scale("n8", None, lambda c: x_cm[:, c, :], turned=True)


_INS = ['x', 'c', 'ada_w', 'ada_b', 'norm_mix', 'norm_ffn', 'w_out', 'ffn_gate', 'ffn_up', 'ffn_down', 'w_in_even',
        'qn_a', 'kn_a', 'lam_q1', 'lam_k1', 'lam_q2', 'lam_k2', 'subln_a', 'qn_b', 'kn_b', 'w_in_odd', 'qn_c', 'kn_c',
        'sinks_c', 'ssm_norm_2', 'ssm_w_in_2', 'ssm_conv_w_2', 'ssm_conv_b_2', 'ssm_dt_bias_2', 'ssm_a_log_2', 'ssm_d_2',
        'ssm_gate_norm_2', 'ssm_w_out_2', 'cv_norm_2', 'cv_w_pw1_2', 'cv_b_pw1_2', 'cv_dw_w_2', 'cv_dw_b_2', 'cv_ln_g_2',
        'cv_ln_b_2', 'cv_w_pw2_2', 'cv_b_pw2_2', 'ffn_norm_2', 'ffn_w_gate_2', 'ffn_w_up_2', 'ffn_w_down_2',
        'final_norm_2']
SUBLAYERS = 8


def kernel(**inputs):
    import numpy as np
    import concourse.bacc as bacc
    from concourse.bass_utils import run_bass_kernel_spmd

    nc = bacc.Bacc("TRN2", target_bir_lowering=False, num_devices=1)
    arrays, aps = {}, {}
    for name in _INS:
        a = np.ascontiguousarray(inputs[name])
        arrays[f"in_{name}_dram"] = a
        aps[name] = nc.dram_tensor(f"in_{name}_dram", a.shape, mybir.dt.from_np(a.dtype), kind="ExternalInput").ap()
    out = nc.dram_tensor("out_0_dram", (1, S, D), F32, kind="ExternalOutput").ap()
    build(nc, aps, out, SUBLAYERS)
    return run_bass_kernel_spmd(nc, [arrays], core_ids=[0]).results[0]["out_0_dram"]
```

```python
import math
from contextlib import ExitStack

import concourse.bass as bass
from concourse import mybir

ALU = mybir.AluOpType
ACT = mybir.ActivationFunctionType
AX_X = mybir.AxisListType.X
F32 = mybir.dt.float32
F32R = mybir.dt.float32r

P = 128
S = 512
NT = S // P
D = 1024
DC = D // P
HD = 64
F = 2816
FC = F // P
SLOT_W = 256
SLOT_K = 8
A_HEADS, B_HEADS, I_HEADS, C_HEADS, KV_HEADS = 4, 8, 8, 16, 4
TOPK = 128
DI = 2048
MH = 32
MG = 4
HPG = MH // MG
NCONV = 24
TAPS = 31
PE_TAPS = 8
BIG = 1.0e30
SCORE_MASKED = -3.0e38
SCORE_TAKEN = -3.3e38
LAM_INIT = 0.8 - 0.6 * math.exp(0.0)

AQ, AK, AV, BQ, BK, BV, IQ, IK, IW = 0, 512, 1024, 1536, 2048, 2112, 2176, 2688, 2752

N_EVEN, N_ODD, N_SSM, N_CV = 12, 7, 21, 8
N_GU, N_DOWN = 2 * FC // 2, 12


def slot_bases(stop):
    parts = [("even", N_EVEN), ("out0", 4), ("gu0", N_GU), ("down0", N_DOWN),
             ("odd", N_ODD), ("out1", 4), ("gu1", N_GU), ("down1", N_DOWN),
             ("ssm", N_SSM), ("ssm_out", 8), ("gu2", N_GU), ("down2", N_DOWN),
             ("cv", N_CV), ("pw2", 4), ("gu3", N_GU), ("down3", N_DOWN)]
    at, out = 0, {}
    for name, n in parts:
        out[name] = at
        at += n
    out["end"] = at
    return out


SLOT = slot_bases(8)

ROWS = {}


def stack_rows():
    at = 0
    for name, n in [("ada_b", 96), ("norm_mix", 16), ("c", 8), ("qk_gain", 6)]:
        ROWS[name] = at
        at += n
    ROWS["rows0"] = at
    at = 128
    for name, n in [("norm_ffn", 16), ("cv_norm", 8), ("cv_b_pw1", 16), ("cv_dw_b", 8), ("cv_ln_g", 8), ("cv_ln_b", 8),
                    ("cv_b_pw2", 8), ("ffn_norm", 16), ("ssm_norm", 8), ("ssm_conv_b", 24),
                    ("final_norm", 8)]:
        ROWS[name] = at
        at += n
    assert at <= 256
    ROWS["rows1"] = at - 128
    at = 256
    for name, n in [("conv_w", 96), ("gate_norm", 16), ("subln", 1)]:
        ROWS[name] = at
        at += n
    ROWS["rows2"] = at - 256
    ROWS["dw_w"] = 384


stack_rows()
NSTACK = 5
N_FIRST_LOADS = 10
N_LATER_LOADS = 16
ADA_FIRST, ADA_PROJ, ADA_ALL = 8, 24, 48
ADA_RING = 6
N_CONSTS = 15
AHEAD = 2
STACK_ROWS = [ROWS["rows0"], ROWS["rows1"], ROWS["rows2"], 128, (TAPS - 16) * DC]

def square_counts(sublayers):
    order = [("n0", 8, 1), ("even", 13, 13), ("n1", 8, 1), ("n2", 8, 1), ("odd", 12, 12), ("n3", 8, 1),
             ("n4", 8, 1), ("n5", 8, 1), ("n6", 8, 1), ("ln", 8, 1), ("n7", 8, 1)]
    if sublayers < 8:
        order = order[:order.index((f"n{sublayers}", 8, 1))]
    z = r = 0
    squares, roots = {}, {}
    for name, n, m in order + [("n8", 8, 1)]:
        squares[name], roots[name] = z, r
        z += n
        r += m
    return squares, roots


def build(nc, t, out, sublayers=8):
    with ExitStack() as ctx:
        def sem(name):
            return ctx.enter_context(nc.semaphore(name))

        base = [(nc.sbuf_base + 63) // 64 * 64]

        def place(name, shape, dt=F32, offset=None):
            nbytes = 4
            for n in shape[1:]:
                nbytes *= n
            if offset is None:
                offset = base[0]
                base[0] += (nbytes + 31) // 32 * 32
            return nc.alloc_sbuf_tensor_at(name, shape, dt, offset=offset)

        x_off = base[0]
        x_cm = place("x_cm", [P, DC, S])
        h_hi = place("h_hi", [P, DC, S], F32R)
        h_lo = place("h_lo", [P, DC, S], F32R)
        w_raw = [place(f"w_raw{j}", [P, SLOT_K, SLOT_W]) for j in range(2)]
        w_hi = [place(f"w_hi{j}", [P, SLOT_K, SLOT_W], F32R) for j in range(2)]
        w_lo = [place(f"w_lo{j}", [P, SLOT_K, SLOT_W], F32R) for j in range(2)]
        big = base[0]
        big_size = 2 * FC * S * 4
        base[0] += big_size
        ident = place("ident", [P, P])
        ones = place("ones", [P, P])
        head_ones = place("head_ones", [P, P])
        upto = place("upto", [P, P])
        after = place("after", [P, P])
        dist_off = base[0]
        dist = place("dist", [P, S])
        win_off = base[0]
        dist_win = place("dist_win", [P, 2 * P])
        cols = place("cols", [P, NSTACK * P])
        mod = place("mod", [P, 96])
        cond = place("cond", [P, DC])
        gain = place("gain", [P, 4, DC])
        qk_gain = place("qk_gain", [P, 6])
        neg_lam = place("neg_lam", [P, 1])
        sink_row = place("sink_row", [P, C_HEADS])
        neg_sink = place("neg_sink", [P, C_HEADS])
        dtb_row = place("dtb_row", [P, MH])
        alog_row = place("alog_row", [P, MH])
        dskip_row = place("dskip_row", [P, MH])
        tmp = [place(f"tmp{j}", [P, S]) for j in range(2)]
        sq = [place(f"sq{j}", [P, S]) for j in range(2)]
        root = [place(f"root{j}", [P, S]) for j in range(2)]
        least = place("least", [P, 2, C_HEADS])
        total = place("total", [P, 2, C_HEADS])
        pinv = place("pinv", [P, C_HEADS])
        sink_exp = place("sink_exp", [P, C_HEADS])
        stat = place("stat", [P, 4])
        log_decay = place("log_decay", [P, NT, MH])
        decay = place("decay", [P, 3, NT, MH])
        assert base[0] <= nc.sbuf_usable_end, (base[0], nc.sbuf_usable_end)

        KB = 1024

        def in_big(name, shape, kb, dt=F32):
            nbytes = 4
            for n in shape[1:]:
                nbytes *= n
            assert kb * KB + nbytes <= big_size, name
            return place(name, shape, dt, offset=big + int(kb * KB))

        x_tok = in_big("x_tok", [P, NT, D], 0)
        rows = in_big("rows", [P, NSTACK, P], 16)
        lam_row = in_big("lam_row", [1, 4, HD], 20)
        lam_prod = in_big("lam_prod", [1, 2, HD], 21)
        lam_sum = in_big("lam_sum", [1, 2], 22)
        lam_exp = in_big("lam_exp", [1, 2], 22.5)
        lam_val = in_big("lam_val", [1, 1], 23)
        ada_pair = in_big("ada_pair", [P, 8, SLOT_W], 46)
        ada_w = [in_big(f"ada_w{j}", [P, 4, SLOT_W], 46 + 4 * j if j < 2 else 72 + 4 * (j - 2)) for j in range(ADA_RING)]
        ada_acc = [in_big(f"ada_acc{j}", [P, SLOT_W], 54 + j) for j in range(2)]
        aq = in_big("aq", [P, 4, S], 0)
        ak = in_big("ak", [P, 4, S], 8)
        bq = in_big("bq", [P, 4, S], 16)
        iq = in_big("iq", [P, 4, S], 24)
        bk = in_big("bk", [P, S], 32)
        ik = in_big("ik", [P, S], 34)
        av = in_big("av", [P, NT, S], 36)
        bv = in_big("bv", [P, NT, HD], 44)
        iw = in_big("iw", [P, NT, I_HEADS], 45)
        score = in_big("score", [P, 3, S], 56)
        dist_sel = in_big("dist_sel", [P, 3, S], 62)
        neg_logit = [in_big(f"neg_logit{j}", [P, S], 68 + 2 * j) for j in range(2)]
        prob = [in_big(f"prob{j}", [P, S], 72 + 2 * j) for j in range(4)]
        prob_t = [in_big(f"prob_t{j}", [P, S], 80 + 2 * j) for j in range(2)]
        y_tok = [in_big(f"y_tok{j}", [P, S], 84 + 2 * j) for j in range(2)]
        spare = place("spare", [P, 1])
        stage = tmp + sq
        eps_col = {1e-6: place("eps6", [P, 1]), 1e-5: place("eps5", [P, 1])}
        subln_col = place("subln_col", [P, 1])
        y_wide_buf = root
        top8 = place("top8", [P, 8])
        assert base[0] <= nc.sbuf_usable_end
        cq = in_big("cq", [P, 8, S], 0)
        ck = in_big("ck", [P, 4, S], 16)
        cv = in_big("cv", [P, NT, 2 * P], 24)
        a_hi = in_big("a_hi", [P, FC, S], 0, F32R)
        a_lo = in_big("a_lo", [P, FC, S], FC * S * 4 / KB, F32R)
        z_tok = in_big("z_tok", [P, NT, DI], 0)
        xs_tok = in_big("xs_tok", [P, NT, DI], 32)
        b_tok = in_big("b_tok", [P, NT, MG * P], 64)
        b_cm = in_big("b_cm", [P, MG, S], 72)
        c_cm = in_big("c_cm", [P, MG, S], 80)
        g_hi = in_big("g_hi", [P, NT, DI], 0, F32R)
        g_lo = in_big("g_lo", [P, NT, DI], 32, F32R)
        dt_tok = place("dt_tok", [P, NT, MH], offset=win_off)
        dt_abs = place("dt_abs", [P, NT, MH], offset=win_off + P * 4)
        cb_mask = place("cb_mask", [P, MG * P], offset=dist_off)
        h_off = x_off + DC * S * 4
        xdt = place("xdt", [P, DI], offset=h_off)
        xdec = place("xdec", [P, DI], offset=h_off + 8 * KB)
        state = place("state", [P, DI], offset=h_off + 16 * KB)
        y_ssm = place("y_ssm", [P, DI], offset=h_off + 24 * KB)
        y_out = in_big("y_out", [P, NT, D], 0)
        u_pad = in_big("u_pad", [P, DC, TAPS - 1 + S], 0)
        v_cm = in_big("v_cm", [P, DC, S], 20)

        bank = [ctx.enter_context(nc.psum_tensor(f"bank{j}", [P, S], F32)) for j in range(8)]

        params_in = sem("params_in")
        params_later = sem("params_later")
        bcast_in = sem("bcast_in")
        w_full = [sem(f"w_full{j}") for j in range(2)]
        w_rounded = sem("w_rounded")
        w_split = sem("w_split")
        w_used = sem("w_used")
        consts = sem("consts")
        ada_full = [sem(f"ada_full{j}") for j in range(ADA_RING)]
        ada_dve = sem("ada_dve")
        ada_pool = sem("ada_pool")
        ada_wide_in = [sem(f"ada_wide_in{j}") for j in range(3)]
        ada_col = sem("ada_col")
        rows_t = sem("rows_t")
        cols_ready = sem("cols_ready")
        cond_ready = sem("cond_ready")
        lam_s = sem("lam_s")
        x_t = sem("x_t")
        x_ready = sem("x_ready")
        sq_ready = sem("sq_ready")
        sq_summed = sem("sq_summed")
        root_done = sem("root_done")
        rinv_ready = sem("rinv_ready")
        h_scaled = sem("h_scaled")
        h_shifted = sem("h_shifted")
        h_rounded = sem("h_rounded")
        h_ready = sem("h_ready")
        gains_ready = sem("gains_ready")
        out_t = sem("out_t")
        out_copied = sem("out_copied")
        out_dma = sem("out_dma")
        qk_normed = sem("qk_normed")
        plain_copied = sem("plain_copied")
        s_summed = sem("s_summed")
        s_biased = sem("s_biased")
        s_least = sem("s_least")
        exp_done = sem("exp_done")
        mixed = sem("mixed")
        p_turned = sem("p_turned")
        pt_copied = sem("pt_copied")
        pv_done = sem("pv_done")
        y_stat = sem("y_stat")
        y_scaled = sem("y_scaled")
        y_turned = sem("y_turned")
        y_wide = sem("y_wide")
        y_rounded = sem("y_rounded")
        y_ready = sem("y_ready")
        idx_summed = sem("idx_summed")
        idx_relu = sem("idx_relu")
        idx_added = sem("idx_added")
        silu_done = sem("silu_done")
        gated = sem("gated")
        a_rounded = sem("a_rounded")
        a_ready = sem("a_ready")

        act_chain = sem("act_chain")
        dve_chain = sem("dve_chain")
        y_squares = sem("y_squares")
        y_root = sem("y_root")
        sink_step = sem("sink_step")
        dt_step = sem("dt_step")
        dt_act = sem("dt_act")
        decay_sums = sem("decay_sums")
        decay_ready = sem("decay_ready")
        conv_done = sem("conv_done")
        conv_silu = sem("conv_silu")
        conv_turned = sem("conv_turned")
        conv_copied = sem("conv_copied")
        z_ready = sem("z_ready")
        x_weighted = sem("x_weighted")
        cb_summed = sem("cb_summed")
        cb_masked = sem("cb_masked")
        seg_in = sem("seg_in")
        seg_summed = sem("seg_summed")
        seg_exp = sem("seg_exp")
        mix_ready = sem("mix_ready")
        yd_summed = sem("yd_summed")
        yo_summed = sem("yo_summed")
        st_summed = sem("st_summed")
        st_done = sem("st_done")
        yg_done = sem("yg_done")
        yg_squares = sem("yg_squares")
        yg_root = sem("yg_root")
        ys_scaled = sem("ys_scaled")
        ys_turned = sem("ys_turned")
        ys_wide = sem("ys_wide")
        ys_rounded = sem("ys_rounded")
        ys_ready = sem("ys_ready")
        sig_done = sem("sig_done")
        glu_done = sem("glu_done")
        diag_ready = sem("diag_ready")
        pe_taps_done = sem("pe_taps_done")
        taps_done = sem("taps_done")
        skip_done = sem("skip_done")
        mean_summed = sem("mean_summed")
        centred = sem("centred")

        XR = {nn: DC * nn for nn in range(8)}
        XR[8] = DC * sublayers
        n_sub = sublayers
        SQ_BASE, ROOT_BASE = square_counts(n_sub)
        block = ctx.enter_context(nc.Block())

        ORDER = ["even", "out0", "gu0", "down0", "odd", "out1", "gu1", "down1", "ssm", "ssm_out", "gu2", "down2",
                 "cv", "pw2", "gu3", "down3", "end"]
        end_slot = SLOT[ORDER[2 * n_sub]]
        FFN_W = [(t["ffn_gate"][0], t["ffn_up"][0], t["ffn_down"][0]), (t["ffn_gate"][1], t["ffn_up"][1], t["ffn_down"][1]),
                 (t["ffn_w_gate_2"][0], t["ffn_w_up_2"][0], t["ffn_w_down_2"][0]),
                 (t["ffn_w_gate_2"][1], t["ffn_w_up_2"][1], t["ffn_w_down_2"][1])]

        def col(name, j=0):
            r = ROWS[name] + j
            return cols[:, r:r + 1]

        def col_range(name, j, n):
            r = ROWS[name] + j
            return cols[:, r:r + n]

        def ada_half(g, half):
            hg = 2 * g + half
            return hg % ADA_RING, hg // ADA_RING

        def ada_wide(g):
            j = (g - ADA_PROJ) % 3
            return (ada_pair, w_raw[0], w_raw[1])[j], j

        def h_made():
            return DC * (n_sub + (1 if n_sub > 6 else 0))

        H_BASE = {0: 0, 1: 8, 2: 16, 3: 24, 4: 32, 5: 40, 6: 48, "ln": 56, 7: 64}
        NORM_EPS = {0: 1e-6, 1: 1e-6, 2: 1e-6, 3: 1e-6}
        NORM_GAIN = {4: ("ssm_norm", 0), 5: ("ffn_norm", 0), 6: ("cv_norm", 0), 7: ("ffn_norm", 8), 8: ("final_norm", 0)}
        SHIFT_COL = {0: 0, 1: 24, 2: 48, 3: 72}

        def ssm_loads(sp, load_slot):
            w = t["ssm_w_in_2"][0]
            n = SLOT["ssm"]
            load_slot(n, [(0, w[:, DI + 3072:DI + 3072 + MH])])
            for j in range(12):
                load_slot(n + 1 + j, [(0, w[:, DI + 256 * j:DI + 256 * j + 256])])
            for j in range(8):
                load_slot(n + 13 + j, [(0, w[:, 256 * j:256 * j + 256])])
            for m in range(4):
                for k in range(2):
                    load_slot(SLOT["ssm_out"] + 2 * m + k,
                              [(0, t["ssm_w_out_2"][0][1024 * k:1024 * k + 1024, 256 * m:256 * m + 256])])

        @block.sync
        def _(sp):
            def row128(ap):
                return ap.rearrange("(r p) -> r p", p=P)

            def load_rows(stack, row, src, signal=params_later):
                n = src.shape[0]
                sp.dma_start(rows[row:row + n, stack, 0:src.shape[1]], src).then_inc(signal, 16)

            load_rows(0, ROWS["c"], row128(t["c"][0]), params_in)
            sp.dma_start(x_tok[:], t["x"][0].rearrange("(t p) d -> p t d", p=P)).then_inc(params_in, 16)
            load_rows(0, ROWS["ada_b"], t["ada_b"].rearrange("l (r p) -> (l r) p", p=P), params_in)
            load_rows(0, ROWS["norm_mix"], t["norm_mix"].rearrange("l (r p) -> (l r) p", p=P), params_in)
            for j, name in enumerate(["qn_a", "kn_a", "qn_b", "kn_b", "qn_c", "kn_c"]):
                r = ROWS["qk_gain"] + j
                sp.dma_start(rows[r:r + 1, 0, :].rearrange("o (a d) -> o a d", a=2),
                             t[name].unsqueeze(1).to_broadcast([1, 2, HD])).then_inc(params_in, 16)

            def later_loads():
                load_rows(1, ROWS["norm_ffn"] - 128, t["norm_ffn"].rearrange("l (r p) -> (l r) p", p=P))
                load_rows(1, ROWS["ffn_norm"] - 128, t["ffn_norm_2"].rearrange("l (r p) -> (l r) p", p=P))
                for name, src in [("cv_norm", "cv_norm_2"), ("cv_b_pw1", "cv_b_pw1_2"), ("cv_dw_b", "cv_dw_b_2"),
                                  ("cv_ln_g", "cv_ln_g_2"), ("cv_ln_b", "cv_ln_b_2"), ("cv_b_pw2", "cv_b_pw2_2"),
                                  ("ssm_norm", "ssm_norm_2"), ("ssm_conv_b", "ssm_conv_b_2")]:
                    load_rows(1, ROWS[name] - 128, row128(t[src][0]))
                load_rows(1, ROWS["final_norm"] - 128, row128(t["final_norm_2"]))
                load_rows(2, ROWS["conv_w"] - 256, t["ssm_conv_w_2"][0].rearrange("k (r p) -> (k r) p", p=P))
                load_rows(2, ROWS["gate_norm"] - 256, row128(t["ssm_gate_norm_2"][0]))
                load_rows(2, ROWS["subln"] - 256, t["subln_a"])
                taps = t["cv_dw_w_2"][0].rearrange("k (r p) -> (k r) p", p=P)
                load_rows(3, 0, taps[0:P, :])
                load_rows(4, 0, taps[P:TAPS * DC, :])
                bcast_loads()

            def bcast_loads():
                for j, name in enumerate(["lam_q1", "lam_k1", "lam_q2", "lam_k2"]):
                    sp.dma_start(lam_row[0:1, j, :], t[name]).then_inc(bcast_in, 16)
                for dst, name in [(sink_row, "sinks_c"), (dtb_row, "ssm_dt_bias_2"), (alog_row, "ssm_a_log_2"),
                                  (dskip_row, "ssm_d_2")]:
                    sp.dma_start(dst[:], t[name].partition_broadcast(P)
                                 if len(t[name].shape) == 1 else t[name][0].partition_broadcast(P)).then_inc(bcast_in, 16)

            def load_slot(n, parts):
                if n >= 2:
                    sp.wait_ge(w_split, 2 * (n - 1))
                for at, src in parts:
                    sp.dma_start(w_raw[n % 2][:, 0:src.shape[0] // P, at:at + src.shape[1]],
                                 src.rearrange("(k p) m -> p k m", p=P)).then_inc(w_full[n % 2], 16)

            def load_ada(g):
                l, c0 = divmod(g * SLOT_W, 6 * D)
                if g >= ADA_PROJ:
                    w, j = ada_wide(g)
                    if g >= ADA_PROJ + 3:
                        sp.wait_ge(ada_col, g - 2)
                    elif j == 0:
                        sp.wait_ge(ada_col, ADA_PROJ)
                    else:
                        sp.wait_ge(w_split, 2 * (SLOT["out0"] + j))
                    sp.dma_start(w[:], t["ada_w"][l, :, c0:c0 + SLOT_W].rearrange("(k p) m -> p k m", p=P)
                                 ).then_inc(ada_wide_in[j], 16)
                    return
                for half in range(2):
                    buf, _ = ada_half(g, half)
                    if g >= ADA_RING // 2:
                        sp.wait_ge(ada_dve, 8 * (g - 3) + 4 * half + 4)
                    src = t["ada_w"][l, 512 * half:512 * half + 512, c0:c0 + SLOT_W]
                    sp.dma_start(ada_w[buf][:], src.rearrange("(k p) m -> p k m", p=P)).then_inc(ada_full[buf], 16)

            def load_swiglu(f):
                wg, wu, wd = FFN_W[f]
                n0 = SLOT[f"gu{f}"]
                with sp.Fori(0, FC // 2) as i:
                    for j, w in enumerate((wg, wu)):
                        sp.wait_ge(w_split, i * 4 + 2 * (n0 + j - 1))
                        sp.dma_start(w_raw[(n0 + j) % 2][:], w.rearrange("(k p) m -> p k m", p=P)[
                            :, :, bass.ds(i * SLOT_W, SLOT_W)]).then_inc(w_full[(n0 + j) % 2], 16)
                n0 = SLOT[f"down{f}"]
                with sp.Fori(0, 2) as i:
                    for j in range(6):
                        g, k0 = divmod(j, 3)
                        nk = 8 if k0 < 2 else FC - 16
                        sp.wait_ge(w_split, i * 12 + 2 * (n0 + j - 1))
                        sp.dma_start(w_raw[(n0 + j) % 2][:, 0:nk, :],
                                     wd.rearrange("(k p) m -> p k m", p=P)[
                                         :, 8 * k0:8 * k0 + nk, bass.ds(i * 2 * SLOT_W + g * SLOT_W, SLOT_W)]
                                     ).then_inc(w_full[(n0 + j) % 2], 16)

            we = t["w_in_even"][0]
            even = [[(0, we[:, BK:BK + HD]), (64, we[:, BK:BK + HD]), (128, we[:, IK:IK + HD]), (192, we[:, IK:IK + HD])],
                    [(0, we[:, BV:BV + HD]), (64, we[:, IW:IW + I_HEADS])]]
            for c0 in (IQ, BQ, AQ, AK, AV):
                even += [[(0, we[:, c0 + 256 * j:c0 + 256 * j + 256])] for j in range(2)]
            for g in range(3):
                load_ada(g)
            for n in range(2):
                load_slot(n, even[n])
            for g in range(3, ADA_FIRST):
                load_ada(g)
            even += [[(0, t["w_out"][0][:, 256 * m:256 * m + 256])] for m in range(4)]
            for n in range(N_EVEN):
                load_slot(n + 2, even[n + 2])
                if n == 0:
                    later_loads()
                if n < 8:
                    for g in range(ADA_FIRST + 2 * n, ADA_FIRST + 2 * n + 2):
                        load_ada(g)
            for g in range(ADA_PROJ, ADA_ALL):
                load_ada(g)
            sp.wait_ge(ada_col, ADA_ALL)
            for m in range(2, 4):
                load_slot(SLOT["out0"] + m, even[SLOT["out0"] + m])
            if n_sub > 1:
                load_swiglu(0)
            if n_sub > 2:
                wo = t["w_in_odd"][0]
                odd = [[(64 * q, wo[:, 1024 + 64 * (2 * j + q // 2):1088 + 64 * (2 * j + q // 2)]) for q in range(4)]
                       for j in range(2)]
                odd += [[(0, wo[:, 1280:1536])]]
                odd += [[(0, wo[:, 256 * j:256 * j + 256])] for j in range(4)]
                for n, parts in enumerate(odd):
                    load_slot(SLOT["odd"] + n, parts)
                for m in range(4):
                    load_slot(SLOT["out1"] + m, [(0, t["w_out"][1][:, 256 * m:256 * m + 256])])
            if n_sub > 3:
                load_swiglu(1)
            if n_sub > 4:
                ssm_loads(sp, load_slot)
            if n_sub > 5:
                load_swiglu(2)
            if n_sub > 6:
                for j in range(4):
                    for q, c0 in enumerate((256 * j, D + 256 * j)):
                        load_slot(SLOT["cv"] + 2 * j + q, [(0, t["cv_w_pw1_2"][0][:, c0:c0 + 256])])
                for m in range(4):
                    load_slot(SLOT["pw2"] + m, [(0, t["cv_w_pw2_2"][0][:, 256 * m:256 * m + 256])])
            if n_sub > 7:
                load_swiglu(3)
            sp.wait_ge(out_copied, DC)
            for i in range(NT):
                sp.dma_start(out[0, P * i:P * i + P, :], y_out[:, i, :]).then_inc(out_dma, 16)
            sp.wait_ge(out_dma, 16 * NT)

        tok_slots = {1, 10, 11, SLOT["odd"] + 2, SLOT["ssm"]} | set(range(SLOT["ssm"] + 13, SLOT["ssm"] + 21))
        parts_of = {0: 4, 1: 2, SLOT["odd"]: 4, SLOT["odd"] + 1: 4}
        widths = {1: 72, SLOT["ssm"]: MH}
        loads_upto = {}
        count = [0, 0]
        for n in range(SLOT["end"]):
            loads_upto[n] = count[n % 2]
            count[n % 2] += parts_of.get(n, 1)

        def scan_pool(pool):
            by_head = lambda ap: ap.rearrange("p (h e) -> p h e", e=HD)
            bc = lambda ap: ap.unsqueeze(2).to_broadcast([P, MH, HD])
            pool.wait_ge(conv_copied, 20)
            pool.wait_ge(decay_ready, 1)
            pool.wait_ge(dt_step, 3)
            pool.wait_ge(w_used, 2 * SLOT["ssm_out"])
            for i in range(NT):
                def place_decays(q):
                    Q = 8 * i + q
                    if Q >= 2:
                        pool.wait_ge(seg_summed, Q - 1)
                    pool.tensor_tensor(root[q % 2][:].rearrange("p (j l) -> p j l", l=P),
                                       after[:].unsqueeze(1).to_broadcast([P, 4, P]),
                                       log_decay[:, i, 4 * q:4 * q + 4].unsqueeze(2).to_broadcast([P, 4, P]), ALU.mult
                                       ).then_inc(seg_in, 1)

                if i >= 1:
                    pool.wait_ge(yd_summed, 8 * i)
                    pool.wait_ge(st_summed, 4 * i)
                    pool.wait_ge(ys_ready, 4 * i)
                place_decays(0)
                place_decays(1)
                pool.tensor_tensor(by_head(xdt[:]), by_head(xs_tok[:, i, :]), bc(dt_tok[:, i, :]), ALU.mult
                                   ).then_inc(x_weighted, 1)
                place_decays(2)
                place_decays(3)
                pool.wait_ge(x_weighted, 2 * i + 1)
                if i < NT - 1:
                    pool.tensor_tensor(by_head(xdec[:]), by_head(xdt[:]), bc(decay[:, 1, i, :]), ALU.mult).then_inc(x_weighted, 1)
                place_decays(4)
                if i >= 1:
                    pool.wait_ge(ys_turned, 4 * i)
                pool.tensor_tensor(by_head(y_ssm[:]), by_head(xs_tok[:, i, :]), bc(dskip_row[:]), ALU.mult
                                   ).then_inc(skip_done, 1)
                for q in range(5, 8):
                    place_decays(q)
                for k in range(4):
                    pool.wait_ge(ys_rounded, 4 * i + k + 1)
                    pool.tensor_tensor(g_lo[:, i, S * k:S * k + S], root[k % 2][:], g_hi[:, i, S * k:S * k + S].bitcast(F32),
                                       ALU.subtract).then_inc(ys_ready, 1)

        @block.gpsimd
        def _(pool):
            step = [0]

            def then(ins):
                step[0] += 1
                ins.then_inc(consts, 1)
                pool.wait_ge(consts, step[0])

            then(pool.memset(ident[:], 0.0))
            then(pool.affine_select(out=ident[:], in_=ident[:], compare_op=ALU.not_equal, fill=1.0, base=0,
                                    pattern=[[-1, P]], channel_multiplier=1))
            then(pool.memset(ones[:], 1.0))
            then(pool.memset(head_ones[:], 0.0))
            then(pool.memset(head_ones[0:HD, 0:HD], 1.0))
            then(pool.memset(head_ones[HD:P, HD:P], 1.0))
            then(pool.memset(upto[:], 1.0))
            then(pool.memset(after[:], 1.0))
            then(pool.iota(dist[:], pattern=[[-1, S]], base=S - P, channel_multiplier=1, allow_small_or_imprecise_dtypes=True))
            then(pool.iota(dist_win[:], pattern=[[-1, 2 * P]], base=P, channel_multiplier=1, allow_small_or_imprecise_dtypes=True))
            then(pool.affine_select(out=upto[:], in_=upto[:], compare_op=ALU.is_ge, fill=0.0, base=0,
                                    pattern=[[1, P]], channel_multiplier=-1))
            then(pool.affine_select(out=after[:], in_=after[:], compare_op=ALU.is_gt, fill=0.0, base=0,
                                    pattern=[[-1, P]], channel_multiplier=1))
            then(pool.affine_select(out=dist[:], in_=dist[:], compare_op=ALU.is_ge, fill=BIG, base=S - P,
                                    pattern=[[-1, S]], channel_multiplier=1))
            then(pool.affine_select(out=dist_win[:], in_=dist_win[:], compare_op=ALU.is_ge, fill=BIG, base=P,
                                    pattern=[[-1, 2 * P]], channel_multiplier=1))
            then(pool.affine_select(out=dist_win[:], in_=dist_win[:], compare_op=ALU.is_gt, fill=BIG, base=0,
                                    pattern=[[1, 2 * P]], channel_multiplier=-1))
            assert step[0] == N_CONSTS, step[0]

            def low_part(n, parity, nk, width):
                for m in range(2):
                    half = slice(width // 2 * m, width // 2 * m + width // 2)
                    pool.wait_ge(w_rounded, n * 2 + (m + 1))
                    pool.tensor_tensor(w_lo[parity][:, 0:nk, half], w_raw[parity][:, 0:nk, half],
                                       w_hi[parity][:, 0:nk, half].bitcast(F32), ALU.subtract).then_inc(w_split, 1)

            def tap_diagonals(c):
                for j in range(PE_TAPS // 4):
                    if c >= 1:
                        pool.wait_ge(pe_taps_done, c)
                    at = ROWS["dw_w"] + DC * 4 * j + c
                    w = cols[:, at:at + 3 * DC + 1:DC]
                    pool.tensor_tensor(root[j][:].rearrange("p (k q) -> p k q", q=P), ident[:].unsqueeze(1).to_broadcast([P, 4, P]),
                                       w.unsqueeze(2).to_broadcast([P, 4, P]), ALU.mult).then_inc(diag_ready, 1)

            def weigh_ada(g):
                w, j = ada_wide(g)
                at = 3 * (g - ADA_PROJ)
                pool.wait_ge(ada_wide_in[j], 16 * ((g - ADA_PROJ) // 3 + 1))
                pool.tensor_tensor(w[:], w[:], cond[:].unsqueeze(2).to_broadcast([P, 8, SLOT_W]), ALU.mult).then_inc(ada_pool, 1)
                pool.wait_ge(ada_pool, at + 1)
                pool.tensor_tensor(w[:, 0:4, :], w[:, 0:4, :], w[:, 4:8, :], ALU.add).then_inc(ada_pool, 1)
                pool.wait_ge(ada_pool, at + 2)
                pool.tensor_tensor(w[:, 0:2, :], w[:, 0:2, :], w[:, 2:4, :], ALU.add).then_inc(ada_pool, 1)

            n = 0
            while n < end_slot:
                if n == SLOT["out0"] + 2:
                    for g in range(ADA_PROJ, ADA_ALL):
                        weigh_ada(g)
                if n == SLOT["ssm_out"] + 2:
                    scan_pool(pool)
                if n not in [SLOT[f"gu{f}"] for f in range(4)]:
                    low_part(n, n % 2, SLOT_K, widths.get(n, SLOT_W))
                    m = n - SLOT["cv"]
                    if 3 <= m <= 9:
                        tap_diagonals(m - 3)
                    if m == 9:
                        tap_diagonals(DC - 1)
                    n += 1
                    continue
                with pool.Fori(0, FC // 2) as i:
                    for j in range(2):
                        low_part(i * 2 + (n + j), (n + j) % 2, SLOT_K, SLOT_W)
                n += N_GU
                with pool.Fori(0, 2) as i:
                    for j in range(6):
                        low_part(i * 6 + (n + j), (n + j) % 2, 8 if j % 3 < 2 else FC - 16, SLOT_W)
                n += N_DOWN

        def ssm_pe(pe, take, freed, slot_tok, slot_cm, h_chunk, out_project, follows):
            n0 = SLOT["ssm"]
            for m in range(2):
                take(m, dt_step, 1)
            dst = [bank[i // 2][:, SLOT_W * (i % 2):SLOT_W * (i % 2) + MH] for i in range(NT)]
            slot_tok(n0, dst, MH, h_chunk(4))

            def turn(c):
                if c >= 20:
                    return
                pe.wait_ge(conv_silu, c + 1)
                take(6 + c % 2, conv_copied, c + 1)
                src = tmp[c % 2][:] if c < 16 else b_cm[:, c - 16, :]
                for i in range(NT):
                    ins = pe.transpose(bank[6 + c % 2][:, P * i:P * i + P], src[:, P * i:P * i + P], ident[:])
                ins.then_inc(conv_turned, 1)

            for s in range(12):
                dst = []
                for q in range(2):
                    c = 2 * s + q
                    dst.append(take((c + 2) % 4, conv_done, c + 1))
                slot_cm(n0 + 1 + s, (n0 + 1 + s) % 2, lambda k: h_hi[:, k, :], lambda k: h_lo[:, k, :], dst)
                if s == 0:
                    pe.wait_ge(dt_step, 3)
                    take(5, decay_ready, 1)
                    for j, tri in enumerate((upto, after, ones)):
                        ins = pe.matmul(bank[5][:, P * j:P * j + P], tri[:], log_decay[:].rearrange("p i h -> p (i h)"),
                                        start=True, stop=True)
                    ins.then_inc(decay_sums, 1)
                if s >= 1:
                    turn(2 * s - 2)
                    turn(2 * s - 1)
            for s in range(8):
                n = n0 + 13 + s
                banks = ((2 * s + 2) % 4, (2 * s + 3) % 4)
                for m in range(2):
                    take(banks[m], z_ready, 2 * s + m + 1)
                slot_tok(n, [bank[banks[i // 2]][:, SLOT_W * (i % 2):SLOT_W * (i % 2) + SLOT_W] for i in range(NT)], SLOT_W)

            for i in range(NT):
                tok = slice(P * i, P * i + P)
                take(0, cb_masked, i + 1)
                pe.wait_ge(conv_silu, NCONV)
                for g in range(MG):
                    ins = pe.matmul(bank[0][:, P * g:P * g + P], b_cm[:, g, tok], c_cm[:, g, tok], start=True, stop=True)
                ins.then_inc(cb_summed, 1)

                def segments(q):
                    Q = 8 * i + q
                    pe.wait_ge(seg_in, Q + 1)
                    take(1 + q % 2, seg_exp, Q + 1)
                    for j in range(4):
                        ins = pe.matmul(bank[1 + q % 2][:, P * j:P * j + P], root[q % 2][:, P * j:P * j + P], upto[:],
                                        start=True, stop=True)
                    ins.then_inc(seg_summed, 1)

                def within(q):
                    Q, g = 8 * i + q, q // 2
                    pe.wait_ge(mix_ready, Q + 1)
                    pe.wait_ge(x_weighted, 2 * i + 2 if i < NT - 1 else 2 * i + 1)
                    if q % 2 == 0:
                        take(3 + g % 2, yg_done, 4 * i + g + 1)
                    for j in range(4):
                        at = 256 * (q % 2) + HD * j
                        ins = pe.matmul(bank[3 + g % 2][:, at:at + HD], sq[q % 2][:, P * j:P * j + P],
                                        xdt[:, HD * (4 * q + j):HD * (4 * q + j) + HD], start=True, stop=True)
                    ins.then_inc(yd_summed, 1)

                def carried(g):
                    if i > 0:
                        pe.wait_ge(st_done, 4 * (i - 1) + g + 1)
                        take(5 + g % 2, yg_done, 4 * i + g + 1)
                        pe.matmul(bank[5 + g % 2][:], c_cm[:, g, tok], state[:, S * g:S * g + S], start=True, stop=True
                                  ).then_inc(yo_summed, 1)

                def own_state(g):
                    if i < NT - 1:
                        take(7, st_done, 4 * i + g + 1)
                        pe.matmul(bank[7][:], b_tok[:, i, P * g:P * g + P], xdec[:, S * g:S * g + S], start=True, stop=True
                                  ).then_inc(st_summed, 1)

                for q in range(8 + 2):
                    if q < 8:
                        segments(q)
                        if q % 2 == 0:
                            carried(q // 2)
                    if q >= 2:
                        within(q - 2)
                        if q % 2 == 1:
                            own_state((q - 2) // 2)
                for k in range(4):
                    K = 4 * i + k
                    pe.wait_ge(ys_scaled, i + 1)
                    take(5 + k % 2, ys_wide, K + 1)
                    for c in range(4):
                        at = P * (4 * k + c)
                        ins = pe.transpose(bank[5 + k % 2][:, P * c:P * c + P], y_ssm[:, at:at + P], ident[:])
                    ins.then_inc(ys_turned, 1)
            gh = g_hi[:].rearrange("p i (c q) -> p c i q", q=P)
            gl = g_lo[:].rearrange("p i (c q) -> p c i q", q=P)
            pe.wait_ge(ys_ready, 16)
            out_project(SLOT["ssm_out"], 40, lambda k: gh[:, k, :, :], lambda k: gl[:, k, :, :], kslots=2,
                        then_norm=follows(5))

        def cv_pe(pe, take, freed, slot_cm, h_chunk, out_project, follows):
            n0 = SLOT["cv"]

            def conv_taps(c):
                pe.wait_ge(glu_done, c + 1)
                pe.wait_ge(diag_ready, 2 * c + 2)
                take(6 + c % 2, taps_done, c + 1)
                for k in range(PE_TAPS):
                    ins = pe.matmul(bank[6 + c % 2][:], root[k // 4][:, P * (k % 4):P * (k % 4) + P], u_pad[:, c, k:k + S],
                                    start=k == 0, stop=k == PE_TAPS - 1)
                ins.then_inc(pe_taps_done, 1)

            for j in range(4):
                for q, by in enumerate((glu_done, sig_done)):
                    dst = [take(2 * q + m, by, 2 * j + m + 1) for m in range(2)]
                    slot_cm(n0 + 2 * j + q, (n0 + 2 * j + q) % 2, lambda k: h_hi[:, k, :], lambda k: h_lo[:, k, :], dst,
                            before=h_chunk(6) if j == 0 and q == 0 else None)
                    if 2 * j + q >= 2:
                        conv_taps(2 * j + q - 2)
            conv_taps(6)
            conv_taps(7)
            take(4, centred, DC)
            for c in range(DC):
                pe.wait_ge(taps_done, c + 1)
                ins = pe.matmul(bank[4][:], ones[:], v_cm[:, c, :], start=c == 0, stop=c == DC - 1)
            ins.then_inc(mean_summed, 1)
            z0, r = SQ_BASE["ln"], ROOT_BASE["ln"]
            take(4, root_done, r + 1)
            for c in range(DC):
                pe.wait_ge(sq_ready, z0 + c + 1)
                pe.matmul(bank[4][:], ones[:], sq[(z0 + c) % 2][:], start=c == 0, stop=c == DC - 1).then_inc(sq_summed, 1)
            out_project(SLOT["pw2"], 56, lambda k: h_hi[:, k, :], lambda k: h_lo[:, k, :],
                        before=lambda k: pe.wait_ge(h_ready, H_BASE["ln"] + k + 1), then_norm=follows(7))

        @block.tensor
        def _(pe):
            freed = [None] * 8

            def take(b, by, count):
                if freed[b] is not None:
                    pe.wait_ge(*freed[b])
                freed[b] = (by, count)
                return bank[b]

            def slot_cm(n, parity, src_hi, src_lo, dst, nk=SLOT_K, k0=0, first=True, last=True, before=None, widths=(P, P)):
                def three(m, k):
                    hi, lo = w_hi[parity][:, k, P * m:P * m + P], w_lo[parity][:, k, P * m:P * m + P]
                    pe.matmul(dst[m][:], hi, src_hi(k0 + k), start=first and k == 0, stop=False)
                    pe.matmul(dst[m][:], hi, src_lo(k0 + k), start=False, stop=False)
                    ins = pe.matmul(dst[m][:], lo, src_hi(k0 + k), start=False, stop=last and k == nk - 1)
                    if k == nk - 1:
                        ins.then_inc(w_used, 1)

                if before is not None:
                    pe.wait_ge(w_split, n * 2 + 2)
                    for k in range(nk):
                        before(k)
                        for m in range(2):
                            three(m, k)
                    return
                for m in range(2):
                    pe.wait_ge(w_split, n * 2 + (m + 1))
                    for k in range(nk):
                        three(m, k)

            def half_cm(n, m, dst):
                pe.wait_ge(w_split, 2 * n + m + 1)
                for k in range(SLOT_K):
                    hi, lo = w_hi[n % 2][:, k, P * m:P * m + P], w_lo[n % 2][:, k, P * m:P * m + P]
                    pe.matmul(dst[:], hi, h_hi[:, k, :], start=k == 0, stop=False)
                    pe.matmul(dst[:], hi, h_lo[:, k, :], start=False, stop=False)
                    ins = pe.matmul(dst[:], lo, h_hi[:, k, :], start=False, stop=k == SLOT_K - 1)
                ins.then_inc(w_used, 1)

            def slot_tok(n, dst, width, before=None):
                parity = n % 2
                pe.wait_ge(w_split, 2 * n + 2)
                for i in range(NT):
                    for k in range(SLOT_K):
                        if before is not None and i == 0:
                            before(k)
                        a_hi_, a_lo_ = h_hi[:, k, P * i:P * i + P], h_lo[:, k, P * i:P * i + P]
                        b_hi_, b_lo_ = w_hi[parity][:, k, 0:width], w_lo[parity][:, k, 0:width]
                        pe.matmul(dst[i], a_hi_, b_hi_, start=k == 0, stop=False)
                        pe.matmul(dst[i], a_lo_, b_hi_, start=False, stop=False)
                        ins = pe.matmul(dst[i], a_hi_, b_lo_, start=False, stop=k == SLOT_K - 1)
                    if i % 2 == 1:
                        ins.then_inc(w_used, 1)

            def norm_sums(nn, c0=0, c1=DC):
                z0, r = SQ_BASE[f"n{nn}"], ROOT_BASE[f"n{nn}"]
                if c0 == 0:
                    take(4, root_done, r + 1)
                for c in range(c0, c1):
                    pe.wait_ge(sq_ready, z0 + c + 1)
                    pe.matmul(bank[4][:], ones[:], sq[(z0 + c) % 2][:], start=c == 0, stop=c == DC - 1).then_inc(sq_summed, 1)

            def h_chunk(nh):
                def wait(k):
                    pe.wait_ge(h_ready, H_BASE[nh] + k + 1)
                return wait

            ada_at = [0]

            def ada_sums(upto_group):
                for g in range(ada_at[0], upto_group):
                    if g == 8:
                        pe.wait_ge(gains_ready, 1)
                    if g >= ADA_PROJ:
                        w, _ = ada_wide(g)
                        pe.wait_ge(ada_pool, 3 * (g - ADA_PROJ) + 3)
                        chunks = [w[:, k, :] for k in range(2)]
                    else:
                        pe.wait_ge(ada_dve, 8 * g + 8)
                        chunks = [ada_acc[g % 2][:]]
                    for j in range(2):
                        for k, w in enumerate(chunks):
                            ins = pe.matmul(bank[7][:, 2 * g + j:2 * g + j + 1], w[:, P * j:P * j + P], ones[:, 0:1],
                                            start=k == 0, stop=k == len(chunks) - 1)
                    ins.then_inc(ada_col, 1)
                ada_at[0] = max(ada_at[0], upto_group)

            pe.wait_ge(consts, 2)
            pe.wait_ge(params_in, 16 * N_FIRST_LOADS)
            n = STACK_ROWS[0]
            pe.transpose(bank[5][:, 0:n], rows[0:n, 0, :], ident[0:n, 0:n]).then_inc(rows_t, 1)
            freed[5] = (cols_ready, 1)
            for c in range(DC):
                take(c % 4, x_ready, c + 1)
                for i in range(NT):
                    ins = pe.transpose(bank[c % 4][:, P * i:P * i + P], x_tok[:, i, P * c:P * c + P], ident[:])
                ins.then_inc(x_t, 1)
            pe.wait_ge(consts, N_CONSTS)
            norm_sums(0)
            ada_sums(ADA_FIRST)

            def later_rows():
                pe.wait_ge(params_later, 16 * N_LATER_LOADS)
                take(5, cols_ready, NSTACK)
                for s in range(1, NSTACK):
                    n = STACK_ROWS[s]
                    ins = pe.transpose(bank[5][:, P * (s - 1):P * (s - 1) + n], rows[0:n, s, :], ident[0:n, 0:n])
                ins.then_inc(rows_t, 1)
                pe.wait_ge(lam_s, 4)
                take(6, lam_s, 6)
                pe.matmul(bank[6][:, 0:1], ones[0:1, :], lam_val[:], start=True, stop=True).then_inc(lam_s, 1)

            def project(parts, nh, base_slot, qk_sq0, qk_root0, qk0, plain0, after_slot=None):
                chunk = 0
                qk = plain = 0
                pending = []

                def head_sums():
                    z, r = pending.pop(0)
                    take(4, root_done, r + 1)
                    pe.wait_ge(sq_ready, z + 1)
                    pe.matmul(bank[4][:], head_ones[:], sq[z % 2][:], start=True, stop=True).then_inc(sq_summed, 1)

                for s, part in enumerate(parts):
                    n = base_slot + s
                    banks = (chunk % 4, (chunk + 1) % 4)
                    before = h_chunk(nh) if s == 0 else None
                    if part[0] == "tok":
                        width = part[1]
                        per = 1 if width > P else 0
                        for m in range(2):
                            take(banks[m], plain_copied, plain0 + plain + 1 + m)
                        dst = [bank[banks[i // 2]][:, SLOT_W * (i % 2):SLOT_W * (i % 2) + width] for i in range(NT)]
                        slot_tok(n, dst, width, before)
                        plain += 2
                        while pending:
                            head_sums()
                    else:
                        dst = []
                        for m in range(2):
                            if part[m] == "qk":
                                dst.append(take(banks[m], qk_normed, qk0 + qk + 1 + (m if part[0] == "qk" else 0)))
                            else:
                                plain += 1
                                dst.append(take(banks[m], plain_copied, plain0 + plain))
                        if before is not None:
                            slot_cm(n, n % 2, lambda k: h_hi[:, k, :], lambda k: h_lo[:, k, :], dst, before=before)
                        for m in range(2):
                            if before is None:
                                half_cm(n, m, dst[m])
                            while pending:
                                head_sums()
                            if part[m] == "qk":
                                pending.append((qk_sq0 + qk, qk_root0 + qk))
                                qk += 1
                    chunk += 2
                    if after_slot is not None:
                        after_slot(s)
                while pending:
                    head_sums()

            def out_project(base_slot, x_base, src_hi, src_lo, kslots=1, before=None, then_norm=None):
                for m in range(4):
                    dst = []
                    for q in range(2):
                        b = (2 * m + q) % 4
                        dst.append(take(b, x_ready, x_base + 2 * m + q + 1))
                    for k in range(kslots):
                        n = base_slot + kslots * m + k
                        slot_cm(n, n % 2, src_hi, src_lo, dst, k0=SLOT_K * k, first=k == 0, last=k == kslots - 1,
                                before=before if m == 0 else None)
                    if m >= 1:
                        norm_sums(then_norm, 2 * m - 2, 2 * m)
                norm_sums(then_norm, 6, 8)

            def swiglu(f, nh, then_norm):
                n0 = SLOT[f"gu{f}"]
                for b in range(4):
                    take(b, None, None)
                m0 = FC * f
                for j in range(2):
                    slot_cm(n0 + j, (n0 + j) % 2, lambda k: h_hi[:, k, :], lambda k: h_lo[:, k, :],
                            [bank[2 * j], bank[2 * j + 1]], before=h_chunk(nh) if j == 0 else None)
                with pe.Fori(1, FC // 2) as i:
                    for j, (by, c0) in enumerate(((silu_done, m0), (gated, m0 + AHEAD))):
                        pe.wait_ge(by, i * 2 + c0)
                        slot_cm(i * 2 + (n0 + j), (n0 + j) % 2, lambda k: h_hi[:, k, :], lambda k: h_lo[:, k, :],
                                [bank[2 * j], bank[2 * j + 1]])
                pe.wait_ge(gated, m0 + FC + AHEAD)
                n0 = SLOT[f"down{f}"]
                x0 = DC * (2 * f + 2)
                for k in range(FC):
                    pe.wait_ge(a_ready, m0 + k + 1 + AHEAD)

                def down_step(i, waits):
                    for g in range(2):
                        m = 2 * i + g
                        if waits:
                            pe.wait_ge(x_ready, i * 4 + (x0 - 4 + 2 * g + 2))
                        for k0 in range(3):
                            j = 3 * g + k0
                            slot_cm(i * 6 + (n0 + j), (n0 + j) % 2, lambda k: a_hi[:, k, :], lambda k: a_lo[:, k, :],
                                    [bank[2 * g], bank[2 * g + 1]], nk=8 if k0 < 2 else FC - 16, k0=8 * k0,
                                    first=k0 == 0, last=k0 == 2)
                            if k0 == 0 and m >= 1:
                                norm_sums(then_norm, 2 * m - 2, 2 * m)
                down_step(0, False)
                down_step(1, True)
                norm_sums(then_norm, 6, 8)
                for b in range(4):
                    freed[b] = (x_ready, x0 + 5 + b)

            def attention(name, scores, blocks, values, npair, nyb, u0, heads, waits=(), ring=3, back=7, ada=None):
                for w in waits:
                    pe.wait_ge(*w)
                units = [(i, h) for i in range(NT) for h in range(heads)]
                U = len(units)
                hw = S * nyb // heads

                def do_scores(u):
                    i, h = units[u]
                    for m in range(npair):
                        v = npair * u + m
                        b = (u0["s"] + v) % ring
                        take(b, s_biased, u0["s"] + v + 1)
                        scores(i, h, m, bank[b])

                def do_turn(u):
                    i, h = units[u]
                    b = 3 + (u0["t"] + u) % 2
                    if npair == 2:
                        pe.wait_ge(mixed, u0["mix"] + 2 * (u + 1))
                    else:
                        pe.wait_ge(exp_done, u0["e"] + u + 1)
                    take(b, pt_copied, u0["t"] + u + 1)
                    src = prob[(2 * u) % 4] if npair == 2 else prob[u % 4]
                    for q in range(len(blocks(i))):
                        ins = pe.transpose(bank[b][:, P * q:P * q + P], src[:, P * q:P * q + P], ident[:])
                    ins.then_inc(p_turned, 1)

                def do_values(u):
                    i, h = units[u]
                    pe.wait_ge(pt_copied, u0["t"] + u + 1)
                    yb, at = divmod(h * hw, S)
                    b = 5 + (i * nyb + yb) % 2
                    if at == 0:
                        take(b, y_scaled, u0["y"] + nyb * i + yb + 1)
                    js = blocks(i)
                    for q, j in enumerate(js):
                        ins = pe.matmul(bank[b][:, at:at + hw], prob_t[(u0["t"] + u) % 2][:, P * q:P * q + P], values(j, h),
                                        start=q == 0, stop=q == len(js) - 1)
                    ins.then_inc(pv_done, 1)

                def tile_back(k):
                    pe.wait_ge(y_scaled, u0["y"] + k + 1)
                    take(back, y_wide, u0["y"] + k + 1)
                    for c in range(4):
                        ins = pe.transpose(bank[back][:, P * c:P * c + P], y_tok[k % 2][:, P * c:P * c + P], ident[:])
                    ins.then_inc(y_turned, 1)

                done_rows = 0
                for step in range(U + 3):
                    if step < U:
                        do_scores(step)
                    if ada is not None and step % 2 == 1:
                        ada_sums(ada + step // 2)
                    if 2 <= step < U + 2:
                        do_turn(step - 2)
                    if step >= 3:
                        do_values(step - 3)
                        while done_rows < NT * nyb and (done_rows + 1) * (heads // nyb) <= step - 3 - 1:
                            tile_back(done_rows)
                            done_rows += 1
                while done_rows < NT * nyb:
                    tile_back(done_rows)
                    done_rows += 1

            idx_units = [(i, h) for i in range(1, NT) for h in range(I_HEADS)]

            def index_scores(v):
                i, h = idx_units[v]
                b = 5 + v % 2
                w = P * (i + 1)
                take(b, idx_relu, v + 1)
                lo = HD * (h % 2)
                pe.matmul(bank[b][:, 0:w], iq[lo:lo + HD, h // 2, P * i:P * i + P], ik[lo:lo + HD, 0:w],
                          start=True, stop=True).then_inc(idx_summed, 1)

            def after_even(s):
                ada_sums(min(ADA_FIRST + 2 * (s + 1), ADA_PROJ))
                if s == 2:
                    later_rows()
                if 4 <= s < 10:
                    pe.wait_ge(plain_copied, 7)
                    for v in range(4 * (s - 4), 4 * (s - 4) + 4):
                        index_scores(v)

            EVEN_PARTS = [("qk", "plain"), ("tok", 72), ("plain", "plain"), ("plain", "plain"), ("qk", "qk"), ("qk", "qk"),
                          ("qk", "qk"), ("qk", "qk"), ("qk", "qk"), ("qk", "qk"), ("tok", 256), ("tok", 256)]
            project(EVEN_PARTS, 0, 0, SQ_BASE["even"], ROOT_BASE["even"], 0, 0, after_even)

            def diff_scores(i, h, m, d):
                lo = HD * m
                pe.matmul(d[:, 0:P * (i + 1)], aq[lo:lo + HD, h, P * i:P * i + P], ak[lo:lo + HD, h, 0:P * (i + 1)],
                          start=True, stop=True).then_inc(s_summed, 1)

            attention("diff", diff_scores, lambda i: list(range(i + 1)), lambda j, h: av[:, j, P * h:P * h + P], 2, 1,
                      dict(s=0, mix=0, e=0, t=0, y=0), A_HEADS, [(qk_normed, 13), (plain_copied, 11)],
                      ring=2, back=2, ada=ADA_PROJ)

            def dsa_scores(i, h, m, d):
                lo = HD * (h % 2)
                pe.matmul(d[:, 0:P * (i + 1)], bq[lo:lo + HD, h // 2, P * i:P * i + P], bk[lo:lo + HD, 0:P * (i + 1)],
                          start=True, stop=True).then_inc(s_summed, 1)

            attention("dsa", dsa_scores, lambda i: list(range(i + 1)), lambda j, h: bv[:, j, :], 1, 1,
                      dict(s=32, mix=32, e=32, t=16, y=4), B_HEADS, ring=2, back=2, ada=ADA_PROJ + 8)
            ada_sums(ADA_ALL)
            freed[7] = (gains_ready, 2)

            follows = lambda k: k if n_sub > k else 8
            out_project(SLOT["out0"], 8, lambda k: h_hi[:, k, :], lambda k: h_lo[:, k, :],
                        before=lambda k: pe.wait_ge(y_ready, 8), then_norm=follows(1))
            if n_sub > 1:
                swiglu(0, 1, follows(2))
            if n_sub > 2:
                ODD_PARTS = [("qk", "qk"), ("qk", "qk"), ("tok", 256)] + [("qk", "qk")] * 4
                project(ODD_PARTS, 2, SLOT["odd"], SQ_BASE["odd"], ROOT_BASE["odd"], 13, 11)

                def win_scores(i, h, m, d):
                    lo = HD * (h % 2)
                    k0 = P * max(i - 1, 0)
                    k1 = P * (i + 1)
                    pe.matmul(d[:, 0:k1 - k0], cq[lo:lo + HD, h // 2, P * i:P * i + P], ck[lo:lo + HD, h // 4, k0:k1],
                              start=True, stop=True).then_inc(s_summed, 1)

                attention("win", win_scores, lambda i: list(range(max(i - 1, 0), i + 1)),
                          lambda j, h: cv[:, j, HD * (h // 4):HD * (h // 4) + HD], 1, 2,
                          dict(s=64, mix=32, e=64, t=48, y=8), C_HEADS, [(qk_normed, 25), (plain_copied, 13)])
                out_project(SLOT["out1"], 24, lambda k: h_hi[:, k, :], lambda k: h_lo[:, k, :],
                            before=lambda k: pe.wait_ge(y_ready, 16), then_norm=follows(3))
            if n_sub > 3:
                swiglu(1, 3, follows(4))
            if n_sub > 4:
                ssm_pe(pe, take, freed, slot_tok, slot_cm, h_chunk, out_project, follows)
            if n_sub > 5:
                swiglu(2, 5, follows(6))
            if n_sub > 6:
                cv_pe(pe, take, freed, slot_cm, h_chunk, out_project, follows)
            if n_sub > 7:
                swiglu(3, 7, 8)
            for c in range(DC):
                pe.wait_ge(h_scaled, h_made() + c + 1)
                take(c % 4, out_copied, c + 1)
                for i in range(NT):
                    ins = pe.transpose(bank[c % 4][:, P * i:P * i + P], stage[c % 4][:, P * i:P * i + P], ident[:])
                ins.then_inc(out_t, 1)

        def ssm_act(act, round_half):
            n0 = SLOT["ssm"]
            act.wait_ge(bcast_in, 16 * 8)
            act.activation(alog_row[:], alog_row[:], ACT.Exp).then_inc(dt_act, 1)
            for m in range(2):
                round_half(n0 + 2, m)
            act.wait_ge(dt_step, 2)
            act.activation(dt_abs[:], dt_abs[:], ACT.Exp, scale=-1.0).then_inc(dt_act, 1)
            act.wait_ge(dt_act, 2)
            act.activation(dt_abs[:], dt_abs[:], ACT.Ln, bias=1.0).then_inc(dt_act, 1)

            def conv_act(c):
                act.wait_ge(conv_done, c + 1)
                dst = tmp[c % 2][:] if c < 16 else b_cm[:, c - 16, :] if c < 20 else c_cm[:, c - 20, :]
                act.activation(dst, tmp[c % 2][:], ACT.Silu).then_inc(conv_silu, 1)

            def copy_out(c):
                if c < 20:
                    act.wait_ge(conv_turned, c + 1)
                    src = bank[6 + c % 2][:].rearrange("p (i q) -> p i q", q=P)
                    dst = xs_tok[:, :, P * c:P * c + P] if c < 16 else b_tok[:, :, P * (c - 16):P * (c - 16) + P]
                    act.activation(dst, src, ACT.Copy).then_inc(conv_copied, 1)

            for s in range(12):
                for q in range(2):
                    round_half(n0 + 1 + s + 2, q)
                    conv_act(2 * s + q)
                    if s == 1 and q == 1:
                        act.wait_ge(decay_sums, 1)
                        act.activation(decay[:], bank[5][:, 0:3 * P].rearrange("p (j i h) -> p j i h", j=3, i=NT), ACT.Exp
                                       ).then_inc(decay_ready, 1)
                    if s >= 1:
                        copy_out(2 * s - 2 + q)
            for s in range(8):
                for m in range(2):
                    act.wait_ge(w_used, 2 * (n0 + 13 + s) + m + 1)
                    v = bank[(2 * s + m + 2) % 4][:].rearrange("p (i w) -> p i w", i=2)
                    act.activation(z_tok[:, 2 * m:2 * m + 2, SLOT_W * s:SLOT_W * s + SLOT_W], v, ACT.Silu).then_inc(z_ready, 1)
                for m in range(2):
                    round_half(n0 + 13 + s + 2, m)
            for i in range(NT):
                for q in range(8):
                    Q = 8 * i + q
                    act.wait_ge(seg_summed, Q + 1)
                    if Q >= 2:
                        act.wait_ge(mix_ready, Q - 1)
                    act.activation(tmp[q % 2][:], bank[1 + q % 2][:], ACT.Exp).then_inc(seg_exp, 1)
                act.wait_ge(mix_ready, 8 * i + 8)
                for g in range(MG):
                    act.wait_ge(yg_done, 4 * i + g + 1)
                    if g >= 2:
                        act.wait_ge(yg_squares, 4 * i + g - 1)
                    act.activation(tmp[g % 2][:], y_ssm[:, S * g:S * g + S], ACT.Square,
                                   accum_out=stat[:, g:g + 1]).then_inc(yg_squares, 1)
                act.wait_ge(yg_squares, 4 * (i + 1))
                act.activation(stat[:], stat[:], ACT.Sqrt, bias=eps_col[1e-5][:], scale=1.0 / S).then_inc(yg_root, 1)
                for k in range(4):
                    K = 4 * i + k
                    act.wait_ge(ys_wide, K + 1)
                    act.activation(g_hi[:, i, S * k:S * k + S], root[k % 2][:], ACT.Copy).then_inc(ys_rounded, 1)

        @block.scalar
        def _(act):
            chain = [0]

            def link(ins):
                chain[0] += 1
                ins.then_inc(act_chain, 1)
                act.wait_ge(act_chain, chain[0])

            def slot_rows(n):
                for f in range(4):
                    if 0 <= n - SLOT[f"down{f}"] < N_DOWN and (n - SLOT[f"down{f}"]) % 3 == 2:
                        return FC - 16
                return SLOT_K

            def round_half(n, m):
                if n >= end_slot:
                    return
                half_w = widths.get(n, SLOT_W) // 2
                half = slice(half_w * m, half_w * m + half_w)
                nk = slot_rows(n)
                if m == 0:
                    act.wait_ge(w_full[n % 2], 16 * (loads_upto[n] + parts_of.get(n, 1)))
                if n >= 2:
                    whole = n - 2 in tok_slots or n in widths
                    act.wait_ge(w_used, 2 * (n - 2) + (2 if whole else m + 1))
                act.activation(w_hi[n % 2][:, 0:nk, half], w_raw[n % 2][:, 0:nk, half], ACT.Copy).then_inc(w_rounded, 1)

            def norm_squares(nn, c0=0, c1=DC):
                z0 = SQ_BASE[f"n{nn}"]
                for c in range(c0, c1):
                    act.wait_ge(x_ready, XR[nn] + c + 1)
                    if z0 + c >= 2:
                        act.wait_ge(sq_summed, z0 + c - 1)
                    act.activation(sq[(z0 + c) % 2][:], x_cm[:, c, :], ACT.Square).then_inc(sq_ready, 1)

            def round_and_square(base, per_group, nn):
                for m in range(4):
                    for j in range(per_group * m, per_group * m + per_group):
                        if m >= 1 and j == per_group * m:
                            norm_squares(nn, 2 * m - 2, 2 * m)
                        if j == 4 * per_group - 1:
                            act.activation(spare[:], eps_col[1e-6][:], ACT.Sqrt)
                            norm_squares(nn, 6, 8)
                        for q in range(2):
                            round_half(base + j + 2, q)

            def rms(name, z_last, width, eps):
                act.wait_ge(sq_summed, z_last + 1)
                r = ROOT_BASE[name]
                act.activation(root[r % 2][:], bank[4][:], ACT.Sqrt, bias=eps_col[eps][:], scale=1.0 / width
                               ).then_inc(root_done, 1)

            def norm(nn):
                rms(f"n{nn}", SQ_BASE[f"n{nn}"] + DC - 1, D, NORM_EPS.get(nn, 1e-5))
                if nn == 8:
                    return
                for c in range(DC):
                    act.wait_ge(h_scaled, H_BASE[nn] + c + 1)
                    shift = mod[:, SHIFT_COL[nn] + c:SHIFT_COL[nn] + c + 1] if nn < 4 else 0.0
                    act.activation(h_hi[:, c, :], stage[c % 4][:], ACT.Identity, bias=shift).then_inc(h_rounded, 1)

            def project(parts, base_slot, sq0, root0, qk0, dests, after_slot=None):
                qk = 0
                pending = []

                def head_root():
                    z, r, j = pending.pop(0)
                    act.wait_ge(sq_summed, z + 1)
                    if j >= 2:
                        act.wait_ge(qk_normed, j - 1)
                    act.activation(root[r % 2][:], bank[4][:], ACT.Sqrt, bias=eps_col[1e-6][:], scale=1.0 / HD
                                   ).then_inc(root_done, 1)

                for s, part in enumerate(parts):
                    n = base_slot + s
                    if part[0] == "tok":
                        for m in range(2):
                            act.wait_ge(w_used, 2 * n + m + 1)
                            dests(s, m)
                        for m in range(2):
                            round_half(n + 2, m)
                        while pending:
                            head_root()
                        if after_slot is not None:
                            after_slot(s)
                        continue
                    for m in range(2):
                        b = (2 * s + m) % 4
                        act.wait_ge(w_used, 2 * n + m + 1)
                        if part[m] == "qk":
                            z = sq0 + qk
                            if z >= 2:
                                act.wait_ge(sq_summed, z - 1)
                            act.activation(sq[z % 2][:], bank[b][:], ACT.Square).then_inc(sq_ready, 1)
                        else:
                            dests(s, m)
                        round_half(n + 2, m)
                        while pending:
                            head_root()
                        if part[m] == "qk":
                            pending.append((sq0 + qk, root0 + qk, qk0 + qk))
                            qk += 1
                    if after_slot is not None:
                        after_slot(s)
                while pending:
                    head_root()

            def attention(npair, nyb, u0, heads, chunk0, width, kind, back=7):
                hpl = heads // nyb
                units = [(i, h) for i in range(NT) for h in range(heads)]
                U, L = len(units), NT * nyb
                for step in range(U + 8):
                    if step < U:
                        i, h = units[step]
                        w = width(i)
                        for m in range(npair):
                            v = u0["s"] + npair * step + m
                            c = npair * h + m
                            act.wait_ge(s_least, v + 1)
                            if npair == 2:
                                if step >= 2:
                                    act.wait_ge(p_turned, u0["t"] + step - 1)
                                dst = prob[(2 * step + m) % 4]
                            else:
                                act.wait_ge(p_turned, u0["t"] + max(step - 3, 0))
                                dst = prob[step % 4]
                            act.activation(dst[:, 0:w], neg_logit[v % 2][:, 0:w], ACT.Exp, scale=-1.0,
                                           bias=least[:, i % 2, c:c + 1], accum_out=total[:, i % 2, c:c + 1]
                                           ).then_inc(exp_done, 1)
                    if 2 <= step < U + 2:
                        u = step - 2
                        i, h = units[u]
                        T = u0["t"] + u
                        act.wait_ge(p_turned, T + 1)
                        if T >= 2:
                            act.wait_ge(pv_done, T - 1)
                        act.activation(prob_t[T % 2][:, 0:width(i)], bank[3 + T % 2][:, 0:width(i)], ACT.Copy
                                       ).then_inc(pt_copied, 1)
                    for k in range(L):
                        Y = u0["y"] + k
                        if step == (k + 1) * hpl + 3:
                            if kind == "diff":
                                act.wait_ge(pv_done, u0["t"] + (k + 1) * hpl)
                                act.activation(tmp[0][:], bank[5 + k % 2][:], ACT.Square).then_inc(y_squares, 1)
                                act.wait_ge(y_stat, k + 1)
                                act.activation(stat[:], stat[:], ACT.Sqrt, bias=eps_col[1e-6][:], scale=1.0 / P
                                               ).then_inc(y_root, 1)
                        if step == (k + 1) * hpl + 5:
                            act.wait_ge(y_turned, Y + 1)
                            if Y >= 2:
                                act.wait_ge(y_ready, Y - 1)
                            c0 = chunk0 + 4 * (k % nyb)
                            ti = k // nyb
                            wide = y_wide_buf[Y % 2]
                            act.activation(wide[:], bank[back][:], ACT.Identity,
                                           scale=subln_col[:] if kind == "diff" else 1.0).then_inc(y_wide, 1)
                            act.wait_ge(y_wide, Y + 1)
                            act.activation(h_hi[:, c0:c0 + 4, P * ti:P * ti + P],
                                           wide[:].rearrange("p (c q) -> p c q", q=P), ACT.Copy).then_inc(y_rounded, 1)
                    if kind == "win" and step >= hpl and step % hpl == 0 and step <= U:
                        k = step // hpl - 1
                        act.wait_ge(sink_step, 3 * k + 1)
                        act.activation(sink_exp[:, 0:hpl], sink_exp[:, 0:hpl], ACT.Exp).then_inc(sink_step, 1)

            def swiglu(f, then_norm):
                m0, n0 = FC * f, SLOT[f"gu{f}"]

                def round_in_loop(i, j, m):
                    par = (n0 + j) % 2
                    half = slice(P * m, P * m + P)
                    if m == 0:
                        act.wait_ge(w_full[par], i * 16 + 16 * (loads_upto[n0 + 2 + j] + 1))
                    act.wait_ge(w_used, i * 4 + (2 * (n0 + j) + m + 1))
                    act.activation(w_hi[par][:, :, half], w_raw[par][:, :, half], ACT.Copy).then_inc(w_rounded, 1)

                with act.Fori(0, FC // 2) as i:
                    for q in range(2):
                        act.wait_ge(w_used, i * 4 + (2 * n0 + q + 1))
                        act.wait_ge(gated, i * 2 + (m0 + q + AHEAD))
                        act.activation(sq[q][:], bank[q][:], ACT.Silu).then_inc(silu_done, 1)
                        round_in_loop(i, 0, q)
                    for q in range(2):
                        round_in_loop(i, 1, q)
                        act.wait_ge(gated, i * 2 + (m0 + q + 1 + AHEAD))
                        act.activation(a_hi[:, bass.ds(i * 2 + q, 1), :], tmp[q][:].unsqueeze(1), ACT.Copy
                                       ).then_inc(a_rounded, 1)
                round_and_square(SLOT[f"down{f}"], 3, then_norm)

            def round_slots(base, n):
                for j in range(n):
                    for m in range(2):
                        round_half(base + j + 2, m)

            act.wait_ge(cols_ready, 1)
            act.activation(cond[:], col_range("c", 0, DC), ACT.Silu).then_inc(cond_ready, 1)
            for c in range(DC):
                act.wait_ge(x_t, c + 1)
                act.activation(x_cm[:, c, :], bank[c % 4][:], ACT.Copy).then_inc(x_ready, 1)
            round_slots(-2, 2)
            norm_squares(0)
            norm(0)

            def even_dest(s, m):
                if s == 0:
                    act.activation(ik[:], bank[1][:], ACT.Copy).then_inc(plain_copied, 1)
                elif s == 1:
                    v = bank[2 + m][:].rearrange("p (i w) -> p i w", i=2)
                    act.activation(bv[:, 2 * m:2 * m + 2, :], v[:, :, 0:HD], ACT.Copy)
                    act.activation(iw[:, 2 * m:2 * m + 2, :], v[:, :, HD:HD + I_HEADS], ACT.Copy,
                                   scale=I_HEADS ** -0.5).then_inc(plain_copied, 1)
                elif s in (2, 3):
                    c = 2 * (s - 2) + m
                    act.activation(iq[:, c, :], bank[(2 * s + m) % 4][:], ACT.Copy).then_inc(plain_copied, 1)
                else:
                    v = bank[(2 * s + m) % 4][:].rearrange("p (i w) -> p i w", i=2)
                    act.activation(av[:, 2 * m:2 * m + 2, 256 * (s - 10):256 * (s - 10) + 256], v, ACT.Copy
                                   ).then_inc(plain_copied, 1)

            idx_units = [(i, h) for i in range(1, NT) for h in range(I_HEADS)]

            def index_relu(s):
                if s == 2:
                    act.wait_ge(lam_s, 2)
                    act.activation(lam_exp[:], lam_sum[:], ACT.Exp).then_inc(lam_s, 1)
                if not 4 <= s < 10:
                    return
                for v in range(4 * (s - 4), 4 * (s - 4) + 4):
                    i, h = idx_units[v]
                    act.wait_ge(idx_summed, v + 1)
                    if v >= 2:
                        act.wait_ge(idx_added, v - 1)
                    w = P * (i + 1)
                    act.activation(neg_logit[v % 2][:, 0:w], bank[5 + v % 2][:, 0:w], ACT.Relu, scale=HD ** -0.5
                                   ).then_inc(idx_relu, 1)

            EVEN = [("qk", "plain"), ("tok",), ("plain", "plain"), ("plain", "plain")] + [("qk", "qk")] * 6 + [("tok",), ("tok",)]
            project(EVEN, 0, SQ_BASE["even"], ROOT_BASE["even"], 0, even_dest, index_relu)
            act.wait_ge(w_used, 2 * N_EVEN)
            attention(2, 1, dict(s=0, t=0, y=0), A_HEADS, 0, lambda i: P * (i + 1), "diff", back=2)
            attention(1, 1, dict(s=32, t=16, y=4), B_HEADS, 4, lambda i: P * (i + 1), "dsa", back=2)
            follows = lambda k: k if n_sub > k else 8
            round_and_square(SLOT["out0"], 1, follows(1))
            if n_sub > 1:
                norm(1)
                swiglu(0, follows(2))
            if n_sub > 2:
                norm(2)

                def odd_dest(s, m):
                    v = bank[(2 * s + m) % 4][:].rearrange("p (i w) -> p i w", i=2)
                    act.activation(cv[:, 2 * m:2 * m + 2, :], v, ACT.Copy).then_inc(plain_copied, 1)

                ODD = [("qk", "qk"), ("qk", "qk"), ("tok",)] + [("qk", "qk")] * 4
                project(ODD, SLOT["odd"], SQ_BASE["odd"], ROOT_BASE["odd"], 13, odd_dest)
                act.wait_ge(w_used, 2 * SLOT["out1"])
                attention(1, 2, dict(s=64, t=48, y=8), C_HEADS, 0, lambda i: P * (2 if i else 1), "win")
                round_and_square(SLOT["out1"], 1, follows(3))
            if n_sub > 3:
                norm(3)
                swiglu(1, follows(4))
            if n_sub > 4:
                norm(4)
                ssm_act(act, round_half)
                round_and_square(SLOT["ssm_out"], 2, follows(5))
            if n_sub > 5:
                norm(5)
                swiglu(2, follows(6))
            if n_sub > 6:
                norm(6)
                for c in range(DC):
                    if c % 2 == 0:
                        round_slots(SLOT["cv"] + c, 1)
                    act.wait_ge(w_used, 2 * (SLOT["cv"] + 2 * (c // 2) + 1) + c % 2 + 1)
                    if c >= 2:
                        act.wait_ge(glu_done, c - 1)
                    act.activation(tmp[c % 2][:], bank[2 + c % 2][:], ACT.Sigmoid, bias=col("cv_b_pw1", DC + c)
                                   ).then_inc(sig_done, 1)
                    round_half(SLOT["cv"] + 2 * (c // 2) + 1 + 2, c % 2)
                z0 = SQ_BASE["ln"]
                for c in range(DC):
                    act.wait_ge(centred, c + 1)
                    act.wait_ge(sq_summed, z0 + c - 1)
                    act.activation(sq[(z0 + c) % 2][:], v_cm[:, c, :], ACT.Square).then_inc(sq_ready, 1)
                rms("ln", z0 + DC - 1, D, 1e-5)
                for c in range(DC):
                    act.wait_ge(h_scaled, H_BASE["ln"] + c + 1)
                    act.activation(stage[c % 4][:], stage[c % 4][:], ACT.Silu, bias=col("cv_ln_b", c), scale=col("cv_ln_g", c)
                                   ).then_inc(h_shifted, 1)
                    act.wait_ge(h_shifted, c + 1)
                    act.activation(h_hi[:, c, :], stage[c % 4][:], ACT.Copy).then_inc(h_rounded, 1)
                round_and_square(SLOT["pw2"], 1, follows(7))
            if n_sub > 7:
                norm(7)
                swiglu(3, follows(8))
            norm(8)

        def ssm_dve(dve, link):
            n0 = SLOT["ssm"]
            bc_tile = lambda row: row.unsqueeze(1).to_broadcast([P, NT, MH])
            dve.wait_ge(w_used, 2 * n0 + 2)
            for m in range(2):
                v = bank[m][:].rearrange("p (i w) -> p i w", i=2)[:, :, 0:MH]
                ins = dve.tensor_tensor(dt_tok[:, 2 * m:2 * m + 2, :], v, dtb_row[:].unsqueeze(1).to_broadcast([P, 2, MH]), ALU.add)
            ins.then_inc(dt_step, 1)
            dve.wait_ge(dt_step, 1)
            dve.scalar_tensor_tensor(out=dt_abs[:], in0=dt_tok[:], scalar=-1.0, in1=dt_tok[:], op0=ALU.mult, op1=ALU.max
                                     ).then_inc(dt_step, 1)
            dve.wait_ge(dt_act, 3)
            link(dve.scalar_tensor_tensor(out=dt_tok[:], in0=dt_tok[:], scalar=0.0, in1=dt_abs[:], op0=ALU.max, op1=ALU.add))
            dve.scalar_tensor_tensor(out=log_decay[:], in0=dt_tok[:], scalar=-1.0, in1=bc_tile(alog_row[:]),
                                     op0=ALU.mult, op1=ALU.mult).then_inc(dt_step, 1)
            for c in range(NCONV):
                src, acc = bank[(c + 2) % 4], tmp[c % 2]
                dve.wait_ge(w_used, 2 * (n0 + 1) + c + 1)
                if 2 <= c < 18:
                    dve.wait_ge(conv_turned, c - 1)
                elif c >= 18:
                    dve.wait_ge(conv_silu, c - 1)
                w = lambda k: col("conv_w", NCONV * k + c)
                link(dve.tensor_scalar(acc[:], src[:], w(3), col("ssm_conv_b", c), ALU.mult, ALU.add))
                for k in (2, 1, 0):
                    sh = 3 - k
                    ins = dve.scalar_tensor_tensor(out=acc[:, sh:S], in0=src[:, 0:S - sh], scalar=w(k), in1=acc[:, sh:S],
                                                   op0=ALU.mult, op1=ALU.add)
                    if k:
                        link(ins)
                ins.then_inc(conv_done, 1)
            dve.wait_ge(decay_ready, 1)
            dve.wait_ge(z_ready, 16)
            dve.wait_ge(w_used, 2 * SLOT["ssm_out"])

            def heads(ap, n=HPG):
                return ap.rearrange("p (h e) -> p h e", e=HD)

            for i in range(NT):
                dve.wait_ge(cb_summed, i + 1)
                if i >= 1:
                    dve.wait_ge(mix_ready, 8 * i)
                dve.tensor_tensor(cb_mask[:].rearrange("p (g l) -> p g l", l=P), bank[0][:].rearrange("p (g l) -> p g l", l=P),
                                  upto[:].unsqueeze(1).to_broadcast([P, MG, P]), ALU.mult).then_inc(cb_masked, 1)

                def weights(q):
                    Q, g = 8 * i + q, q // 2
                    dve.wait_ge(seg_exp, Q + 1)
                    dve.wait_ge(cb_masked, i + 1)
                    if Q >= 2:
                        dve.wait_ge(yd_summed, Q - 1)
                    dve.tensor_tensor(sq[q % 2][:].rearrange("p (j l) -> p j l", l=P),
                                      tmp[q % 2][:].rearrange("p (j l) -> p j l", l=P),
                                      cb_mask[:, P * g:P * g + P].unsqueeze(1).to_broadcast([P, 4, P]), ALU.mult
                                      ).then_inc(mix_ready, 1)

                def gate_group(g):
                    G = 4 * i + g
                    y = y_ssm[:, S * g:S * g + S]
                    hd = slice(HPG * g, HPG * g + HPG)
                    xg, zg = xs_tok[:, i, S * g:S * g + S], z_tok[:, i, S * g:S * g + S]
                    bc = lambda a: a.unsqueeze(2).to_broadcast([P, HPG, HD])
                    dve.wait_ge(skip_done, i + 1)
                    dve.wait_ge(yd_summed, 8 * i + 2 * g + 2)
                    link(dve.tensor_tensor(y, bank[3 + g % 2][:], y, ALU.add))
                    if i >= 1:
                        dve.wait_ge(yo_summed, 4 * (i - 1) + g + 1)
                        link(dve.tensor_tensor(heads(xg), heads(bank[5 + g % 2][:]), bc(decay[:, 0, i, hd]), ALU.mult))
                        link(dve.tensor_tensor(y, y, xg, ALU.add))
                    dve.tensor_tensor(y, y, zg, ALU.mult).then_inc(yg_done, 1)
                    if i < NT - 1:
                        st = state[:, S * g:S * g + S]
                        dve.wait_ge(st_summed, G + 1)
                        if i == 0:
                            dve.tensor_copy(st, bank[7][:]).then_inc(st_done, 1)
                        else:
                            link(dve.tensor_tensor(heads(st), heads(st), bc(decay[:, 2, i, hd]), ALU.mult))
                            dve.tensor_tensor(st, st, bank[7][:], ALU.add).then_inc(st_done, 1)

                for q in range(8):
                    weights(q)
                    if q in (3, 5, 7):
                        gate_group((q - 3) // 2)
                gate_group(3)
                dve.wait_ge(yg_root, i + 1)
                link(dve.reciprocal(stat[:], stat[:]))
                yv = y_ssm[:].rearrange("p (g e) -> p g e", e=S)
                dve.tensor_tensor(yv, yv, stat[:].unsqueeze(2).to_broadcast([P, MG, S]), ALU.mult).then_inc(ys_scaled, 1)

                for k in range(4):
                    K = 4 * i + k
                    dve.wait_ge(ys_turned, K + 1)
                    if k < 2:
                        dve.wait_ge(seg_summed, 8 * i + 8)
                    else:
                        dve.wait_ge(ys_ready, K - 1)
                    gcols = cols[:, ROWS["gate_norm"] + 4 * k:ROWS["gate_norm"] + 4 * k + 4]
                    dve.tensor_tensor(root[k % 2][:].rearrange("p (c q) -> p c q", q=P),
                                      bank[5 + k % 2][:].rearrange("p (c q) -> p c q", q=P),
                                      gcols.unsqueeze(2).to_broadcast([P, 4, P]), ALU.mult).then_inc(ys_wide, 1)

        def cv_dve(dve, link):
            n0 = SLOT["cv"]
            pad = TAPS - 1
            link(dve.memset(u_pad[:, :, 0:pad], 0.0))

            def own_taps(c):
                v = v_cm[:, c, :]
                tap = lambda k: cols[:, ROWS["dw_w"] + DC * k + c:ROWS["dw_w"] + DC * k + c + 1]
                link(dve.tensor_scalar(v, u_pad[:, c, PE_TAPS:PE_TAPS + S], tap(PE_TAPS), col("cv_dw_b", c), ALU.mult, ALU.add))
                for k in range(PE_TAPS + 1, TAPS):
                    link(dve.scalar_tensor_tensor(out=v, in0=u_pad[:, c, k:k + S], scalar=tap(k), in1=v,
                                                  op0=ALU.mult, op1=ALU.add))
                dve.wait_ge(pe_taps_done, c + 1)
                dve.tensor_tensor(v, bank[6 + c % 2][:], v, ALU.add).then_inc(taps_done, 1)

            for c in range(DC):
                dve.wait_ge(sig_done, c + 1)
                dve.scalar_tensor_tensor(out=u_pad[:, c, pad:pad + S], in0=bank[c % 2][:], scalar=col("cv_b_pw1", c),
                                         in1=tmp[c % 2][:], op0=ALU.add, op1=ALU.mult).then_inc(glu_done, 1)
                if c % 2 == 1:
                    dve.wait_ge(glu_done, c + 1)
                    own_taps(c - 1)
                    own_taps(c)
            dve.wait_ge(mean_summed, 1)
            for c in range(DC):
                dve.scalar_tensor_tensor(out=v_cm[:, c, :], in0=bank[4][:], scalar=-1.0 / D, in1=v_cm[:, c, :],
                                         op0=ALU.mult, op1=ALU.add).then_inc(centred, 1)
            dve.wait_ge(centred, DC)

        @block.vector
        def _(dve):
            chain = [0]

            def link(ins):
                chain[0] += 1
                ins.then_inc(dve_chain, 1)
                dve.wait_ge(dve_chain, chain[0])

            def rinv(name, job=0):
                r = ROOT_BASE[name] + job
                dve.wait_ge(root_done, r + 1)
                dve.reciprocal(root[r % 2][:], root[r % 2][:]).then_inc(rinv_ready, 1)
                dve.wait_ge(rinv_ready, r + 1)
                return root[r % 2]

            def norm_scale(name, scale_chunk, low_chunk):
                ri = rinv(name)
                for c in range(DC + 2):
                    if c < DC:
                        if c >= 4:
                            dve.wait_ge(h_ready, LOW[0] + c - 3)
                        scale_chunk(c, stage[c % 4], ri).then_inc(h_scaled, 1)
                    if c >= 2:
                        dve.wait_ge(h_rounded, LOW[0] + c - 1)
                        low_chunk(c - 2, stage[(c - 2) % 4]).then_inc(h_ready, 1)
                LOW[0] += DC

            LOW = [0]

            def out_copy(c):
                dve.wait_ge(out_t, c + 1)
                dve.tensor_copy(y_out[:, :, P * c:P * c + P], bank[c % 4][:].rearrange("p (i q) -> p i q", q=P)
                                ).then_inc(out_copied, 1)

            def norm(nn):
                g = (lambda c: gain[:, nn, c:c + 1]) if nn < 4 else (lambda c: col(NORM_GAIN[nn][0], NORM_GAIN[nn][1] + c))

                def scale_chunk(c, dst, ri):
                    return dve.scalar_tensor_tensor(out=dst[:], in0=x_cm[:, c, :], scalar=g(c), in1=ri[:],
                                                    op0=ALU.mult, op1=ALU.mult)

                def low_chunk(c, src):
                    if nn < 4:
                        return dve.scalar_tensor_tensor(
                            out=h_lo[:, c, :], in0=src[:], scalar=mod[:, SHIFT_COL[nn] + c:SHIFT_COL[nn] + c + 1],
                            in1=h_hi[:, c, :].bitcast(F32), op0=ALU.add, op1=ALU.subtract)
                    return dve.tensor_tensor(h_lo[:, c, :], src[:], h_hi[:, c, :].bitcast(F32), ALU.subtract)

                norm_scale(f"n{nn}", scale_chunk, low_chunk)

            def final_norm():
                ri = rinv("n8")
                for c in range(DC):
                    if c >= 4:
                        dve.wait_ge(out_t, c - 3)
                    dve.scalar_tensor_tensor(out=stage[c % 4][:], in0=x_cm[:, c, :], scalar=col("final_norm", c), in1=ri[:],
                                             op0=ALU.mult, op1=ALU.mult).then_inc(h_scaled, 1)
                    if c >= 2:
                        out_copy(c - 2)
                out_copy(DC - 2)
                out_copy(DC - 1)

            def ada_group(g):
                acc, at = ada_acc[g % 2], 8 * g
                if g >= 2:
                    dve.wait_ge(ada_col, g - 1)
                for k in range(8):
                    buf, uses = ada_half(g, k // 4)
                    w = ada_w[buf][:, k % 4, :]
                    if k % 4 == 0:
                        dve.wait_ge(ada_full[buf], 16 * (uses + 1))
                    if k == 0:
                        dve.tensor_scalar(acc[:], w, cond[:, 0:1], None, ALU.mult).then_inc(ada_dve, 1)
                    else:
                        dve.wait_ge(ada_dve, at + k)
                        dve.scalar_tensor_tensor(out=acc[:], in0=w, scalar=cond[:, k:k + 1], in1=acc[:],
                                                 op0=ALU.mult, op1=ALU.add).then_inc(ada_dve, 1)

            def qk_norm(j, r, b, g, dst):
                dve.wait_ge(root_done, r + 1)
                dve.reciprocal(root[r % 2][:], root[r % 2][:]).then_inc(rinv_ready, 1)
                dve.wait_ge(rinv_ready, r + 1)
                dve.scalar_tensor_tensor(out=dst, in0=bank[b][:], scalar=g, in1=root[r % 2][:], op0=ALU.mult, op1=ALU.mult
                                         ).then_inc(qk_normed, 1)

            def x_add(x0, gates, bias=False, last_slots=lambda m: 0):
                for m in range(4):
                    for q in range(2):
                        c = 2 * m + q
                        dve.wait_ge(w_used, 2 * last_slots(m) + q + 1)
                        dve.scalar_tensor_tensor(out=x_cm[:, c, :], in0=bank[c % 4][:], scalar=gates(c), in1=x_cm[:, c, :],
                                                 op0=ALU.add if bias else ALU.mult, op1=ALU.add).then_inc(x_ready, 1)

            def swiglu(f, gate):
                m0, n0 = FC * f, SLOT[f"gu{f}"]
                with dve.Fori(0, FC // 2) as i:
                    for q in range(2):
                        dve.wait_ge(w_used, i * 4 + (2 * n0 + 2 + q + 1))
                        dve.wait_ge(silu_done, i * 2 + (m0 + q + 1))
                        dve.wait_ge(a_ready, i * 2 + (m0 + AHEAD))
                        dve.tensor_tensor(tmp[q][:], sq[q][:], bank[2 + q][:], ALU.mult).then_inc(gated, 1)
                    for q in range(2):
                        dve.wait_ge(a_rounded, i * 2 + (m0 + q + 1))
                        hi = a_hi[:, bass.ds(i * 2 + q, 1), :].bitcast(F32)
                        dve.tensor_tensor(a_lo[:, bass.ds(i * 2 + q, 1), :], tmp[q][:].unsqueeze(1), hi, ALU.subtract
                                          ).then_inc(a_ready, 1)
                n0 = SLOT[f"down{f}"]
                with dve.Fori(0, 2) as i:
                    for j in range(4):
                        dve.wait_ge(w_used, i * 12 + (2 * (n0 + 3 * (j // 2) + 2) + j % 2 + 1))
                        xc = x_cm[:, bass.ds(i * 4 + j, 1), :].squeeze(1)
                        if gate is None:
                            dve.tensor_tensor(xc, bank[j][:], xc, ALU.add).then_inc(x_ready, 1)
                        else:
                            dve.scalar_tensor_tensor(out=xc, in0=bank[j][:], scalar=mod[:, bass.ds(i * 4 + (gate + j), 1)],
                                                     in1=xc, op0=ALU.mult, op1=ALU.add).then_inc(x_ready, 1)

            dve.memset(eps_col[1e-6][:], 1e-6).then_inc(gated, AHEAD)
            dve.memset(eps_col[1e-5][:], 1e-5).then_inc(a_ready, AHEAD)
            n = STACK_ROWS[0]
            dve.wait_ge(rows_t, 1)
            dve.tensor_copy(cols[:, 0:n], bank[5][:, 0:n]).then_inc(cols_ready, 1)
            dve.wait_ge(cols_ready, 1)
            dve.wait_ge(cond_ready, 1)
            for g in range(ADA_FIRST):
                ada_group(g)
            for j in range(6):
                ins = dve.tensor_scalar(qk_gain[:, j:j + 1], col("qk_gain", j), -(HD ** -0.5) if j % 2 == 0 else 1.0, None,
                                        ALU.mult)
            link(ins)

            def later_params():
                dve.wait_ge(bcast_in, 16 * 8)
                pairs = lam_row[:].rearrange("o (a b) d -> o a b d", b=2)
                dve.tensor_tensor(lam_prod[:], pairs[:, :, 0, :], pairs[:, :, 1, :], ALU.mult).then_inc(lam_s, 1)
                dve.wait_ge(lam_s, 1)
                dve.tensor_reduce(lam_sum[:], lam_prod[:], AX_X, ALU.add).then_inc(lam_s, 1)
                dve.wait_ge(lam_s, 3)
                link(dve.tensor_tensor(lam_val[:], lam_exp[0:1, 1:2], lam_exp[0:1, 0:1], ALU.subtract))
                dve.tensor_scalar(lam_val[:], lam_val[:], -LAM_INIT, None, ALU.add).then_inc(lam_s, 1)
                dve.wait_ge(lam_s, 5)
                dve.tensor_copy(neg_lam[:], bank[6][:, 0:1]).then_inc(lam_s, 1)
                dve.wait_ge(rows_t, 2)
                for s in range(1, NSTACK):
                    n = STACK_ROWS[s]
                    dve.tensor_copy(cols[:, P * s:P * s + n], bank[5][:, P * (s - 1):P * (s - 1) + n]).then_inc(cols_ready, 1)
                dve.wait_ge(cols_ready, NSTACK)
                dve.tensor_scalar(subln_col[:], col("subln"), 1.0 - LAM_INIT, None, ALU.mult)
                link(dve.tensor_scalar(neg_sink[:], sink_row[:], -1.0, None, ALU.mult))

            dve.wait_ge(ada_col, 8)
            link(dve.tensor_tensor(mod[:, 0:16], bank[7][:, 0:16], col_range("ada_b", 0, 16), ALU.add))

            def make_gain(nn, scale0, name, j):
                return dve.scalar_tensor_tensor(out=gain[:, nn, :], in0=mod[:, scale0:scale0 + 8], scalar=1.0,
                                                in1=col_range(name, j, 8), op0=ALU.add, op1=ALU.mult)

            make_gain(0, 8, "norm_mix", 0).then_inc(gains_ready, 1)
            norm(0)
            dve.wait_ge(h_ready, DC)
            link(dve.tensor_scalar(tmp[0][:, 0:P], dist[:, S - P:S], BIG / 10, SCORE_MASKED, ALU.is_ge, ALU.mult))

            idx_units = [(i, h) for i in range(1, NT) for h in range(I_HEADS)]

            def index_add(s):
                for v in range(4 * (s - 4), 4 * (s - 4) + 4):
                    i, h = idx_units[v]
                    w = P * (i + 1)
                    dve.wait_ge(idx_relu, v + 1)
                    sc, r = score[:, i - 1, 0:w], neg_logit[v % 2][:, 0:w]
                    if h == 0:
                        dve.tensor_scalar(sc, r, iw[:, i, 0:1], None, ALU.mult).then_inc(idx_added, 1)
                    else:
                        dve.wait_ge(idx_added, v)
                        dve.scalar_tensor_tensor(out=sc, in0=r, scalar=iw[:, i, h:h + 1], in1=sc, op0=ALU.mult, op1=ALU.add
                                                 ).then_inc(idx_added, 1)

            def take_top(i, r0, r1):
                w = P * (i + 1)
                sc = score[:, i - 1, 0:w]
                if r0 == 0:
                    dve.wait_ge(idx_added, I_HEADS * i)
                    diag = score[:, i - 1, P * i:w]
                    link(dve.tensor_tensor(diag, diag, tmp[0][:, 0:P], ALU.add))
                for _ in range(r0, r1):
                    link(dve.max(top8[:], sc))
                    link(dve.match_replace(sc, top8[:], sc, SCORE_TAKEN))
                if r1 == TOPK // 8:
                    link(dve.tensor_scalar(sc, sc, (SCORE_MASKED + SCORE_TAKEN) / 2 - 1e37, BIG, ALU.is_gt, ALU.mult))
                    link(dve.tensor_tensor(dist_sel[:, i - 1, 0:w], sc, dist[:, S - w:S], ALU.add))

            jr = [0]

            def even_slot(s):
                if s == 0:
                    items = [(0, 3, bk[:])]
                elif s in (4, 5):
                    items = [((2 * s + m) % 4, 2, bq[:, 2 * (s - 4) + m, :]) for m in range(2)]
                elif s in (6, 7):
                    items = [((2 * s + m) % 4, 0, aq[:, 2 * (s - 6) + m, :]) for m in range(2)]
                elif s in (8, 9):
                    items = [((2 * s + m) % 4, 1, ak[:, 2 * (s - 8) + m, :]) for m in range(2)]
                else:
                    items = []
                return items

            pending = []

            def flush_qk(keep):
                while len(pending) > keep:
                    b, g, dst = pending.pop(0)
                    qk_norm(jr[0], ROOT_BASE["even"] + jr[0], b, qk_gain[:, g:g + 1], dst)
                    jr[0] += 1

            for s in range(N_EVEN):
                pending += even_slot(s)
                if s > 0:
                    flush_qk(1 if 4 <= s < 10 else 0)
                if s < 8:
                    for g in range(ADA_FIRST + 2 * s, ADA_FIRST + 2 * s + 2):
                        ada_group(g)
                if s == 2:
                    later_params()
                if 4 <= s < 10:
                    index_add(s)
                if 6 <= s < 12:
                    i = (s - 6) // 2 + 1
                    take_top(i, 8 * (s % 2), 8 * (s % 2) + 8)
            def attention(npair, nyb, u0, heads, chunk0, width, dist_of, kind, ring=3):
                hpl = heads // nyb
                units = [(i, h) for i in range(NT) for h in range(heads)]
                U, L = len(units), NT * nyb
                slope = [2.0 ** (-8.0 * (h + 1) / heads) for h in range(heads)]
                for step in range(U + 8):
                    if step < U:
                        i, h = units[step]
                        w = width(i)
                        for m in range(npair):
                            v = u0["s"] + npair * step + m
                            c = npair * h + m
                            neg = neg_logit[v % 2][:, 0:w]
                            dve.wait_ge(s_summed, v + 1)
                            if v >= 2:
                                dve.wait_ge(exp_done, v - 1)
                            dve.scalar_tensor_tensor(out=neg, in0=dist_of(i), scalar=slope[h],
                                                     in1=bank[v % ring][:, 0:w], op0=ALU.mult, op1=ALU.add
                                                     ).then_inc(s_biased, 1)
                            dve.wait_ge(s_biased, v + 1)
                            lc = least[:, i % 2, c:c + 1]
                            if kind == "win":
                                link(dve.tensor_reduce(lc, neg, AX_X, ALU.min))
                                dve.tensor_tensor(lc, lc, neg_sink[:, h:h + 1], ALU.min).then_inc(s_least, 1)
                            else:
                                dve.tensor_reduce(lc, neg, AX_X, ALU.min).then_inc(s_least, 1)
                    if npair == 2 and 1 <= step < U + 1:
                        u = step - 1
                        i, h = units[u]
                        w = width(i)
                        dve.wait_ge(exp_done, u0["s"] + 2 * u + 2)
                        if u >= 1:
                            dve.wait_ge(mixed, 2 * u)
                        link(dve.reciprocal(pinv[:, 0:2], total[:, i % 2, 2 * h:2 * h + 2]))
                        link(dve.tensor_tensor(pinv[:, 1:2], pinv[:, 1:2], neg_lam[:], ALU.mult))
                        p0, p1 = prob[(2 * u) % 4][:, 0:w], prob[(2 * u + 1) % 4][:, 0:w]
                        dve.tensor_scalar(p0, p0, pinv[:, 0:1], None, ALU.mult).then_inc(mixed, 1)
                        dve.wait_ge(mixed, 2 * u + 1)
                        dve.scalar_tensor_tensor(out=p0, in0=p1, scalar=pinv[:, 1:2], in1=p0, op0=ALU.mult, op1=ALU.add
                                                 ).then_inc(mixed, 1)
                    for k in range(L):
                        Y = u0["y"] + k
                        i = k // nyb
                        if kind == "win" and step == (k + 1) * hpl:
                            c0 = hpl * (k % 2)
                            if k >= 1:
                                dve.wait_ge(sink_step, 3 * k)
                            dve.wait_ge(s_least, u0["s"] + (k + 1) * hpl)
                            dve.tensor_tensor(sink_exp[:, 0:hpl], least[:, i % 2, c0:c0 + hpl], sink_row[:, c0:c0 + hpl], ALU.add
                                              ).then_inc(sink_step, 1)
                        if step == (k + 1) * hpl + 4:
                            rows_ = bank[5 + k % 2]
                            if kind == "diff":
                                dve.wait_ge(y_squares, k + 1)
                                if k >= 1:
                                    dve.wait_ge(y_scaled, k)
                                dve.tensor_reduce(stat[:], tmp[0][:].rearrange("p (h e) -> p h e", e=P), AX_X, ALU.add
                                                  ).then_inc(y_stat, 1)
                                dve.wait_ge(y_root, k + 1)
                                link(dve.reciprocal(stat[:], stat[:]))
                                sc, e = stat[:], P
                            else:
                                dve.wait_ge(pv_done, u0["t"] + (k + 1) * hpl)
                                c0 = hpl * (k % nyb)
                                if kind == "win":
                                    dve.wait_ge(sink_step, 3 * k + 2)
                                    tt = total[:, i % 2, c0:c0 + hpl]
                                    dve.tensor_tensor(tt, tt, sink_exp[:, 0:hpl], ALU.add).then_inc(sink_step, 1)
                                    dve.wait_ge(sink_step, 3 * k + 3)
                                dve.wait_ge(mixed, 2 * 16)
                                dve.wait_ge(y_scaled, Y)
                                link(dve.reciprocal(pinv[:, 0:hpl], total[:, i % 2, c0:c0 + hpl]))
                                sc, e = pinv[:, 0:hpl], HD
                            if Y >= 2:
                                dve.wait_ge(y_turned, Y - 1)
                            n = S // e
                            dve.tensor_tensor(y_tok[k % 2][:].rearrange("p (h e) -> p h e", e=e),
                                              rows_[:].rearrange("p (h e) -> p h e", e=e),
                                              sc.unsqueeze(2).to_broadcast([P, n, e]), ALU.mult).then_inc(y_scaled, 1)
                        if step == (k + 1) * hpl + 6:
                            dve.wait_ge(y_rounded, Y + 1)
                            c0 = chunk0 + 4 * (k % nyb)
                            dve.tensor_tensor(h_lo[:, c0:c0 + 4, P * i:P * i + P],
                                              y_wide_buf[Y % 2][:].rearrange("p (c q) -> p c q", q=P),
                                              h_hi[:, c0:c0 + 4, P * i:P * i + P].bitcast(F32), ALU.subtract
                                              ).then_inc(y_ready, 1)

            causal = lambda i: P * (i + 1)
            attention(2, 1, dict(s=0, t=0, y=0), A_HEADS, 0, causal, lambda i: dist[:, S - P * (i + 1):S], "diff",
                      ring=2)
            attention(1, 1, dict(s=32, t=16, y=4), B_HEADS, 4, causal,
                      lambda i: dist_sel[:, i - 1, 0:P * (i + 1)] if i else dist[:, S - P:S], "dsa", ring=2)
            dve.wait_ge(ada_col, ADA_ALL)
            link(dve.tensor_tensor(mod[:, 16:96], bank[7][:, 16:96], col_range("ada_b", 16, 80), ALU.add))
            make_gain(1, 32, "norm_ffn", 0)
            make_gain(2, 48 + 8, "norm_mix", 8)
            make_gain(3, 48 + 32, "norm_ffn", 8).then_inc(gains_ready, 1)

            x_add(8, lambda c: mod[:, 16 + c:17 + c], last_slots=lambda m: SLOT["out0"] + m)
            if n_sub > 1:
                norm(1)
                swiglu(0, 40)
            if n_sub > 2:
                norm(2)
                for s in (0, 1, 3, 4, 5, 6):
                    for m in range(2):
                        b = (2 * s + m) % 4
                        j = 2 * s + m if s < 2 else 2 * s + m - 2
                        dst = ck[:, j, :] if s < 2 else cq[:, j - 4, :]
                        qk_norm(13 + j, ROOT_BASE["odd"] + j, b, qk_gain[:, 5:6] if s < 2 else qk_gain[:, 4:5], dst)
                attention(1, 2, dict(s=64, t=48, y=8), C_HEADS, 0, lambda i: P * (2 if i else 1),
                          lambda i: dist_win[:] if i else dist_win[:, P:2 * P], "win")
                x_add(24, lambda c: mod[:, 64 + c:65 + c], last_slots=lambda m: SLOT["out1"] + m)
            if n_sub > 3:
                norm(3)
                swiglu(1, 88)
            if n_sub > 4:
                norm(4)
                ssm_dve(dve, link)
                for m in range(4):
                    for q in range(2):
                        c = 2 * m + q
                        dve.wait_ge(w_used, 2 * (SLOT["ssm_out"] + 2 * m + 1) + q + 1)
                        dve.tensor_tensor(x_cm[:, c, :], bank[c % 4][:], x_cm[:, c, :], ALU.add).then_inc(x_ready, 1)
            if n_sub > 5:
                norm(5)
                swiglu(2, None)
            if n_sub > 6:
                norm(6)
                cv_dve(dve, link)
                norm_scale("ln", lambda c, dst, ri: dve.tensor_tensor(dst[:], v_cm[:, c, :], ri[:], ALU.mult),
                           lambda c, src: dve.tensor_tensor(h_lo[:, c, :], src[:], h_hi[:, c, :].bitcast(F32), ALU.subtract))
                x_add(56, lambda c: col("cv_b_pw2", c), bias=True, last_slots=lambda m: SLOT["pw2"] + m)
            if n_sub > 7:
                norm(7)
                swiglu(3, None)
            final_norm()


_INS = ['x', 'c', 'ada_w', 'ada_b', 'norm_mix', 'norm_ffn', 'w_out', 'ffn_gate', 'ffn_up', 'ffn_down', 'w_in_even',
        'qn_a', 'kn_a', 'lam_q1', 'lam_k1', 'lam_q2', 'lam_k2', 'subln_a', 'qn_b', 'kn_b', 'w_in_odd', 'qn_c', 'kn_c',
        'sinks_c', 'ssm_norm_2', 'ssm_w_in_2', 'ssm_conv_w_2', 'ssm_conv_b_2', 'ssm_dt_bias_2', 'ssm_a_log_2', 'ssm_d_2',
        'ssm_gate_norm_2', 'ssm_w_out_2', 'cv_norm_2', 'cv_w_pw1_2', 'cv_b_pw1_2', 'cv_dw_w_2', 'cv_dw_b_2', 'cv_ln_g_2',
        'cv_ln_b_2', 'cv_w_pw2_2', 'cv_b_pw2_2', 'ffn_norm_2', 'ffn_w_gate_2', 'ffn_w_up_2', 'ffn_w_down_2',
        'final_norm_2']
SUBLAYERS = 8


def kernel(**inputs):
    import numpy as np
    import concourse.bacc as bacc
    from concourse.bass_utils import run_bass_kernel_spmd

    nc = bacc.Bacc("TRN2", target_bir_lowering=False, num_devices=1)
    arrays, aps = {}, {}
    for name in _INS:
        a = np.ascontiguousarray(inputs[name])
        arrays[f"in_{name}_dram"] = a
        aps[name] = nc.dram_tensor(f"in_{name}_dram", a.shape, mybir.dt.from_np(a.dtype), kind="ExternalInput").ap()
    out = nc.dram_tensor("out_0_dram", (1, S, D), F32, kind="ExternalOutput").ap()
    build(nc, aps, out, SUBLAYERS)
    return run_bass_kernel_spmd(nc, [arrays], core_ids=[0]).results[0]["out_0_dram"]
```
